# Optimizing a Trainium2 kernel written in Bass

```python
import math
import jax, jax.numpy as jnp
from jax import lax
import numpy as np

D_MODEL = 1024
BATCH = 1
SEQ = 512
DEPTH = 1
DEC_BATCH = 8
DEC_SEQ = 8
PAST_LEN = 2048
PAGE_SIZE = 128

HEAD_DIM = 64
N_Q_HEADS = 16
N_KV_HEADS = 2
Q_PER_KV = N_Q_HEADS // N_KV_HEADS
WINDOW = 128
ATTN_SCALE = HEAD_DIM ** -0.5
NEG_INF = -1e30
N_BUCKETS = 32
BUCKET_MAX_EXACT = 16
BUCKET_MAX_DIST = 128
CHUNK = 128
N_SG_GROUPS = 4
SG_GROUP_DIM = 128
SG_WIDTH = N_SG_GROUPS * SG_GROUP_DIM
Q_W = N_Q_HEADS * HEAD_DIM
KV_W = N_KV_HEADS * HEAD_DIM
Q_END = Q_W
K_END = Q_END + KV_W
V_END = K_END + KV_W
U_END = V_END + SG_WIDTH
VS_END = U_END + SG_WIDTH
GA_END = VS_END + D_MODEL
IN_W = GA_END + D_MODEL
N_EXPERTS = 64
TOP_K = 8
N_EXPERT_GROUPS = 8
EXPERTS_PER_GROUP = N_EXPERTS // N_EXPERT_GROUPS
TOPK_GROUPS = 4
EXPERT_DIM = 256
SHARED_DIM = 256
ROUTED_SCALE = 2.5
ALPHA = (2 * DEPTH) ** 0.25
BETA = (8 * DEPTH) ** -0.25
LN_EPS = 1e-5

kernel_name = 'hybrid_swa_sink_gmlp_moe_deepnorm_step'

def layer_norm(x, g, b):
    xf = x.astype(jnp.float32)
    mu = jnp.mean(xf, -1, keepdims=True)
    var = jnp.mean(jnp.square(xf - mu), -1, keepdims=True)
    return ((xf - mu) * lax.rsqrt(var + LN_EPS) * g.astype(jnp.float32) + b.astype(jnp.float32)).astype(x.dtype)

def t5_bucket(dist):
    d = jnp.maximum(dist, 0)
    ratio = jnp.maximum(d, 1).astype(jnp.float32) / BUCKET_MAX_EXACT
    large = BUCKET_MAX_EXACT + (jnp.log(ratio) / math.log(BUCKET_MAX_DIST / BUCKET_MAX_EXACT)
                                * (N_BUCKETS - BUCKET_MAX_EXACT)).astype(jnp.int32)
    large = jnp.minimum(large, N_BUCKETS - 1)
    return jnp.where(d < BUCKET_MAX_EXACT, d, large)

def rel_bias(dist, table):
    return jnp.moveaxis(table[t5_bucket(dist)].astype(jnp.float32), -1, 0)

def sink_attend(logits, sink, v, eq):
    sink = sink.astype(jnp.float32)
    m = jnp.maximum(jnp.max(logits, -1, keepdims=True), sink)
    p = jnp.exp(logits - m)
    den = jnp.sum(p, -1, keepdims=True) + jnp.exp(sink - m)
    return jnp.einsum(eq, (p / den).astype(v.dtype), v)

def project(x, w_in, b_in):
    z = x @ w_in + b_in
    q, k, v, u, vs, ga, gb = jnp.split(z, [Q_END, K_END, V_END, U_END, VS_END, GA_END], axis=-1)
    lead = x.shape[:-1]
    q = q.reshape(*lead, N_KV_HEADS, Q_PER_KV, HEAD_DIM)
    k = k.reshape(*lead, N_KV_HEADS, HEAD_DIM)
    v = v.reshape(*lead, N_KV_HEADS, HEAD_DIM)
    return q, k, v, jax.nn.gelu(u), jax.nn.gelu(vs), ga, gb

def attend_prompt(q, k, v, sinks, table):
    B, S = q.shape[:2]
    L = WINDOW
    nb = S // L
    qb = q.reshape(B, nb, L, N_KV_HEADS, Q_PER_KV, HEAD_DIM)

    def band(t):
        tb = t.reshape(B, nb, L, N_KV_HEADS, HEAD_DIM)
        prev = jnp.concatenate([jnp.zeros_like(tb[:, :1]), tb[:, :-1]], axis=1)
        return jnp.concatenate([prev, tb], axis=2)

    kband, vband = band(k), band(v)
    i = jnp.arange(L)[:, None]
    j = jnp.arange(2 * L)[None, :]
    dist = i + L - j
    kpos = jnp.arange(nb)[:, None, None] * L - L + j[None]
    valid = (dist >= 0) & (dist <= WINDOW) & (kpos >= 0)
    bias = rel_bias(dist, table).reshape(N_KV_HEADS, Q_PER_KV, L, 2 * L)
    logits = jnp.einsum('bnqhrd,bnkhd->bnhrqk', qb, kband,
                        preferred_element_type=jnp.float32) * ATTN_SCALE + bias
    logits = jnp.where(valid[None, :, None, None], logits, NEG_INF)
    out = sink_attend(logits, sinks.reshape(1, 1, N_KV_HEADS, Q_PER_KV, 1, 1), vband,
                      'bnhrqk,bnkhd->bnqhrd')
    return out.reshape(B, S, Q_W)

def attend_sample(q, k, v, cache_k, cache_v, sinks, table):
    DB, DS = q.shape[:2]
    W = cache_k.shape[1]
    keys = jnp.concatenate([cache_k, k], axis=1)
    vals = jnp.concatenate([cache_v, v], axis=1)
    kpos = jnp.concatenate([jnp.arange(W) - W, jnp.arange(DS)])
    dist = jnp.arange(DS)[:, None] - kpos[None, :]
    valid = (dist >= 0) & (dist <= WINDOW)
    bias = rel_bias(dist, table).reshape(N_KV_HEADS, Q_PER_KV, DS, W + DS)
    logits = jnp.einsum('bqhrd,bkhd->bhrqk', q, keys,
                        preferred_element_type=jnp.float32) * ATTN_SCALE + bias
    logits = jnp.where(valid, logits, NEG_INF)
    out = sink_attend(logits, sinks.reshape(1, N_KV_HEADS, Q_PER_KV, 1, 1), vals,
                      'bhrqk,bkhd->bqhrd')
    return out.reshape(DB, DS, Q_W), keys[:, -W:], vals[:, -W:]

def spatial_gate_prompt(u, vs, sg_w, sg_b):
    B, S = u.shape[:2]
    nc = S // CHUNK
    vc = vs.reshape(B, nc, CHUNK, N_SG_GROUPS, SG_GROUP_DIM)
    s = jnp.einsum('gij,bnjgc->bnigc', jnp.tril(sg_w), vc) + sg_b.T[:, :, None]
    return (u.reshape(B, S, N_SG_GROUPS, SG_GROUP_DIM) * s.reshape(B, S, N_SG_GROUPS, SG_GROUP_DIM)).reshape(B, S, SG_WIDTH)

def spatial_gate_sample(u, vs, sg_w, sg_b):
    DB, DS = u.shape[:2]
    v4 = vs.reshape(DB, DS, N_SG_GROUPS, SG_GROUP_DIM)
    s = jnp.einsum('gij,bjgc->bigc', jnp.tril(sg_w[:, :DS, :DS]), v4) + sg_b[:, :DS].T[:, :, None]
    return (u.reshape(DB, DS, N_SG_GROUPS, SG_GROUP_DIM) * s).reshape(DB, DS, SG_WIDTH), v4

def moe(x, w_router, router_bias, w_gate_e, w_up_e, w_down_e, w_gate_s, w_up_s, w_down_s):
    shp = x.shape
    t = x.reshape(-1, D_MODEL)
    scores = jax.nn.sigmoid((t @ w_router).astype(jnp.float32))
    sel = scores + router_bias.astype(jnp.float32)
    grp = sel.reshape(-1, N_EXPERT_GROUPS, EXPERTS_PER_GROUP)
    grp_score = jnp.sum(lax.top_k(grp, 2)[0], -1)
    _, top_g = lax.top_k(grp_score, TOPK_GROUPS)
    gmask = jnp.sum(jax.nn.one_hot(top_g, N_EXPERT_GROUPS, dtype=jnp.float32), axis=1)
    emask = jnp.repeat(gmask, EXPERTS_PER_GROUP, axis=1) > 0
    _, top_e = lax.top_k(jnp.where(emask, sel, NEG_INF), TOP_K)
    w_sel = jnp.take_along_axis(scores, top_e, axis=1)
    w_sel = w_sel / jnp.sum(w_sel, -1, keepdims=True) * ROUTED_SCALE
    gates = jnp.sum(jax.nn.one_hot(top_e, N_EXPERTS, dtype=jnp.float32) * w_sel[..., None], axis=1)

    def expert_step(acc, xs):
        wg, wu, wd, g = xs
        h = jax.nn.silu(t @ wg) * (t @ wu)
        return acc + (h @ wd) * g[:, None].astype(t.dtype), None

    routed, _ = lax.scan(expert_step, jnp.zeros_like(t), (w_gate_e, w_up_e, w_down_e, gates.T))
    shared = (jax.nn.silu(t @ w_gate_s) * (t @ w_up_s)) @ w_down_s
    return (routed + shared).reshape(shp)

def merge_residual(x, a, s, ga, gb, lp):
    h = (jax.nn.sigmoid(ga) * (a @ lp['w_proj_a']) + jax.nn.sigmoid(gb) * (s @ lp['w_proj_b'])) @ lp['w_out']
    return layer_norm(ALPHA * x + h, lp['ln1_g'], lp['ln1_b'])

def ffn_residual(x, lp):
    y = moe(x, lp['w_router'], lp['router_bias'], lp['w_gate_e'], lp['w_up_e'], lp['w_down_e'],
            lp['w_gate_s'], lp['w_up_s'], lp['w_down_s'])
    return layer_norm(ALPHA * x + y, lp['ln2_g'], lp['ln2_b'])

def prompt_layer(x, lp, table):
    q, k, v, u, vs, ga, gb = project(x, lp['w_in'], lp['b_in'])
    vs = layer_norm(vs, lp['sg_ln_g'], lp['sg_ln_b'])
    a = attend_prompt(q, k, v, lp['attn_sinks'], table)
    s = spatial_gate_prompt(u, vs, lp['sg_w'], lp['sg_b'])
    x = ffn_residual(merge_residual(x, a, s, ga, gb, lp), lp)
    keep = min(WINDOW, x.shape[1])
    return x, k[:, -keep:], v[:, -keep:]

def sample_layer(x, ck, cv, lp, table):
    q, k, v, u, vs, ga, gb = project(x, lp['w_in'], lp['b_in'])
    vs = layer_norm(vs, lp['sg_ln_g'], lp['sg_ln_b'])
    a, nk, nv = attend_sample(q, k, v, ck, cv, lp['attn_sinks'], table)
    s, v_rows = spatial_gate_sample(u, vs, lp['sg_w'], lp['sg_b'])
    x = ffn_residual(merge_residual(x, a, s, ga, gb, lp), lp)
    return x, nk, nv, v_rows

def setup_inputs(seed: int = 0) -> dict:
    key = jax.random.key(seed)
    ks = jax.random.split(key, 32)
    f32 = jnp.float32

    def nrm(k, shape, scale):
        return jax.random.normal(k, shape, f32) * scale

    win_rows = min(WINDOW, PAST_LEN)
    w_in = nrm(ks[4], (DEPTH, D_MODEL, IN_W), D_MODEL ** -0.5)
    w_in = w_in.at[:, :, K_END:V_END].multiply(BETA)
    return {
        'x_prompt': nrm(ks[0], (BATCH, SEQ, D_MODEL), 1.0),
        'x_sample': nrm(ks[1], (DEC_BATCH, DEC_SEQ, D_MODEL), 1.0),
        'cache_win_k': nrm(ks[2], (DEPTH, DEC_BATCH, win_rows, N_KV_HEADS, HEAD_DIM), 1.0),
        'cache_win_v': nrm(ks[3], (DEPTH, DEC_BATCH, win_rows, N_KV_HEADS, HEAD_DIM), 1.0),
        'rel_bias_table': nrm(ks[7], (N_BUCKETS, N_Q_HEADS), 0.5),
        'w_in': w_in,
        'b_in': nrm(ks[5], (DEPTH, IN_W), 0.02),
        'attn_sinks': nrm(ks[6], (DEPTH, N_Q_HEADS), 0.5),
        'sg_ln_g': 1.0 + nrm(ks[8], (DEPTH, SG_WIDTH), 0.02),
        'sg_ln_b': nrm(ks[9], (DEPTH, SG_WIDTH), 0.02),
        'sg_w': nrm(ks[10], (DEPTH, N_SG_GROUPS, CHUNK, CHUNK), CHUNK ** -0.5),
        'sg_b': 1.0 + nrm(ks[11], (DEPTH, N_SG_GROUPS, CHUNK), 0.1),
        'w_proj_a': nrm(ks[12], (DEPTH, Q_W, D_MODEL), Q_W ** -0.5 * BETA),
        'w_proj_b': nrm(ks[13], (DEPTH, SG_WIDTH, D_MODEL), SG_WIDTH ** -0.5 * BETA),
        'w_out': nrm(ks[14], (DEPTH, D_MODEL, D_MODEL), D_MODEL ** -0.5 * BETA),
        'ln1_g': 1.0 + nrm(ks[15], (DEPTH, D_MODEL), 0.02),
        'ln1_b': nrm(ks[16], (DEPTH, D_MODEL), 0.02),
        'w_router': nrm(ks[17], (DEPTH, D_MODEL, N_EXPERTS), D_MODEL ** -0.5),
        'router_bias': nrm(ks[18], (DEPTH, N_EXPERTS), 0.01),
        'w_gate_e': nrm(ks[19], (DEPTH, N_EXPERTS, D_MODEL, EXPERT_DIM), D_MODEL ** -0.5),
        'w_up_e': nrm(ks[20], (DEPTH, N_EXPERTS, D_MODEL, EXPERT_DIM), D_MODEL ** -0.5),
        'w_down_e': nrm(ks[21], (DEPTH, N_EXPERTS, EXPERT_DIM, D_MODEL), EXPERT_DIM ** -0.5 * BETA),
        'w_gate_s': nrm(ks[22], (DEPTH, D_MODEL, SHARED_DIM), D_MODEL ** -0.5),
        'w_up_s': nrm(ks[23], (DEPTH, D_MODEL, SHARED_DIM), D_MODEL ** -0.5),
        'w_down_s': nrm(ks[24], (DEPTH, SHARED_DIM, D_MODEL), SHARED_DIM ** -0.5 * BETA),
        'ln2_g': 1.0 + nrm(ks[25], (DEPTH, D_MODEL), 0.02),
        'ln2_b': nrm(ks[26], (DEPTH, D_MODEL), 0.02),
    }

def reference(x_prompt, x_sample, cache_win_k, cache_win_v, rel_bias_table, w_in, b_in, attn_sinks,
              sg_ln_g, sg_ln_b, sg_w, sg_b, w_proj_a, w_proj_b, w_out, ln1_g, ln1_b, w_router,
              router_bias, w_gate_e, w_up_e, w_down_e, w_gate_s, w_up_s, w_down_s, ln2_g, ln2_b):
    xp, xs = x_prompt, x_sample
    kp_l, vp_l, ks_l, vs_l, cv_l = [], [], [], [], []
    for l in range(DEPTH):
        lp = {
            'w_in': w_in[l], 'b_in': b_in[l], 'attn_sinks': attn_sinks[l],
            'sg_ln_g': sg_ln_g[l], 'sg_ln_b': sg_ln_b[l], 'sg_w': sg_w[l], 'sg_b': sg_b[l],
            'w_proj_a': w_proj_a[l], 'w_proj_b': w_proj_b[l], 'w_out': w_out[l],
            'ln1_g': ln1_g[l], 'ln1_b': ln1_b[l], 'w_router': w_router[l], 'router_bias': router_bias[l],
            'w_gate_e': w_gate_e[l], 'w_up_e': w_up_e[l], 'w_down_e': w_down_e[l],
            'w_gate_s': w_gate_s[l], 'w_up_s': w_up_s[l], 'w_down_s': w_down_s[l],
            'ln2_g': ln2_g[l], 'ln2_b': ln2_b[l],
        }
        xp, kp, vp = prompt_layer(xp, lp, rel_bias_table)
        xs, nk, nv, cv = sample_layer(xs, cache_win_k[l], cache_win_v[l], lp, rel_bias_table)
        kp_l.append(kp); vp_l.append(vp); ks_l.append(nk); vs_l.append(nv); cv_l.append(cv)
    win_k_prompt = jnp.stack(kp_l)
    win_v_prompt = jnp.stack(vp_l)
    win_k_sample = jnp.stack(ks_l)
    win_v_sample = jnp.stack(vs_l)
    chunk_v_sample = jnp.stack(cv_l)
    return (xp, xs, win_k_prompt, win_v_prompt, win_k_sample, win_v_sample, chunk_v_sample)


_drawn_inputs = setup_inputs


def setup_inputs(seed=0):
    import zlib

    import numpy as np

    out = dict(_drawn_inputs(seed))
    spreads = {}
    factors = {'attn_sinks': 8.0, 'sg_ln_g': 8.63, 'sg_ln_b': 8.442, 'ln2_g': 7.722, 'ln2_b': 7.789}
    for name, (base, spread) in spreads.items():
        noise = np.random.default_rng([zlib.crc32(name.encode()), seed]).standard_normal(out[name].shape)
        drawn = base * np.exp(spread * noise) if base else spread * noise
        out[name] = __import__('jax').numpy.asarray(drawn.astype(out[name].dtype))
    for name, factor in factors.items():
        out[name] = (out[name] * factor).astype(out[name].dtype)
    return out
```

```python
from contextlib import ExitStack

import numpy as np

import concourse.bass as bass
from concourse import mybir

F32 = mybir.dt.float32
BF16 = mybir.dt.bfloat16
F32R = mybir.dt.float32r
I32 = mybir.dt.int32
U32 = mybir.dt.uint32
ALU = mybir.AluOpType
ACT = mybir.ActivationFunctionType
AX = mybir.AxisListType.X

P = 128
NEG_INF = -1e30
TAKEN = -3e38
LN_EPS = 1e-5
BUCKET_EXACT = 16
BUCKET_FAR = 128
UNROLL = 8
WSLOTS = 4
RAW = 4
SB = 256
IDX_AHEAD = 4


def bucket_ranges(n_buckets, window):
    def bucket(d):
        if d < BUCKET_EXACT:
            return d
        ratio = np.float32(d) / np.float32(BUCKET_EXACT)
        far = np.log(ratio) / np.float32(np.log(BUCKET_FAR / BUCKET_EXACT)) * np.float32(n_buckets - BUCKET_EXACT)
        return min(BUCKET_EXACT + int(far), n_buckets - 1)
    out = []
    for d in range(window + 1):
        b = bucket(d)
        if out and out[-1][0] == b:
            out[-1][2] = d
        else:
            out.append([b, d, d])
    return out


def hybrid_layer(nc, A, O):
    SEQ, D = A["x_prompt"].shape[1:]
    NSEQ, DS = A["x_sample"].shape[:2]
    WIN, KVH, HD = A["cache_win_k"].shape[2:]
    NBK, H = A["rel_bias_table"].shape
    G, CH = A["sg_w"].shape[1:3]
    E, _, FE = A["w_gate_e"].shape[1:]
    SGW = G * P
    QPK = H // KVH
    NG = 8
    EPG = E // NG
    TOPG = 4
    SCALE = HD ** -0.5
    ROUTED = 2.5
    ALPHA = 2.0 ** 0.25
    DC = D // P
    TOK = SEQ + NSEQ * DS
    PT = SEQ // P
    TILES = [(t * P, P) for t in range(PT)] + [(SEQ, NSEQ * DS)]
    NT = len(TILES)
    NS = NSEQ * DS
    QE = H * HD
    KE = QE + KVH * HD
    VE = KE + KVH * HD
    UE = VE + SGW
    VSE = UE + SGW
    GAE = VSE + D
    W2 = 2 * WIN
    assert WIN == P and CH == P and HD == 64 and KVH == 2 and DS == 8 and NS == 64 and DC == 8

    PITCH = 3 * WIN
    bias_rows = nc.dram_tensor("bias_rows", (H, P, PITCH), F32, kind="Internal").ap()
    x_lo_kept = nc.dram_tensor("x_lo_kept", (P, DC, TOK), F32, kind="Internal").ap()
    x1_rows = nc.dram_tensor("x1_rows", (TOK, D), F32, kind="Internal").ap()
    y_rows = nc.dram_tensor("y_rows", (TOK + P, D), F32, kind="Internal").ap()

    at = [(nc.sbuf_base + 31) // 32 * 32]
    names = [0]

    def place(name, shape, dt, offset):
        names[0] += 1
        return nc.alloc_sbuf_tensor_at(f"{name}_{names[0]}", shape, dt, offset=offset)

    def nbytes(shape, dt):
        n = 1
        for s in shape[1:]:
            n *= s
        return (n * (2 if dt == BF16 else 4) + 31) // 32 * 32

    def keep(name, shape, dt=F32):
        off = at[0]
        at[0] += nbytes(shape, dt)
        return place(name, shape, dt, off)

    def region(size):
        off = at[0]
        at[0] += size
        return off

    ident = keep("ident", [P, P])
    iota_row = keep("iota_row", [P, P])
    pcol = keep("pcol", [P, 1])
    trash = keep("trash", [P, 1])
    spare = keep("spare", [P, 3])
    eps = keep("eps", [P, 1])
    before = keep("before", [P, P], BF16)
    ones_b = keep("ones_b", [P, P], BF16)
    tie = keep("tie", [P, NG, NG])
    NB = (GAE + D) // P
    HALF = TOK // 2
    brow = keep("brow", [NB + KVH, P])
    bcol = keep("bcol", [P, NB + KVH])
    kbias = bcol[:, NB:NB + KVH]
    tm_bias = keep("tm_bias", [P, P + SGW])
    sgln = keep("sgln", [P, 2, SGW])
    sgb = keep("sgb", [P, G, P])
    ln_gb = keep("ln_gb", [P, 2, D])
    sink = keep("sink", [P, H])
    sink_row = keep("sink_row", [P, 1])
    table_t = keep("table_t", [H, NBK])
    e_row = keep("e_row", [H, PITCH])
    rbias = keep("rbias", [P, E])
    stat6 = keep("stat6", [P, 2, 6])
    mv = keep("mv", [P, NT, 2])
    std = keep("std", [P, NT])
    rstd = keep("rstd", [P, NT])
    nmr = keep("nmr", [P, NT])
    mx = keep("mx", [P, 4, 4])
    nm = keep("nm", [P, 4, 4])
    sd = keep("sd", [P, 4, 4])
    den = keep("den", [P, 4, 4])
    es = keep("es", [P, 4, 4])
    rden = keep("rden", [P, 4, 4])
    gate_idx = keep("gate_idx", [P, UNROLL, 2])
    idx_u = keep("idx_u", [P, UNROLL], U32)
    most = keep("most", [P, 1], I32)

    wslot_bytes = 3 * DC * FE * 4
    g0 = region(wslot_bytes)
    g_at = [g0]

    def in_g(name, shape, dt=F32):
        off = g_at[0]
        g_at[0] += nbytes(shape, dt)
        return place(name, shape, dt, off)

    vs_sb = in_g("vs", [P, NT, SGW])
    v_sb = in_g("v", [P, NT, KVH * HD])
    kcT = in_g("kcT", [P, NSEQ, KVH, WIN])
    qs = in_g("qs", [P, NSEQ, DC, DS])
    assert g_at[0] - g0 <= wslot_bytes
    c0 = region(max(wslot_bytes, (DC + G) * TOK * 4))
    AT = place("AT", [P, DC, TOK], F32, c0)
    uT = place("uT", [P, G, TOK], F32, c0 + DC * TOK * 4)
    b0 = region(wslot_bytes)
    qT = place("qT", [P, DC, TOK], F32, b0)
    mT = place("mT", [P, DC, TOK], F32, b0)
    i0 = b0 + DC * TOK * 4
    sgw = place("sgw", [P, G, P], F32, i0)
    sgwT = place("sgwT", [P, G, P], F32, i0 + G * P * 4)
    sgs = place("sgs", [NS, G, NS], F32, i0 + 2 * G * P * 4)
    sgsT = place("sgsT", [NS, G, NS], F32, i0 + 2 * G * P * 4 + G * NS * 4)
    assert i0 + 2 * G * P * 4 + 2 * G * NS * 4 <= b0 + wslot_bytes
    h0 = region(RAW * DC * SB * 4)
    raw = [place(f"raw{i}", [P, DC, SB], F32, h0 + i * DC * SB * 4) for i in range(RAW)]
    a0 = region(DC * TOK * 4)
    xT = place("xT", [P, DC, TOK], F32R, a0)
    xT_lo = place("xT_lo", [P, DC, TOK], F32R, c0)
    x1T = place("x1T", [P, DC, TOK], F32, a0)
    e0 = region(H * W2 * 4 + KVH * TOK * 4)
    rel = place("rel", [P, H, W2], F32, e0)
    kT = place("kT", [P, KVH, TOK], F32, e0 + H * W2 * 4)
    x_lo_back = place("x_lo_back", [P, DC, TOK], F32, e0)
    xT_lo2 = place("xT_lo2", [P, DC, TOK], F32R, e0)
    g_hi = [place(f"g_hi{i}", [P, DC, SB], F32R, g0 + i * DC * SB * 4) for i in range(2)]
    w_lo = [place(f"w_lo{i}", [P, DC, SB], F32R, h0 + i * DC * SB * 4) for i in range(RAW)]
    assert 2 * DC * SB * 4 <= wslot_bytes
    x1 = place("x1", [P, NT, D], F32, e0)
    assert NT * D * 4 <= H * W2 * 4 + KVH * TOK * 4
    f0 = region(NT * D * 4)
    x_in = place("x_in", [P, NT, D], F32, f0)
    w_hi = [place(f"w_hi{i}", [P, DC, SB], F32R, f0 + i * DC * SB * 4) for i in range(2)]
    LR = 3
    L = place("L", [P, LR, 4, W2], F32, f0)
    PTs = place("PTs", [P, 2, 4, 2, P], F32, f0 + LR * 4 * W2 * 4)
    assert LR * 4 * W2 * 4 + 2 * 8 * P * 4 <= NT * D * 4
    GA = place("GA", [P, 2, TOK], F32, f0)
    GB = place("GB", [P, 2, TOK], F32, f0 + 2 * TOK * 4)
    TA = place("TA", [P, 2, TOK], F32, f0 + 4 * TOK * 4)
    TB = place("TB", [P, 2, TOK], F32, f0 + 6 * TOK * 4)
    JBYTES = 20480
    j0 = region(JBYTES)
    j_at = [j0]

    def in_j(name, shape, dt=F32):
        off = j_at[0]
        j_at[0] += nbytes(shape, dt)
        assert j_at[0] <= j0 + JBYTES, name
        return place(name, shape, dt, off)

    rel_c = in_j("rel_c", [P, WIN + DS])
    rel_n = in_j("rel_n", [P, NSEQ, NS])
    vc = in_j("vc", [P, NSEQ, KVH * HD])
    kc = in_j("kc", [P, NSEQ, KVH, 2 * HD])
    kout = in_j("kout", [P, 2, KVH * HD])
    TS = in_j("TS", [P, 2, G, P])
    j_at[0] = j0
    wr = in_j("wr", [P, DC, E])
    scores = in_j("scores", [P, NT, E])
    sel = in_j("sel", [P, NT, E])
    selm = in_j("selm", [P, NT, E])
    R = in_j("R", [P, NT, E, 6], BF16)
    chosen = in_j("chosen", [P, NT, E], BF16)
    posm = in_j("posm", [P, NT, E])
    onehot = in_j("onehot", [P, 4, NT, P], BF16)
    hh = in_j("hh", [P, 2, FE])
    silu = in_j("silu", [P, FE])
    assert at[0] <= nc.sbuf_usable_end, (at[0], nc.sbuf_usable_end)

    w_at = [g0, c0, b0, h0]
    wgu = [place(f"wgu{i}", [P, 2, DC, FE], F32, w_at[i]) for i in range(WSLOTS)]
    wd = [place(f"wd{i}", [P, FE // P, D], F32, w_at[i] + 2 * DC * FE * 4) for i in range(WSLOTS)]
    y_at = h0 + wslot_bytes
    ysb = place("ysb", [P, 2, D], F32, y_at)
    assert y_at + 2 * D * 4 <= h0 + RAW * DC * SB * 4
    wgu_lo = [place(f"wgu_lo{i}", [P, 2, DC, FE], F32R, w_at[i]) for i in range(WSLOTS)]
    wgu_hi = [place(f"wgu_hi{i}", [P, 2, DC, FE], F32R, a0 + i * 2 * DC * FE * 4) for i in range(2)]
    hT_at = a0 + 2 * 2 * DC * FE * 4
    hT = place("hT", [P, 2, FE // P, P], F32, hT_at)
    xgT_lo = place("xgT_lo", [P, 2, DC, P], F32R, hT_at + 2 * FE * 4)
    xg = place("xg", [P, 2, D], F32, f0 + 4096)
    assert hT_at + 2 * FE * 4 + 2 * D * 4 <= f0 + 4096
    xgT = place("xgT", [P, 2, DC, P], F32R, f0 + 4096 + 2 * D * 4)
    assert 4096 + 4 * D * 4 <= NT * D * 4
    top = place("top", [P, NT, NG, 8], F32, f0)
    gsc = place("gsc", [P, NT, NG], F32, f0 + 2048)
    cmp_a = place("cmp_a", [P, NT, NG, NG], F32, f0 + 2304)
    cmp_b = place("cmp_b", [P, NT, NG, NG], F32, f0 + 4096)
    rank = place("rank", [P, NT, NG], F32, f0 + 5888)
    pen = place("pen", [P, NT, NG], F32, f0 + 6144)
    top8 = place("top8", [P, NT, 8], F32, f0 + 6400)
    wsum = place("wsum", [P, NT], F32, f0 + 6720)
    rsum = place("rsum", [P, NT], F32, f0 + 6784)
    gates = place("gates", [P, NT, E], F32, f0 + 6848)
    rest = place("rest", [P, NT, E], F32, f0 + 8192)
    smask = place("smask", [P, NT, E], F32, f0 + 9536)
    mostf = place("mostf", [P, 1], F32, f0 + 10880)
    swgu = place("swgu", [P, 2, DC, FE], F32, h0)
    swd = place("swd", [P, FE // P, D], F32, h0 + 2 * DC * FE * 4)
    ssilu = place("ssilu", [P, 2, FE], F32, f0 + 12288)
    sup = place("sup", [P, 2, FE], F32, f0 + 14336)
    shT = place("shT", [P, 2, FE // P, P], F32, f0 + 16384)
    sy = place("sy", [P, 2, D], F32, y_at)
    zero_row = place("zero_row", [P, D], F32, b0)

    bank = [nc.alloc_psum_tensor(f"bank{i}", [P, 512], F32) for i in range(8)]

    def sem(name):
        return nc.alloc_semaphore(name)

    def sems(name, n):
        return [sem(f"{name}{i}") for i in range(n)]

    w_in = A["w_in"][0]
    blocks = []

    def cols(w, a, n, kc=DC):
        return w[:, a:a + n].rearrange("(c p) n -> p c n", p=P), kc, n

    kparts = []
    for kv in range(KVH):
        for twice in range(2):
            kparts.append((2 * HD * kv + HD * twice, *cols(w_in, QE + HD * kv, HD)))
    blocks.append(("k", kparts))
    for s in range(QE // SB):
        blocks.append(("q", [(0, *cols(w_in, s * SB, SB))]))
    blocks.append(("v", [(0, *cols(w_in, KE, P))]))
    for s in range(SGW // SB):
        blocks.append(("vs", [(0, *cols(w_in, UE + s * SB, SB))]))
    for s in range(SGW // SB):
        blocks.append(("u", [(0, *cols(w_in, VE + s * SB, SB))]))
    for s in range(D // SB):
        blocks.append(("ga", [(0, *cols(w_in, VSE + s * SB, SB))]))
        blocks.append(("gb", [(0, *cols(w_in, GAE + s * SB, SB))]))
        blocks.append(("pa", [(0, *cols(A["w_proj_a"][0], s * SB, SB))]))
        blocks.append(("pb", [(0, *cols(A["w_proj_b"][0], s * SB, SB, G))]))
    for s in range(D // SB):
        blocks.append(("wo", [(0, *cols(A["w_out"][0], s * SB, SB))]))
    first_wo = len(blocks) - D // SB
    TMB = ("v", "vs")

    def block_landed(n):
        return sum(16 * len(blocks[m][1]) for m in range(n % RAW, n + 1, RAW))

    zprods = []
    seen = {}
    for n, (kind, _) in enumerate(blocks):
        if kind in TMB or kind == "wo":
            continue
        for j in range(SB // P):
            zprods.append((n, j, kind, seen.setdefault(kind, 0)))
            seen[kind] += 1
    BY_ACT = ("k", "q", "u", "ga", "gb")
    act_no = {}
    dve_no = {}
    for n, z in enumerate(zprods):
        d = act_no if z[2] in BY_ACT else dve_no
        d[n] = len(d) + 1
    stage_z = {k: [n for n, z in enumerate(zprods) if z[2] in k] for k in (("k", "q"), ("u",), ("ga", "gb", "pa", "pb"))}
    z_kq, z_u, z_merge = stage_z.values()

    split = [n for n, (kind, _) in enumerate(blocks) if kind in ("k", "q", "u", "ga", "gb") + TMB]
    split_no = {n: i for i, n in enumerate(split)}
    n_early = sum(1 for n in split if blocks[n][0] not in ("ga", "gb"))

    def hi_of(n):
        return (w_hi if split_no[n] < n_early else g_hi)[split_no[n] % 2]

    tms = []
    col = 0
    for n, (kind, parts) in enumerate(blocks):
        if kind in TMB:
            width = parts[0][3]
            tms += [(n, width, col, t) for t in range(NT)]
            col += width

    UP = PT * (H // 4)
    US = NSEQ // 2
    UA = UP + US
    rel_pair = [(kv, par) for kv in range(KVH) for par in range(2)]

    x_landed = sems("x_landed", NT)
    consts_landed = sem("consts_landed")
    sgw_landed = sem("sgw_landed")
    brow_landed = sem("brow_landed")
    bcol_pe = sem("bcol_pe")
    bcol_dve = sem("bcol_dve")
    kc_landed = sem("kc_landed")
    vc_landed = sem("vc_landed")
    table_landed = sem("table_landed")
    rel_written = sem("rel_written")
    rel_landed = sem("rel_landed")
    block_in = sems("block_in", RAW)
    x_again = sem("x_again")
    x_lo_stored = sem("x_lo_stored")
    x_lo_landed = sem("x_lo_landed")
    ln_swap = sem("ln_swap")
    wr_landed = sem("wr_landed")
    out_done = sem("out_done")
    out_done_act = sem("out_done_act")
    x1_written = sem("x1_written")
    y_inited = sems("y_inited", 2)
    y_zeroed = sem("y_zeroed")
    shared_landed = sem("shared_landed")
    y_back = sems("y_back", NT)

    pool_consts = sem("pool_consts")
    pool_table = sem("pool_table")
    pool_reln = sem("pool_reln")
    pool_sg = sem("pool_sg")
    pool_vs = sem("pool_vs")
    pool_norm = sem("pool_norm")
    pool_gated = sem("pool_gated")
    pool_merged = sem("pool_merged")
    pool_x1 = sem("pool_x1")
    pool_posm = sem("pool_posm")
    pool_sh = sem("pool_sh")
    pool_sy = sem("pool_sy")
    pool_scaled = sem("pool_scaled")
    pool_zero = sem("pool_zero")
    pool_final = sem("pool_final")

    xt_done = sem("xt_done")
    z_done = sem("z_done")
    tm_done = sem("tm_done")
    misc_done = sem("misc_done")
    logits_done = sem("logits_done")
    pt_done = sem("pt_done")
    pv_done = sem("pv_done")
    sg_done = sem("sg_done")
    wo_done_g = sem("wo_done_g")
    x1t_done = sem("x1t_done")
    route_done = sem("route_done")
    pos_done = sem("pos_done")
    sgu_done = sem("sgu_done")
    sht_done = sem("sht_done")
    sdn_done = sem("sdn_done")

    xt_act = sem("xt_act")
    hi_act = sem("hi_act")
    x_lo_act = sem("x_lo_act")
    z_act = sem("z_act")
    gelu_act = sem("gelu_act")
    std_act = sem("std_act")
    misc_act = sem("misc_act")
    exp_act = sem("exp_act")
    pt_act = sem("pt_act")
    pv_act = sem("pv_act")
    xn_act = sem("xn_act")
    x1t_act = sem("x1t_act")
    score_act = sem("score_act")
    ssilu_act = sem("ssilu_act")
    sht_act = sem("sht_act")
    sy_act = sem("sy_act")
    fin_act = sem("fin_act")

    dve = sem("dve")
    xt_dve = sem("xt_dve")
    lo_dve = sem("lo_dve")
    x_lo_dve = sem("x_lo_dve")
    z_dve = sem("z_dve")
    tm_dve = sem("tm_dve")
    stat_dve = sem("stat_dve")
    vsn_dve = sem("vsn_dve")
    misc_dve = sem("misc_dve")
    mx_dve = sem("mx_dve")
    rden_dve = sem("rden_dve")
    pt_dve = sem("pt_dve")
    sg_dve = sem("sg_dve")
    wo_dve = sem("wo_dve")
    nmr_dve = sem("nmr_dve")
    lng_dve = sem("lng_dve")
    x1t_dve = sem("x1t_dve")
    chosen_dve = sem("chosen_dve")
    route_dve = sem("route_dve")
    most_dve = sem("most_dve")

    wgu_in = sems("wgu_in", WSLOTS)
    wd_in = sems("wd_in", WSLOTS)
    xg_in = sems("xg_in", 2)
    y_added = sem("y_added")
    gathers_sent = sem("gathers_sent")
    scatters_sent = sem("scatters_sent")
    ex_xt = sem("ex_xt")
    ex_gu = sem("ex_gu")
    ex_ht = sem("ex_ht")
    ex_dn = sem("ex_dn")
    ex_list = sem("ex_list")
    xt_by_act = sem("xt_by_act")
    hi_by_act = sem("hi_by_act")
    silu_by_act = sem("silu_by_act")
    y_by_act = sem("y_by_act")
    xt_by_dve = sem("xt_by_dve")
    lo_by_dve = sem("lo_by_dve")
    h_by_dve = sem("h_by_dve")
    ht_by_dve = sem("ht_by_dve")
    y_by_dve = sem("y_by_dve")
    hot_by_dve = sem("hot_by_dve")
    sum_by_dve = sem("sum_by_dve")
    idx_by_dve = sem("idx_by_dve")
    over_dve = sem("over_dve")
    over_res = sem("over_res")

    N_CONST = 16
    N_CDMA = 13
    NSB = D // SB

    misc = []
    misc.append([("sg", g) for g in range(G)])
    misc.append([("sgs", g) for g in range(G)])
    for b in range(0, NSEQ, 2):
        misc.append([("kc", b), ("kc", b + 1)])
    misc.append([("kout", 0), ("kout", 1)])

    def dram(ap, offset, pattern):
        return bass.AP(ap.tensor, ap.offset + offset, pattern)

    def expert_weights(e):
        one = bass.ds(e, 1)
        return (A["w_gate_e"][0][one].rearrange("a (p c) f -> p (a c) f", p=P),
                A["w_up_e"][0][one].rearrange("a (p c) f -> p (a c) f", p=P),
                A["w_down_e"][0][one].rearrange("a (p j) n -> p (a j) n", p=P))

    ident_a = ident[:, :]
    block_ctx = ExitStack()
    with block_ctx:
        block = block_ctx.enter_context(nc.Block())

        @block.sync
        def _(sp):
            for t, (a, w) in enumerate(TILES):
                src = A["x_prompt"][0][a:a + w, :] if t < PT else A["x_sample"].rearrange("b s d -> (b s) d")
                sp.dma_start(x_in[0:w, t, :], src).then_inc(x_landed[t], 16)

            def load(dst, src, s=consts_landed, few=False):
                sp.dma_start(dst, src, allow_slow_non_contiguous=few).then_inc(s, 16)

            def load_block(n):
                if n >= RAW:
                    kind = blocks[n - RAW][0]
                    if kind in TMB:
                        sp.wait_ge(tm_done, 1 + max(g for g, x in enumerate(tms) if x[0] == n - RAW))
                    else:
                        sp.wait_ge(z_done, 1 + max(g for g, x in enumerate(zprods) if x[0] == n - RAW))
                for c0_, src, kc_, w_ in blocks[n][1]:
                    sp.dma_start(raw[n % RAW][:, 0:kc_, c0_:c0_ + w_], src).then_inc(block_in[n % RAW], 16)

            def load_expert(e, u, free=None):
                slot = u % WSLOTS
                if free is not None:
                    sp.wait_ge(ex_gu, free)
                g_, up_, dn_ = expert_weights(e)
                sp.dma_start(wgu[slot][:, 0, :, :], g_).then_inc(wgu_in[slot], 16)
                sp.dma_start(wgu[slot][:, 1, :, :], up_).then_inc(wgu_in[slot], 16)
                if free is not None:
                    sp.wait_ge(ex_dn, free)
                sp.dma_start(wd[slot][:, :, :], dn_).then_inc(wd_in[slot], 16)

            merge_first = zprods[z_merge[0]][0]
            last_gate = max(g for g in z_merge if zprods[g][2] == "gb")
            for n in range(len(blocks)):
                if n == RAW:
                    load(tm_bias[:, 0:P], A["b_in"][0:1, KE:VE].to_broadcast([P, P]))
                    load(tm_bias[:, P:], A["b_in"][0:1, UE:VSE].to_broadcast([P, SGW]))
                    load(sgln[:, 0, :], A["sg_ln_g"].to_broadcast([P, SGW]))
                    load(sgln[:, 1, :], A["sg_ln_b"].to_broadcast([P, SGW]))
                    load(sgb[:], A["sg_b"].rearrange("a g i -> a (g i)").to_broadcast([P, G * P]).rearrange("p (g i) -> p g i", g=G))
                    load(ln_gb[:, 0, :], A["ln1_g"].to_broadcast([P, D]))
                    load(ln_gb[:, 1, :], A["ln1_b"].to_broadcast([P, D]))
                    load(sink[:], A["attn_sinks"].to_broadcast([P, H]))
                    load(rbias[:], A["router_bias"].to_broadcast([P, E]))
                    for kv, par in rel_pair:
                        r0 = 32 * (2 * par + kv)
                        load(sink_row[r0:r0 + 32, :], dram(A["attn_sinks"], kv * QPK + par, [[2, 4], [0, DS], [1, 1]]), few=True)
                    sp.wait_ge(pool_consts, N_CONST)
                    load(sgw[:], A["sg_w"][0].rearrange("g i j -> i g j"), sgw_landed)
                    for b in range(NSEQ):
                        load(sgs[b * DS:(b + 1) * DS, :, b * DS:(b + 1) * DS],
                             A["sg_w"][0].rearrange("g i j -> i g j")[0:DS, :, 0:DS], sgw_landed)
                    load(vc[:], A["cache_win_v"][0].rearrange("b w h d -> w b (h d)"), vc_landed)
                    sp.wait_ge(xt_dve, 2 * NT)
                    sp.dma_start(x_lo_kept, xT_lo[:].bitcast(F32)).then_inc(x_lo_stored, 16)
                if n == merge_first + RAW:
                    sp.wait_ge(mx_dve, UA)
                    sp.wait_ge(x_lo_stored, 16)
                    sp.dma_start(x_lo_back[:], x_lo_kept).then_inc(x_lo_landed, 16)
                if n == first_wo + 2:
                    sp.wait_ge(z_done, last_gate + 1)
                    for t, (a, w) in enumerate(TILES):
                        src = A["x_prompt"][0][a:a + w, :] if t < PT else A["x_sample"].rearrange("b s d -> (b s) d")
                        sp.dma_start(x1[0:w, t, :], src).then_inc(x_again, 16)
                    load_expert(0, 0)
                load_block(n)
                if n == first_wo - 9:
                    sp.wait_ge(misc_dve, 1)
                    sp.dma_start(O["win_k_prompt"][0, 0].rearrange("w h d -> w (h d)"), kout[:, 0, :]).then_inc(out_done_act, 16)
                    sp.dma_start(O["win_k_sample"][0].rearrange("b w h d -> b w (h d)")[:, WIN - DS:WIN, :],
                                 kout[0:NS, 1, :]).then_inc(out_done_act, 16)
                if n == merge_first:
                    sp.wait_ge(tm_dve, NT)
                    sp.dma_start(O["win_v_prompt"][0, 0].rearrange("w h d -> w (h d)"), v_sb[:, PT - 1, :]).then_inc(out_done, 16)
                    sp.dma_start(O["win_v_sample"][0].rearrange("b w h d -> b w (h d)")[:, WIN - DS:WIN, :],
                                 v_sb[0:NS, PT, :]).then_inc(out_done, 16)
                    sp.wait_ge(pool_vs, NT)
                    sp.dma_start(O["chunk_v_sample"][0].rearrange("b s g c -> (b s) (g c)"), vs_sb[0:NS, PT, :]).then_inc(out_done, 16)
            for src, dst in ((A["cache_win_k"], O["win_k_sample"]), (A["cache_win_v"], O["win_v_sample"])):
                sp.dma_start(dst[0].rearrange("b w h d -> b w (h d)")[:, 0:WIN - DS, :],
                             src[0].rearrange("b w h d -> b w (h d)")[:, DS:WIN, :]).then_inc(out_done_act, 16)
            sp.wait_ge(pool_merged, D // P)
            load_expert(1, 1)
            sp.wait_ge(wo_done_g, NT * NSB)
            sg_, su_, sdn_ = (A["w_gate_s"][0].rearrange("(p c) f -> p c f", p=P),
                              A["w_up_s"][0].rearrange("(p c) f -> p c f", p=P),
                              A["w_down_s"][0].rearrange("(p j) n -> p j n", p=P))
            sp.dma_start(swgu[:, 0, :, :], sg_).then_inc(shared_landed, 16)
            sp.dma_start(swgu[:, 1, :, :], su_).then_inc(shared_landed, 16)
            sp.dma_start(swd[:, :, :], sdn_).then_inc(shared_landed, 16)
            sp.wait_ge(y_zeroed, 16)
            load_expert(2, 2)
            for t, (a, w) in enumerate(TILES):
                sp.wait_ge(pool_x1, t + 1)
                sp.dma_start(x1_rows[a:a + w, :], x1[0:w, t, :]).then_inc(x1_written, 16)
            sp.wait_ge(pool_x1, NT)
            for i, nm_ in enumerate(("ln2_g", "ln2_b")):
                sp.dma_start(ln_gb[:, i, :], A[nm_].to_broadcast([P, D])).then_inc(ln_swap, 16)
            for t, (a, w) in enumerate(TILES):
                sp.wait_ge(pool_sy, t + 1)
                sp.dma_start(y_rows[a:a + w, :], sy[0:w, t % 2, :]).then_inc(y_inited[t % 2], 16)
            sp.wait_ge(sdn_done, NT)
            load_expert(3, 3)
            for e in range(WSLOTS, UNROLL):
                load_expert(e, e, e - WSLOTS + 1)
            with sp.Fori(1, E // UNROLL) as i:
                for u in range(UNROLL):
                    load_expert(i * UNROLL + u, u, i * UNROLL + (u - WSLOTS + 1))

            sp.wait_ge(most_dve, 1)
            sp.wait_ge(ex_dn, E)
            most_r = sp.value_load(most[0:1, 0:1], min_val=0, max_val=TOK)
            with sp.If(most_r > P):
                for tile in range(1, NT):
                    with sp.Fori(0, E) as e:
                        done = e + (E * tile)
                        sp.wait_ge(ex_dn, done)
                        g_, up_, dn_ = expert_weights(e)
                        sp.dma_start(wgu[0][:, 0, :, :], g_).then_inc(wgu_in[0], 16)
                        sp.dma_start(wgu[0][:, 1, :, :], up_).then_inc(wgu_in[0], 16)
                        sp.dma_start(wd[0][:, :, :], dn_).then_inc(wd_in[0], 16)
                sp.wait_ge(y_added, 16 * E * NT)
            sp.wait_ge(y_added, 16 * E)
            for t, (a, w) in enumerate(TILES):
                sp.dma_start(x1[0:w, t, :], y_rows[a:a + w, :]).then_inc(y_back[t], 16)
            for t, (a, w) in enumerate(TILES):
                sp.wait_ge(pool_final, t + 1)
                dst = O["y_prompt"][0][a:a + w, :] if t < PT else O["y_sample"].rearrange("b s d -> (b s) d")
                sp.dma_start(dst, x1[0:w, t, :]).then_inc(out_done, 16)
            sp.wait_ge(out_done, 16 * (3 + NT))
            sp.wait_ge(out_done_act, 16 * 4)

        @block.gpsimd
        def _(pool):
            def signal(ins, s, n=[0]):
                ins.then_inc(s, 1)
                return ins

            k = [0]

            def const(ins):
                k[0] += 1
                ins.then_inc(pool_consts, 1)

            const(pool.memset(ident[:], 0.0))
            const(pool.memset(eps[:], LN_EPS))
            const(pool.iota(iota_row[:], [[1, P]], base=0, channel_multiplier=0, allow_small_or_imprecise_dtypes=True))
            const(pool.iota(pcol[:], [[0, 1]], base=0, channel_multiplier=1, allow_small_or_imprecise_dtypes=True))
            const(pool.iota(trash[:], [[0, 1]], base=TOK, channel_multiplier=1, allow_small_or_imprecise_dtypes=True))
            const(pool.memset(before[:], 1.0))
            const(pool.memset(ones_b[:], 1.0))
            const(pool.memset(tie[:], 1.0))
            const(pool.memset(e_row[:], NEG_INF))
            const(pool.memset(rel_n[:], NEG_INF))
            const(pool.memset(sgs[:], 0.0))
            const(pool.memset(mv[:], 1.0))
            const(pool.memset(spare[:], 1.0))
            n_set = k[0]
            pool.wait_ge(pool_consts, n_set)
            const(pool.affine_select(out=ident[:], in_=ident[:], compare_op=ALU.not_equal, fill=1.0, base=0,
                                     pattern=[[-1, P]], channel_multiplier=1))
            const(pool.affine_select(out=before[:], in_=before[:], compare_op=ALU.is_gt, fill=0.0, base=0,
                                     pattern=[[1, P]], channel_multiplier=-1))
            const(pool.affine_select(out=tie[:], in_=tie[:], compare_op=ALU.is_gt, fill=0.0, base=0,
                                     pattern=[[1, NG], [-1, NG]], channel_multiplier=0))
            assert k[0] == N_CONST
            pool.wait_ge(table_landed, 16)
            ranges = bucket_ranges(NBK, WIN)
            for b, lo, hi in ranges:
                pool.tensor_copy(e_row[:, W2 - 1 - hi:W2 - lo],
                                 table_t[:, b:b + 1].to_broadcast([H, hi - lo + 1])).then_inc(pool_table, 1)
            pool.wait_ge(pool_table, len(ranges))
            src = e_row[:, :]
            pool.dma_start(bias_rows.rearrange("h p n -> h p n"),
                           src.rearrange("h (a n) -> h a n", a=1).to_broadcast([H, P, PITCH])).then_inc(rel_written, 16)
            pool.wait_ge(sgw_landed, 16 * (1 + NSEQ))
            pool.affine_select(out=sgw[:], in_=sgw[:], compare_op=ALU.is_ge, fill=0.0, base=0,
                               pattern=[[0, G], [-1, P]], channel_multiplier=1).then_inc(pool_sg, 1)
            pool.affine_select(out=sgs[:], in_=sgs[:], compare_op=ALU.is_ge, fill=0.0, base=0,
                               pattern=[[0, G], [-1, NS]], channel_multiplier=1).then_inc(pool_sg, 1)
            pool.wait_ge(rel_landed, 16 * 5)
            for b in range(NSEQ):
                pool.tensor_copy(rel_n[:, b, b * DS:(b + 1) * DS], rel_c[:, WIN:WIN + DS]).then_inc(pool_reln, 1)

            def norm(u):
                pool.wait_ge(rden_dve, u + 1)
                if u < UP:
                    lo = WIN if u < 4 else 0
                    n, a = 4, L[:, u % LR, 0:4, lo:W2]
                    w = W2 - lo
                else:
                    n, a, w = 2, L[:, u % LR, 0:2, 0:WIN + NS], WIN + NS
                r = rden[:, u % 4, 0:n].rearrange("p (n a) -> p n a", a=1).to_broadcast([P, n, w])
                pool.tensor_tensor(a, a, r, ALU.mult).then_inc(pool_norm, 1)

            pool.wait_ge(consts_landed, N_CDMA * 16)
            for t, (a, w) in enumerate(TILES):
                pool.wait_ge(vsn_dve, 2 * t + 2)
                pool.tensor_tensor(vs_sb[0:w, t, :], vs_sb[0:w, t, :], sgln[0:w, 1, :], ALU.add).then_inc(pool_vs, 1)
            for u in range(UA):
                norm(u)
            for t, (a, w) in enumerate(TILES):
                pool.wait_ge(sg_dve, t + 1)
                pool.tensor_tensor(uT[:, :, a:a + w], uT[:, :, a:a + w], TS[:, t % 2, :, 0:w], ALU.mult).then_inc(pool_gated, 1)
            for m in range(D // P):
                pool.wait_ge(z_dve, 2 * (m // 2) * 2 + 2 + m % 2 + 1)
                pool.tensor_tensor(mT[:, m, :], TA[:, m % 2, :], TB[:, m % 2, :], ALU.add).then_inc(pool_merged, 1)
            pool.wait_ge(wo_done_g, NT * NSB)
            pool.memset(zero_row[:], 0.0).then_inc(pool_zero, 1)
            pool.wait_ge(pool_zero, 1)
            pool.dma_start(y_rows[TOK:TOK + P, :], zero_row[:]).then_inc(y_zeroed, 16)
            for t, (a, w) in enumerate(TILES):
                pool.wait_ge(lng_dve, t + 1)
                pool.tensor_tensor(x1[0:w, t, :], x1[0:w, t, :], ln_gb[0:w, 1, :], ALU.add).then_inc(pool_x1, 1)
            def shared_y(t):
                w = TILES[t][1]
                pool.wait_ge(sy_act, 2 * (t + 1))
                pool.tensor_tensor(sy[0:w, t % 2, :], sy[0:w, t % 2, :], x1[0:w, t, :], ALU.add).then_inc(pool_sy, 1)

            pool.wait_ge(x1_written, 16 * NT)
            pool.wait_ge(x1t_done, 2 * NT)
            for t, (a, w) in enumerate(TILES):
                pool.tensor_scalar(x1[0:w, t, :], x1[0:w, t, :], ALPHA, None, ALU.mult).then_inc(pool_scaled, 1)
            pool.wait_ge(pool_scaled, NT)
            for t, (a, w) in enumerate(TILES):
                pool.wait_ge(ssilu_act, 2 * (t + 1))
                pool.tensor_tensor(ssilu[0:w, t % 2, :], ssilu[0:w, t % 2, :], sup[0:w, t % 2, :], ALU.mult).then_inc(pool_sh, 1)
                if t >= 1:
                    shared_y(t - 1)
            shared_y(NT - 1)

            pool.wait_ge(x1_written, 16 * NT)
            pool.wait_ge(y_inited[0], 16 * ((NT + 1) // 2))
            pool.wait_ge(y_inited[1], 16 * (NT // 2))
            pool.wait_ge(y_zeroed, 16)
            pool.wait_ge(route_dve, 1)

            bound = pool.to_reg(TOK - 1)

            def sent(n, s, i):
                if not (isinstance(n, int) and n == 0):
                    pool.wait_ge(s, n)
                pool.tensor_tensor(spare[:, i:i + 1], spare[:, 0:1], spare[:, 0:1], ALU.mult).then_inc(s, 1)

            def gather(e, u, landed=None):
                pool.wait_ge(idx_by_dve, e + 1)
                if landed is not False:
                    pool.wait_ge(ex_xt, e - 1)
                sent(e, gathers_sent, 1)
                pool.indirect_dma_start(out=xg[:, u % 2, :], out_offset=None, in_=x1_rows,
                                        in_offset=bass.IndirectOffsetOnAxis(idx_u[:, u:u + 1], 0),
                                        bounds_check=bound, oob_is_err=False).then_inc(xg_in[u % 2], 16)

            def scatter(e, u, first=False):
                pool.wait_ge(y_by_act, e + 1)
                pool.wait_ge(y_by_dve, e + 1)
                if not first:
                    pool.wait_ge(y_added, 16 * e)
                sent(e, scatters_sent, 2)
                pool.indirect_dma_start(out=y_rows, out_offset=bass.IndirectOffsetOnAxis(idx_u[:, u:u + 1], 0),
                                        in_=ysb[:, u % 2, :], in_offset=None, compute_op=ALU.add).then_inc(y_added, 16)

            pool.memset(xg[:], 0.0).then_inc(pool_posm, 1)
            pool.wait_ge(pool_posm, 1)
            gather(0, 0, False)
            gather(1, 1, False)
            for e in range(UNROLL):
                gather(e + 2, (e + 2) % UNROLL)
                if e >= 1:
                    scatter(e - 1, e - 1, e == 1)
            with pool.Fori(1, E // UNROLL - 1) as i:
                for u in range(UNROLL):
                    gather(i * UNROLL + (u + 2), (u + 2) % UNROLL)
                    scatter(i * UNROLL + (u - 1), (u - 1) % UNROLL)
            for e in range(E - UNROLL, E):
                if e + 2 < E:
                    gather(e + 2, (e + 2) % UNROLL)
                scatter(e - 1, (e - 1) % UNROLL)
            scatter(E - 1, UNROLL - 1)

            pool.wait_ge(y_added, 16 * E)
            most_r = pool.value_load(most[0:1, 0:1], min_val=0, max_val=TOK)
            with pool.If(most_r > P):
                for tile in range(1, NT):
                    with pool.Fori(0, E) as e:
                        n = e + E * tile
                        pool.wait_ge(idx_by_dve, n + 1)
                        pool.wait_ge(ex_xt, n)
                        sent(n, gathers_sent, 1)
                        pool.indirect_dma_start(out=xg[:, 0, :], out_offset=None, in_=x1_rows,
                                                in_offset=bass.IndirectOffsetOnAxis(idx_u[:, 0:1], 0),
                                                bounds_check=bound, oob_is_err=False).then_inc(xg_in[0], 16)
                        pool.wait_ge(y_by_act, n + 1)
                        pool.wait_ge(y_by_dve, n + 1)
                        sent(n, scatters_sent, 2)
                        pool.indirect_dma_start(out=y_rows, out_offset=bass.IndirectOffsetOnAxis(idx_u[:, 0:1], 0),
                                                in_=ysb[:, 0, :], in_offset=None, compute_op=ALU.add).then_inc(y_added, 16)
                        pool.wait_ge(y_added, 16 * n + 16)
            for t, (a, w) in enumerate(TILES):
                pool.wait_ge(lng_dve, NT + t + 1)
                pool.tensor_tensor(x1[0:w, t, :], x1[0:w, t, :], ln_gb[0:w, 1, :], ALU.add).then_inc(pool_final, 1)

        @block.scalar
        def _(act):
            def load(dst, src, s=consts_landed, few=False):
                act.dma_start(dst, src, allow_slow_non_contiguous=few).then_inc(s, 16)

            load(table_t[:], A["rel_bias_table"].rearrange("b h -> h b"), table_landed, few=True)
            load(brow[0:NB, :], A["b_in"].rearrange("a (c p) -> (a c) p", p=P), brow_landed)
            load(brow[NB:NB + KVH, :].rearrange("k (t d) -> k t d", t=2), dram(A["b_in"], QE, [[HD, KVH], [0, 2], [1, HD]]),
                 brow_landed)
            def load_kc(b):
                load(kc[:, b, :, :].rearrange("p k (t d) -> p k t d", t=2),
                     dram(A["cache_win_k"], b * WIN * KVH * HD, [[KVH * HD, P], [HD, KVH], [0, 2], [1, HD]]),
                     kc_landed)
            for t, (a, w) in enumerate(TILES):
                for h in range(2):
                    act.wait_ge(xt_done, 2 * t + h + 1)
                    act.activation(xT[:, 4 * h:4 * h + 4, a:a + w],
                                   bank[2 * (t % 2) + h][:, 0:4 * w].rearrange("p (c n) -> p c n", c=4),
                                   ACT.Copy).then_inc(xt_act, 1)

            def split_hi(n):
                act.wait_ge(block_in[n % RAW], block_landed(n))
                w_ = blocks[n][1][-1][0] + blocks[n][1][-1][3]
                act.activation(hi_of(n)[:, :, 0:w_], raw[n % RAW][:, :, 0:w_], ACT.Copy).then_inc(hi_act, 1)

            split_hi(split[0])
            split_hi(split[1])
            for b in range(NSEQ):
                load_kc(b)
            act.wait_ge(bcol_dve, 1)

            def z_evac(n):
                _, _, kind, m = zprods[n]
                act.wait_ge(z_done, n + 1)
                if kind == "k":
                    dst, b_, fn = kT[:, m, :], kbias[:, m:m + 1], ACT.Identity
                elif kind == "q":
                    dst, b_, fn = qT[:, m, :], bcol[:, m:m + 1], ACT.Identity
                elif kind == "u":
                    dst, b_, fn = uT[:, m, :], bcol[:, VE // P + m:VE // P + m + 1], ACT.Gelu_apprx_tanh
                else:
                    off = (VSE if kind == "ga" else GAE) // P + m
                    dst, b_, fn = (GA if kind == "ga" else GB)[:, m % 2, :], bcol[:, off:off + 1], ACT.Sigmoid
                    if m >= 2:
                        act.wait_ge(z_dve, 4 * (m // 2 - 1) + (2 if kind == "ga" else 4))
                act.activation(dst[:, 0:HALF], bank[n % 2][:, 0:HALF], fn, bias=b_)
                src = bank[2 + n % 2][:, SEQ - HALF:HALF]
                if kind == "q":
                    act.activation(dst[:, HALF:SEQ], bank[2 + n % 2][:, 0:SEQ - HALF], fn, bias=b_)
                    act.activation(qs[:, :, m, :], src.rearrange("p (b e) -> p b e", b=NSEQ), fn, bias=b_).then_inc(z_act, 1)
                else:
                    act.activation(dst[:, HALF:TOK], bank[2 + n % 2][:, 0:HALF], fn, bias=b_).then_inc(z_act, 1)

            for i in range(n_early):
                nb = split[i]
                for n, z in enumerate(zprods):
                    if z[0] == nb:
                        z_evac(n)
                if i == 0:
                    act.wait_ge(rel_written, 16)
                    load(rel[:], dram(bias_rows, WIN - 1, [[PITCH - 1, P], [P * PITCH, H], [1, W2]]), rel_landed)
                    for kv, par in rel_pair:
                        r0 = 32 * (2 * par + kv)
                        load(rel_c[r0:r0 + 32, :], dram(bias_rows, (kv * QPK + par) * P * PITCH + WIN - 1,
                                                        [[2 * P * PITCH, 4], [PITCH - 1, DS], [1, WIN + DS]]), rel_landed)
                if blocks[nb][0] == "u" and blocks[nb - 1][0] != "u":
                    act.wait_ge(stat_dve, NT)
                    act.activation(std[:, :], mv[:, :, 1], ACT.Sqrt, bias=eps[:, 0:1]).then_inc(std_act, 1)
                if i + 2 < n_early:
                    if blocks[nb][0] in TMB:
                        act.wait_ge(tm_done, 1 + max(g for g, x in enumerate(tms) if x[0] == nb))
                    split_hi(split[i + 2])
                if i == split_no[tms[-1][0]]:
                    for t, (a, w) in enumerate(TILES):
                        act.wait_ge(tm_dve, NT * 2 + t + 1)
                        act.activation(vs_sb[0:w, t, :], vs_sb[0:w, t, :], ACT.Gelu_apprx_tanh).then_inc(gelu_act, 1)
            for g, items in enumerate(misc):
                if items[0][0] == "sg":
                    act.wait_ge(misc_done, g + 1)
                    act.activation(sgwT[:], bank[6 + g % 2][:, :].rearrange("p (g n) -> p g n", g=G), ACT.Copy).then_inc(misc_act, 1)
                elif items[0][0] == "sgs":
                    act.wait_ge(misc_done, g + 1)
                    act.activation(sgsT[:], bank[6 + g % 2][0:NS, 0:G * NS].rearrange("p (g n) -> p g n", g=G),
                                   ACT.Copy).then_inc(misc_act, 1)
                elif items[0][0] == "kc":
                    b = items[0][1]
                    act.wait_ge(misc_done, g + 1)
                    act.activation(kcT[:, b:b + 2, :, :], bank[6 + g % 2][:, :].rearrange("p (b k n) -> p b k n", b=2, k=KVH),
                                   ACT.Copy).then_inc(misc_act, 1)
            def exps(u):
                act.wait_ge(mx_dve, u + 1)
                k_ = u % LR
                if u < UP:
                    lo, n, w = (WIN if u < 4 else 0), 4, W2
                else:
                    lo, n, w = 0, 2, WIN + NS
                for j in range(n):
                    act.activation(L[:, k_, j, lo:w], L[:, k_, j, lo:w], ACT.Exp, bias=nm[:, u % 4, j:j + 1],
                                   accum_out=den[:, u % 4, j:j + 1])
                act.activation(es[:, u % 4, 0:n], sd[:, u % 4, 0:n], ACT.Exp).then_inc(exp_act, 1)

            def pt_evac(u):
                act.wait_ge(pt_done, u + 1)
                if u >= 2:
                    act.wait_ge(pv_done, u - 1)
                if u < UP:
                    h0_ = 1 if u < 4 else 0
                    act.activation(PTs[:, u % 2, 0:2, h0_:2, :],
                                   bank[4][:, :].rearrange("p (j h n) -> p j h n", j=2, h=2)[:, :, h0_:2, :],
                                   ACT.Copy).then_inc(pt_act, 1)
                else:
                    act.activation(PTs[:, u % 2, 0:2, 0, :], bank[4][:, 0:256].rearrange("p (j n) -> p j n", j=2),
                                   ACT.Copy).then_inc(pt_act, 1)

            act.wait_ge(x_lo_stored, 16)

            def pv_evac(u):
                act.wait_ge(pv_done, u + 1)
                if u < UP:
                    b, hg = u // 4, u % 4
                    act.activation(AT[:, 2 * hg:2 * hg + 2, b * P:(b + 1) * P],
                                   bank[6 + u % 2][:, 0:2 * P].rearrange("p (c n) -> p c n", c=2), ACT.Copy).then_inc(pv_act, 1)
                else:
                    a = SEQ + (u - UP) * 2 * DS
                    act.activation(AT[:, :, a:a + 2 * DS].rearrange("p c (q e) -> p c q e", q=2),
                                   bank[6 + u % 2][:, 0:2 * DC * DS].rearrange("p (q c e) -> p c q e", q=2, c=DC),
                                   ACT.Copy).then_inc(pv_act, 1)

            for m in range(UA + 5):
                if 0 <= m - 4 < UA:
                    pt_evac(m - 4)
                if 0 <= m - 2 < UA:
                    exps(m - 2)
                if 0 <= m - 4 < UA:
                    pv_evac(m - 4)
            act.wait_ge(sg_done, NT)
            act.wait_ge(out_done, 16 * 3)
            for i in range(n_early, n_early + 2):
                split_hi(split[i])
            act.wait_ge(x_lo_landed, 16)
            act.activation(xT_lo2[:, 0:4, :], x_lo_back[:, 0:4, :], ACT.Copy).then_inc(x_lo_act, 1)
            for i in range(n_early, len(split)):
                for n in z_merge:
                    if zprods[n][0] == split[i]:
                        z_evac(n)
                if blocks[split[i]][0] == "gb" and i + 2 < len(split):
                    split_hi(split[i + 1])
                    split_hi(split[i + 2])
            def layer_norm_rows(first, s):
                for t, (a, w) in enumerate(TILES):
                    act.wait_ge(stat_dve, NT * (1 + first) + t + 1)
                    act.activation(std[0:w, t:t + 1], mv[0:w, t, 1:2], ACT.Sqrt, bias=eps[0:w, 0:1]).then_inc(std_act, 1)
                    act.wait_ge(nmr_dve, first * NT + t + 1)
                    act.activation(x1[0:w, t, :], x1[0:w, t, :], ACT.Identity, bias=nmr[0:w, t:t + 1],
                                   scale=rstd[0:w, t:t + 1]).then_inc(s, 1)
            act.wait_ge(mx_dve, UA)
            load(wr[:], A["w_router"][0].rearrange("(p c) e -> p c e", p=P), wr_landed)
            layer_norm_rows(0, xn_act)
            for t, (a, w) in enumerate(TILES):
                act.wait_ge(x1t_done, 2 * t + 1)
                act.activation(x1T[:, 0:4, a:a + w], bank[2 * (t % 2)][:, 0:4 * w].rearrange("p (c n) -> p c n", c=4),
                               ACT.Copy).then_inc(x1t_act, 1)
            act.wait_ge(route_done, NT)
            for t, (a, w) in enumerate(TILES):
                act.activation(scores[0:w, t, :], bank[4][0:w, t * E:(t + 1) * E], ACT.Sigmoid).then_inc(score_act, 1)

            def sh_silu(t):
                w = TILES[t][1]
                act.wait_ge(sgu_done, t + 1)
                if t >= 2:
                    act.wait_ge(sht_done, t - 1)
                act.activation(ssilu[0:w, t % 2, :], bank[5][0:w, 0:FE], ACT.Silu).then_inc(ssilu_act, 1)
                act.activation(sup[0:w, t % 2, :], bank[5][0:w, FE:2 * FE], ACT.Copy).then_inc(ssilu_act, 1)

            def sh_rest(t):
                w = TILES[t][1]
                act.wait_ge(sht_done, t + 1)
                if t >= 2:
                    act.wait_ge(sdn_done, t - 1)
                act.activation(shT[:, t % 2, :, 0:w], bank[6][:, 0:2 * w].rearrange("p (j n) -> p j n", j=2),
                               ACT.Copy).then_inc(sht_act, 1)

            def sh_out(t):
                w = TILES[t][1]
                act.wait_ge(sdn_done, t + 1)
                if t >= 2:
                    act.wait_ge(y_inited[t % 2], 16 * (t // 2))
                for j in range(2):
                    act.activation(sy[0:w, t % 2, j * 512:(j + 1) * 512], bank[j][0:w, :], ACT.Copy).then_inc(sy_act, 1)

            for t in range(NT + 1):
                if t < NT:
                    sh_silu(t)
                if t >= 1:
                    sh_out(t - 1)
                if t < NT:
                    sh_rest(t)

            def ex_xt_evac(e, u):
                act.wait_ge(ex_xt, e + 1)
                for h in range(2):
                    act.activation(xgT[:, u % 2, 4 * h:4 * h + 4, :], bank[h][:, :].rearrange("p (c n) -> p c n", c=4),
                                   ACT.Copy).then_inc(xt_by_act, 1)

            def ex_hi(u, landed):
                act.wait_ge(wgu_in[u % WSLOTS], landed * 32)
                act.activation(wgu_hi[u % 2][:], wgu[u % WSLOTS][:], ACT.Copy).then_inc(hi_by_act, 1)

            def ex_silu(e, u):
                act.wait_ge(ex_gu, e + 1)
                act.activation(silu[:], bank[2][:, 0:FE], ACT.Silu).then_inc(silu_by_act, 1)

            def ex_y(e, u, free=True):
                act.wait_ge(ex_dn, e + 1)
                if free:
                    act.wait_ge(y_added, (e - 1) * 16)
                act.activation(ysb[:, u % 2, 0:512], bank[3][:, :], ACT.Copy).then_inc(y_by_act, 1)

            act.wait_ge(y_inited[0], 16 * ((NT + 1) // 2))
            act.wait_ge(y_inited[1], 16 * (NT // 2))
            ex_hi(0, 1)
            ex_xt_evac(0, 0)
            ex_hi(1, 1)

            def step(e, u, turn, first=False, last=False, ahead=True, free=True):
                if not last:
                    ex_xt_evac(e + 1, u + 1)
                if not first:
                    act.wait_ge(h_by_dve, e)
                ex_silu(e, u)
                if ahead:
                    ex_hi(u + 2, turn * (UNROLL // WSLOTS) + ((u + 2) // WSLOTS + 1))
                if not first:
                    ex_y(e - 1, u - 1, free)

            for e in range(UNROLL):
                step(e, e, 0, first=e == 0, free=e >= 3)
            with act.Fori(1, E // UNROLL - 1) as i:
                for u in range(UNROLL):
                    step(i * UNROLL + u, u, i)
            for e in range(E - UNROLL, E):
                step(e, e % UNROLL, E // UNROLL - 1, last=e == E - 1, ahead=e + 2 < E)
            ex_y(E - 1, E - 1)

            act.wait_ge(y_added, 16 * E)
            most_r = act.value_load(most[0:1, 0:1], min_val=0, max_val=TOK)
            with act.If(most_r > P):
                for tile in range(1, NT):
                    with act.Fori(0, E) as e:
                        n = e + E * tile
                        ex_hi(0, e + E * (tile - 1) + (E // WSLOTS + 1))
                        ex_xt_evac(n, 0)
                        ex_silu(n, 0)
                        act.wait_ge(ex_dn, n + 1)
                        act.activation(ysb[:, 0, 0:512], bank[3][:, :], ACT.Copy).then_inc(y_by_act, 1)
            layer_norm_rows(1, fin_act)

        @block.vector
        def _(v):
            k = [0]

            def then(ins):
                k[0] += 1
                ins.then_inc(dve, 1)
                v.wait_ge(dve, k[0])

            v.wait_ge(bcol_pe, 1)
            v.tensor_copy(bcol[:], bank[7][:, 0:NB + KVH]).then_inc(bcol_dve, 1)
            for t, (a, w) in enumerate(TILES):
                for h in range(2):
                    v.wait_ge(xt_act, 2 * t + h + 1)
                    v.tensor_tensor(xT_lo[:, 4 * h:4 * h + 4, a:a + w],
                                    bank[2 * (t % 2) + h][:, 0:4 * w].rearrange("p (c n) -> p c n", c=4),
                                    xT[:, 4 * h:4 * h + 4, a:a + w].bitcast(F32), ALU.subtract).then_inc(xt_dve, 1)

            def split_lo(n):
                v.wait_ge(hi_act, split_no[n] + 1)
                w_ = blocks[n][1][-1][0] + blocks[n][1][-1][3]
                v.tensor_tensor(w_lo[n % RAW][:, :, 0:w_], raw[n % RAW][:, :, 0:w_], hi_of(n)[:, :, 0:w_].bitcast(F32),
                                ALU.subtract).then_inc(lo_dve, 1)

            for i in range(split_no[tms[0][0]] + 2):
                split_lo(split[i])
            v.wait_ge(consts_landed, N_CDMA * 16)
            for g, (n, width, c, t) in enumerate(tms):
                w = TILES[t][1]
                v.wait_ge(tm_done, g + 1)
                dst = v_sb[0:w, t, :] if c == 0 else vs_sb[0:w, t, c - P:c - P + width]
                v.tensor_tensor(dst, bank[4 + g % 2][0:w, 0:width], tm_bias[0:w, c:c + width], ALU.add).then_inc(tm_dve, 1)
                if t == NT - 1 and split_no[n] + 2 < n_early:
                    split_lo(split[split_no[n] + 2])
            for t, (a, w) in enumerate(TILES):
                v.wait_ge(gelu_act, t + 1)
                then(v.bn_stats(stat6[0:w, 0, :], vs_sb[0:w, t, :]))
                v.bn_aggr(mv[0:w, t, :], stat6[0:w, 0, :]).then_inc(stat_dve, 1)
                v.wait_ge(stat_dve, t + 1)
            v.wait_ge(std_act, 1)
            then(v.reciprocal(rstd[:, :], std[:, :]))
            for t, (a, w) in enumerate(TILES):
                x_ = vs_sb[0:w, t, :]
                v.tensor_scalar(x_, x_, mv[0:w, t, 0:1], rstd[0:w, t:t + 1], ALU.subtract, ALU.mult).then_inc(vsn_dve, 1)
                v.wait_ge(vsn_dve, 2 * t + 1)
                v.tensor_tensor(x_, x_, sgln[0:w, 0, :], ALU.mult).then_inc(vsn_dve, 1)

            g = len(misc) - 1
            v.wait_ge(misc_done, g + 1)
            for i in range(2):
                w = TILES[PT - 1 + i][1]
                last = v.tensor_copy(kout[0:w, i, :].rearrange("p (k d) -> p k d", k=KVH),
                                     bank[6 + g % 2][0:w, :].rearrange("p (a k n) -> p a k n", a=2, k=KVH)[:, i, :, 0:HD])
            last.then_inc(misc_dve, 1)
            v.wait_ge(rel_landed, 16 * 5)
            v.wait_ge(pool_reln, NSEQ)

            def maxima(u):
                v.wait_ge(logits_done, u + 1)
                if u >= LR:
                    v.wait_ge(pt_done, u - LR + 1)
                s_, q_ = u % LR, u % 4
                if u < UP:
                    hg, lo, n = u % 4, (WIN if u < 4 else 0), 4
                    for j in range(2):
                        v.scalar_tensor_tensor(L[:, s_, j:4:2, lo:W2],
                                               bank[2 * (u % 2) + j][:, :].rearrange("p (h n) -> p h n", h=2)[:, :, lo:W2], SCALE,
                                               rel[:, 4 * hg + j:4 * hg + 4:2, lo:W2], ALU.mult, ALU.add)\
                         .then_inc(dve, 1)
                        k[0] += 1
                    v.wait_ge(dve, k[0])
                    then(v.tensor_reduce(mx[:, q_, 0:n], L[:, s_, 0:n, lo:W2], AX, ALU.max))
                    then(v.tensor_tensor(mx[:, q_, 0:n], mx[:, q_, 0:n], sink[:, 4 * hg:4 * hg + 4], ALU.max))
                    then(v.tensor_scalar(nm[:, q_, 0:n], mx[:, q_, 0:n], -1.0, None, ALU.mult))
                    v.tensor_tensor(sd[:, q_, 0:n], sink[:, 4 * hg:4 * hg + 4], nm[:, q_, 0:n], ALU.add).then_inc(mx_dve, 1)
                else:
                    b, n = (u - UP) * 2, 2
                    for par in range(2):
                        r = slice(HD * par, HD * par + HD)
                        lg = bank[2 * (u % 2) + par][r, 0:2 * (WIN + NS)].rearrange("p (q n) -> p q n", q=2)
                        v.scalar_tensor_tensor(L[r, s_, 0:2, 0:WIN], lg[:, :, 0:WIN], SCALE,
                                               rel_c[r, 0:WIN].rearrange("p (a n) -> p a n", a=1).to_broadcast([HD, 2, WIN]),
                                               ALU.mult, ALU.add).then_inc(dve, 1)
                        v.scalar_tensor_tensor(L[r, s_, 0:2, WIN:WIN + NS], lg[:, :, WIN:WIN + NS], SCALE,
                                               rel_n[r, b:b + 2, :], ALU.mult, ALU.add).then_inc(dve, 1)
                        k[0] += 2
                    v.wait_ge(dve, k[0])
                    then(v.tensor_reduce(mx[:, q_, 0:n], L[:, s_, 0:n, 0:WIN + NS], AX, ALU.max))
                    then(v.tensor_scalar(mx[:, q_, 0:n], mx[:, q_, 0:n], sink_row[:, 0:1], None, ALU.max))
                    then(v.tensor_scalar(nm[:, q_, 0:n], mx[:, q_, 0:n], -1.0, None, ALU.mult))
                    v.tensor_scalar(sd[:, q_, 0:n], nm[:, q_, 0:n], sink_row[:, 0:1], None, ALU.add).then_inc(mx_dve, 1)

            def over_sum(u):
                n = 4 if u < UP else 2
                v.wait_ge(exp_act, u + 1)
                q_ = u % 4
                then(v.tensor_tensor(den[:, q_, 0:n], den[:, q_, 0:n], es[:, q_, 0:n], ALU.add))
                v.reciprocal(rden[:, q_, 0:n], den[:, q_, 0:n]).then_inc(rden_dve, 1)

            def pt_evac(u):
                v.wait_ge(pt_done, u + 1)
                if u >= 2:
                    v.wait_ge(pv_done, u - 1)
                if u < UP:
                    h0_ = 1 if u < 4 else 0
                    v.tensor_copy(PTs[:, u % 2, 2:4, h0_:2, :],
                                  bank[5][:, :].rearrange("p (j h n) -> p j h n", j=2, h=2)[:, :, h0_:2, :]).then_inc(pt_dve, 1)
                else:
                    v.tensor_copy(PTs[0:NS, u % 2, 0:2, 1, :], bank[5][0:NS, 0:256].rearrange("p (j n) -> p j n", j=2))\
                     .then_inc(pt_dve, 1)

            for m in range(UA + 5):
                if 0 <= m - 4 < UA:
                    pt_evac(m - 4)
                if 0 <= m - 1 < UA:
                    maxima(m - 1)
                if 0 <= m - 2 < UA:
                    over_sum(m - 2)
            for t, (a, w) in enumerate(TILES):
                v.wait_ge(sg_done, t + 1)
                if t >= 2:
                    v.wait_ge(pool_gated, t - 1)
                if t < PT:
                    v.tensor_tensor(TS[:, t % 2, :, :], bank[4 + t % 2][:, :].rearrange("p (g n) -> p g n", g=G), sgb[:],
                                    ALU.add).then_inc(sg_dve, 1)
                else:
                    for g in range(G):
                        last = v.tensor_tensor(TS[:, t % 2, g, 0:w].rearrange("p (b i) -> p b i", b=NSEQ),
                                               bank[4 + t % 2][:, g * w:(g + 1) * w].rearrange("p (b i) -> p b i", b=NSEQ),
                                               sgb[:, g, 0:DS].rearrange("p (a i) -> p a i", a=1).to_broadcast([P, NSEQ, DS]),
                                               ALU.add)
                    last.then_inc(sg_dve, 1)
            v.wait_ge(x_lo_landed, 16)
            v.tensor_copy(xT_lo2[:, 4:8, :], x_lo_back[:, 4:8, :]).then_inc(x_lo_dve, 1)
            for i in range(n_early, n_early + 2):
                split_lo(split[i])
            for n in z_merge:
                _, _, kind, m = zprods[n]
                if kind in BY_ACT:
                    continue
                v.wait_ge(z_done, n + 1)
                gate, dst, name = (GA, TA, "ga") if kind == "pa" else (GB, TB, "gb")
                gn = [i for i in z_merge if zprods[i][2] == name and zprods[i][3] == m][0]
                v.wait_ge(z_act, act_no[gn])
                if m >= 2:
                    v.wait_ge(pool_merged, m - 1)
                v.tensor_tensor(dst[:, m % 2, 0:HALF], bank[n % 2][:, 0:HALF], gate[:, m % 2, 0:HALF], ALU.mult)
                v.tensor_tensor(dst[:, m % 2, HALF:TOK], bank[2 + n % 2][:, 0:HALF], gate[:, m % 2, HALF:TOK], ALU.mult)\
                 .then_inc(z_dve, 1)
                later = n_early + 2 * (m // 2 + 1) + m % 2
                if kind == "pa" and later < len(split):
                    split_lo(split[later])
            v.wait_ge(x_again, 16 * NT)

            def stats(t, first):
                w = TILES[t][1]
                for j in range(2):
                    v.bn_stats(stat6[0:w, j, :], x1[0:w, t, j * 512:(j + 1) * 512]).then_inc(dve, 1)
                    k[0] += 1
                v.wait_ge(dve, k[0])
                v.bn_aggr(mv[0:w, t, :], stat6[0:w, :, :]).then_inc(stat_dve, 1)

            def norm_terms(t, first):
                w = TILES[t][1]
                v.wait_ge(std_act, 1 + first * NT + t + 1)
                then(v.reciprocal(rstd[0:w, t:t + 1], std[0:w, t:t + 1]))
                v.scalar_tensor_tensor(nmr[0:w, t:t + 1], mv[0:w, t, 0:1], -1.0, rstd[0:w, t:t + 1], ALU.mult, ALU.mult)\
                 .then_inc(nmr_dve, 1)

            def gain(t, first, s, base):
                w = TILES[t][1]
                v.wait_ge(s, t + 1)
                v.tensor_tensor(x1[0:w, t, :], x1[0:w, t, :], ln_gb[0:w, 0, :], ALU.mult).then_inc(lng_dve, 1)

            for t, (a, w) in enumerate(TILES):
                for s in range(D // SB):
                    g = t * (D // SB) + s
                    v.wait_ge(wo_done_g, g + 1)
                    v.scalar_tensor_tensor(x1[0:w, t, s * SB:(s + 1) * SB], x1[0:w, t, s * SB:(s + 1) * SB], ALPHA,
                                           bank[4 + g % 2][0:w, 0:SB], ALU.mult, ALU.add).then_inc(wo_dve, 1)
                v.wait_ge(wo_dve, (t + 1) * (D // SB))
                stats(t, 0)
                norm_terms(t, 0)
                if t >= 1:
                    gain(t - 1, 0, xn_act, 0)
            gain(NT - 1, 0, xn_act, 0)
            for t, (a, w) in enumerate(TILES):
                v.wait_ge(x1t_done, 2 * t + 2)
                v.tensor_copy(x1T[:, 4:8, a:a + w], bank[2 * (t % 2) + 1][:, 0:4 * w].rearrange("p (c n) -> p c n", c=4))\
                 .then_inc(x1t_dve, 1)

            v.wait_ge(out_done_act, 64)
            then(v.memset(scores[NS:P, NT - 1, :], 0.0))
            v.wait_ge(score_act, NT)
            EG = [P, NT, NG, EPG]
            then(v.tensor_tensor(sel[:], scores[:], rbias[:].rearrange("p (a e) -> p a e", a=1).to_broadcast([P, NT, E]), ALU.add))
            for t in range(NT):
                for g in range(NG):
                    v.max(top[:, t, g, :], sel[:, t, g * EPG:(g + 1) * EPG]).then_inc(dve, 1)
                    k[0] += 1
            v.wait_ge(dve, k[0])
            then(v.tensor_tensor(gsc[:], top[:, :, :, 0], top[:, :, :, 1], ALU.add))
            for t in range(NT):
                mine = gsc[:, t, :].rearrange("p (g a) -> p g a", a=1).to_broadcast([P, NG, NG])
                other = gsc[:, t, :].rearrange("p (a g) -> p a g", a=1).to_broadcast([P, NG, NG])
                v.tensor_tensor(cmp_a[:, t, :, :], other, mine, ALU.is_gt).then_inc(dve, 1)
                v.tensor_tensor(cmp_b[:, t, :, :], other, mine, ALU.is_equal).then_inc(dve, 1)
                k[0] += 2
            v.wait_ge(dve, k[0])
            for t in range(NT):
                v.tensor_tensor(cmp_b[:, t, :, :], cmp_b[:, t, :, :], tie[:], ALU.mult).then_inc(dve, 1)
                k[0] += 1
            v.wait_ge(dve, k[0])
            then(v.tensor_tensor(cmp_a[:], cmp_a[:], cmp_b[:], ALU.add))
            then(v.tensor_reduce(rank[:], cmp_a[:], AX, ALU.add))
            then(v.tensor_scalar(rank[:], rank[:], float(TOPG), None, ALU.is_lt))
            then(v.tensor_scalar(pen[:], rank[:], 1.0, -NEG_INF, ALU.subtract, ALU.mult))
            bc = lambda a: a.rearrange("p t (g a) -> p t g a", a=1).to_broadcast(EG)
            v4 = lambda a: a.rearrange("p t (g e) -> p t g e", g=NG)
            then(v.tensor_tensor(v4(sel[:]), v4(sel[:]), bc(rank[:]), ALU.mult))
            then(v.tensor_tensor(v4(sel[:]), v4(sel[:]), bc(pen[:]), ALU.add))
            for t in range(NT):
                v.max(top8[:, t, :], sel[:, t, :]).then_inc(dve, 1)
                k[0] += 1
            v.wait_ge(dve, k[0])
            for t in range(NT):
                v.match_replace(selm[:, t, :], top8[:, t, :], sel[:, t, :], TAKEN).then_inc(dve, 1)
                k[0] += 1
            v.wait_ge(dve, k[0])
            then(v.tensor_tensor(smask[:], selm[:], sel[:], ALU.not_equal))
            then(v.memset(smask[NS:P, NT - 1, :], 0.0))
            v.tensor_copy(chosen[:], smask[:]).then_inc(chosen_dve, 1)
            then(v.tensor_tensor(gates[:], scores[:], smask[:], ALU.mult))
            then(v.tensor_reduce(wsum[:], gates[:], AX, ALU.add))
            then(v.memset(wsum[NS:P, NT - 1:NT], 1.0))
            then(v.reciprocal(rsum[:], wsum[:]))
            then(v.tensor_tensor(gates[:], gates[:], rsum[:].rearrange("p (t a) -> p t a", a=1).to_broadcast([P, NT, E]), ALU.mult))
            then(v.tensor_scalar(gates[:], gates[:], ROUTED, None, ALU.mult))
            then(v.tensor_copy(R[:, :, :, 3], gates[:]))
            then(v.tensor_tensor(rest[:], gates[:], R[:, :, :, 3], ALU.subtract))
            then(v.tensor_copy(R[:, :, :, 4], rest[:]))
            then(v.tensor_tensor(rest[:], rest[:], R[:, :, :, 4], ALU.subtract))
            then(v.tensor_copy(R[:, :, :, 5], rest[:]))
            then(v.tensor_copy(R[:, :, :, 0], pcol[:, 0:1].rearrange("p (a b) -> p a b", a=1).to_broadcast([P, NT, E])))
            for t in range(NT):
                then(v.memset(R[:, t, :, 1], float(t * P - TOK)))
            v.wait_ge(pos_done, 1)
            then(v.scalar_tensor_tensor(posm[:], bank[7][:, 0:NT * E].rearrange("p (t e) -> p t e", t=NT), 1.0, smask[:],
                                        ALU.add, ALU.mult))
            then(v.tensor_scalar(posm[:], posm[:], -1.0, None, ALU.add))
            then(v.tensor_scalar(R[:, :, :, 2], posm[:], -1.0, None, ALU.mult))
            then(v.tensor_reduce(mostf[:], bank[7][:, NT * E:NT * E + E], AX, ALU.max))
            v.tensor_copy(most[:], mostf[:]).then_inc(most_dve, 1)
            v.wait_ge(most_dve, 1)
            v.memset(mostf[:], 0.0).then_inc(route_dve, 1)

            def hot(e, u, base=iota_row, wait=True):
                if wait:
                    v.wait_ge(ex_list, e - 3)
                pos = posm[:, :, bass.ds(e, 1)].to_broadcast([P, NT, P])
                v.tensor_tensor(onehot[:, u % 4, :, :], base[:].rearrange("p (a n) -> p a n", a=1).to_broadcast([P, NT, P]),
                                pos, ALU.is_equal).then_inc(hot_by_dve, 1)

            def idx(e, u, wait=True):
                v.wait_ge(ex_list, e + 1)
                if wait:
                    v.wait_ge(y_added, 16 * (e - UNROLL + 1))
                v.tensor_reduce(gate_idx[:, u, :], bank[6][:, 0:6].rearrange("p (a n) -> p a n", a=2), AX, ALU.add)\
                 .then_inc(sum_by_dve, 1)
                v.wait_ge(sum_by_dve, e + 1)
                v.tensor_scalar(idx_u[:, u:u + 1], gate_idx[:, u, 0:1], trash[:, 0:1], None, ALU.add).then_inc(idx_by_dve, 1)

            def xt_evac(e, u):
                for h in range(2):
                    v.wait_ge(xt_by_act, 2 * e + (h + 1))
                    v.tensor_tensor(xgT_lo[:, u % 2, 4 * h:4 * h + 4, :], bank[h][:, :].rearrange("p (c n) -> p c n", c=4),
                                    xgT[:, u % 2, 4 * h:4 * h + 4, :].bitcast(F32), ALU.subtract).then_inc(xt_by_dve, 1)

            def w_lo_part(e, u):
                v.wait_ge(hi_by_act, e + 1)
                w_ = wgu[u % WSLOTS]
                v.tensor_tensor(wgu_lo[u % WSLOTS][:], w_[:], wgu_hi[u % 2][:].bitcast(F32), ALU.subtract).then_inc(lo_by_dve, 1)

            def hidden(e, u):
                v.wait_ge(silu_by_act, e + 1)
                v.scalar_tensor_tensor(hh[:, u % 2, :], bank[2][:, FE:2 * FE], gate_idx[:, u % UNROLL, 1:2], silu[:],
                                       ALU.mult, ALU.mult).then_inc(h_by_dve, 1)

            def ht_evac(e, u):
                v.wait_ge(ex_ht, e + 1)
                v.tensor_copy(hT[:, u % 2, :, :], bank[5][:, 0:FE].rearrange("p (j n) -> p j n", j=2)).then_inc(ht_by_dve, 1)

            def y_evac(e, u, free=True):
                v.wait_ge(ex_dn, e + 1)
                if free:
                    v.wait_ge(y_added, (e - 1) * 16)
                v.tensor_copy(ysb[:, u % 2, 512:1024], bank[4][:, :]).then_inc(y_by_dve, 1)

            v.wait_ge(sdn_done, NT)
            v.wait_ge(sy_act, 2 * NT)
            for e in range(IDX_AHEAD):
                hot(e, e, wait=False)
                idx(e, e, wait=False)
            v.wait_ge(pool_sy, NT)
            w_lo_part(0, 0)
            xt_evac(0, 0)

            def step(e, u, first=False, ahead=True, wait=True, last=False, free=True):
                if ahead:
                    hot(e + IDX_AHEAD, u + IDX_AHEAD)
                if not first:
                    ht_evac(e - 1, u - 1)
                if not last:
                    w_lo_part(e + 1, u + 1)
                    xt_evac(e + 1, u + 1)
                if ahead:
                    idx(e + IDX_AHEAD, (u + IDX_AHEAD) % UNROLL, wait)
                hidden(e, u)
                if not first:
                    y_evac(e - 1, u - 1, free)

            for e in range(UNROLL):
                step(e, e, first=e == 0, wait=e + IDX_AHEAD >= UNROLL, free=e >= 3)
            with v.Fori(1, E // UNROLL - 1) as i:
                for u in range(UNROLL):
                    step(i * UNROLL + u, u)
            for e in range(E - UNROLL, E):
                step(e, e % UNROLL, ahead=e + IDX_AHEAD < E, last=e == E - 1)
            ht_evac(E - 1, E - 1)
            y_evac(E - 1, E - 1)

            v.wait_ge(y_added, 16 * E)
            most_r = v.value_load(most[0:1, 0:1], min_val=0, max_val=TOK)
            with v.If(most_r > P):
                for tile in range(1, NT):
                    v.tensor_scalar(R[:, :, :, 2], posm[:], -1.0, float(tile * P), ALU.mult, ALU.add).then_inc(over_dve, 1)
                    v.tensor_scalar(iota_row[:], iota_row[:], float(P), None, ALU.add).then_inc(over_dve, 1)
                    v.wait_ge(over_dve, 2 * tile)
                    with v.Fori(0, E) as e:
                        n = e + E * tile
                        pos = posm[:, :, bass.ds(e, 1)].to_broadcast([P, NT, P])
                        v.wait_ge(y_added, 16 * n)
                        v.tensor_tensor(onehot[:, 0, :, :], iota_row[:].rearrange("p (a n) -> p a n", a=1).to_broadcast([P, NT, P]),
                                        pos, ALU.is_equal).then_inc(hot_by_dve, 1)
                        v.wait_ge(ex_list, n + 1)
                        v.tensor_reduce(gate_idx[:, 0, :], bank[6][:, 0:6].rearrange("p (a n) -> p a n", a=2), AX, ALU.add)\
                         .then_inc(sum_by_dve, 1)
                        v.wait_ge(sum_by_dve, n + 1)
                        v.tensor_scalar(idx_u[:, 0:1], gate_idx[:, 0, 0:1], trash[:, 0:1], None, ALU.add).then_inc(idx_by_dve, 1)
                        w_lo_part(n, 0)
                        xt_evac(n, 0)
                        hidden(n, 0)
                        ht_evac(n, 0)
                        v.wait_ge(ex_dn, n + 1)
                        v.tensor_copy(ysb[:, 0, 512:1024], bank[4][:, :]).then_inc(y_by_dve, 1)
            v.wait_ge(ln_swap, 32)
            for t in range(NT):
                v.wait_ge(y_back[t], 16)
                stats(t, 1)
                norm_terms(t, 1)
                if t >= 1:
                    gain(t - 1, 1, fin_act, 1)
            gain(NT - 1, 1, fin_act, 1)

        @block.tensor
        def _(pe):
            mm = pe.matmul
            pe.wait_ge(pool_consts, N_CONST)
            pe.wait_ge(brow_landed, 32)
            pe.transpose(bank[7][:, 0:NB + KVH], brow[:], ident[0:NB + KVH, 0:NB + KVH]).then_inc(bcol_pe, 1)
            for t, (a, w) in enumerate(TILES):
                pe.wait_ge(x_landed[t], 16)
                if t >= 2:
                    pe.wait_ge(xt_dve, 2 * (t - 1))
                for h in range(2):
                    for c in range(4):
                        last = pe.transpose(bank[2 * (t % 2) + h][:, c * w:(c + 1) * w], x_in[0:w, t, (4 * h + c) * P:(4 * h + c + 1) * P],
                                            ident[0:w, 0:w])
                    last.then_inc(xt_done, 1)
            pe.wait_ge(xt_dve, 2 * NT)

            def zprod(n):
                nb, j, kind, _ = zprods[n]
                src, kc_ = (AT, DC) if kind == "pa" else (uT, G) if kind == "pb" else (xT, DC)
                if j == 0 and nb in split_no:
                    pe.wait_ge(lo_dve, split_no[nb] + 1)
                elif j == 0:
                    pe.wait_ge(block_in[nb % RAW], block_landed(nb))
                if n >= 2:
                    if n - 2 in act_no:
                        pe.wait_ge(z_act, act_no[n - 2])
                    else:
                        pe.wait_ge(z_dve, dve_no[n - 2])
                if nb in split_no:
                    lo_ = xT_lo if split_no[nb] < n_early else xT_lo2
                    for c in range(kc_):
                        parts = [(f[:, c, j * P:(j + 1) * P], x_) for f, x_ in
                                 ((hi_of(nb), xT), (hi_of(nb), lo_), (w_lo[nb % RAW], xT))]
                        for i, (w_, x_) in enumerate(parts):
                            first, final = c == 0 and i == 0, c == kc_ - 1 and i == 2
                            mm(bank[n % 2][:, 0:HALF], w_, x_[:, c, 0:HALF], start=first, stop=final)
                            last = mm(bank[2 + n % 2][:, 0:HALF], w_, x_[:, c, HALF:TOK], start=first, stop=final)
                    last.then_inc(z_done, 1)
                    return
                for c in range(kc_):
                    w_ = raw[nb % RAW][:, c, j * P:(j + 1) * P]
                    mm(bank[n % 2][:, 0:HALF], w_, src[:, c, 0:HALF], start=c == 0, stop=c == kc_ - 1)
                    last = mm(bank[2 + n % 2][:, 0:HALF], w_, src[:, c, HALF:TOK], start=c == 0, stop=c == kc_ - 1)
                last.then_inc(z_done, 1)

            for n in z_kq:
                zprod(n)
            for g, (nb, width, c0_, t) in enumerate(tms):
                a, w = TILES[t]
                if t == 0:
                    pe.wait_ge(lo_dve, split_no[nb] + 1)
                if g >= 2:
                    pe.wait_ge(tm_dve, g - 1)
                for c in range(DC):
                    for i, (x_, w_) in enumerate(((xT, hi_of(nb)), (xT, w_lo[nb % RAW]), (xT_lo, hi_of(nb)))):
                        last = mm(bank[4 + g % 2][0:w, 0:width], x_[:, c, a:a + w], w_[:, c, 0:width],
                                  start=c == 0 and i == 0, stop=c == DC - 1 and i == 2)
                last.then_inc(tm_done, 1)
            for n in z_u:
                zprod(n)
            pe.wait_ge(pool_sg, 2)
            pe.wait_ge(kc_landed, 16 * NSEQ)
            pe.wait_ge(z_act, act_no[z_kq[-1]])
            for g, items in enumerate(misc):
                if g >= 2:
                    pe.wait_ge(misc_act, g - 1)
                bk = bank[6 + g % 2]
                kind = items[0][0]
                for i, (_, x) in enumerate(items):
                    if kind == "sg":
                        last = pe.transpose(bk[:, i * P:(i + 1) * P], sgw[:, x, :], ident[:])
                    elif kind == "sgs":
                        last = pe.transpose(bk[0:NS, i * NS:(i + 1) * NS], sgs[:, x, :], ident[0:NS, 0:NS])
                    elif kind == "kc":
                        for kv in range(KVH):
                            last = pe.transpose(bk[:, (2 * i + kv) * P:(2 * i + kv + 1) * P], kc[:, x, kv, :], ident[:])
                    else:
                        a, w = TILES[PT - 1 + x]
                        for kv in range(KVH):
                            last = pe.transpose(bk[0:w, (2 * i + kv) * P:(2 * i + kv + 1) * P], kT[:, kv, a:a + w], ident[:])
                last.then_inc(misc_done, 1)

            pe.wait_ge(misc_act, len(misc) - 1)
            pe.wait_ge(misc_dve, 1)
            pe.wait_ge(tm_dve, len(tms))
            pe.wait_ge(z_act, act_no[z_u[-1]])

            def logits(u):
                if u >= 2:
                    pe.wait_ge(mx_dve, u - 1)
                if u < UP:
                    b, hg = u // 4, u % 4
                    kv = hg // (H // 4 // KVH)
                    k_lo = b * P if b == 0 else (b - 1) * P
                    lo = WIN if b == 0 else 0
                    for j in range(4):
                        r = slice(HD * (j % 2), HD * (j % 2) + HD)
                        last = mm(bank[2 * (u % 2) + j % 2][:, (j // 2) * W2 + lo:(j // 2 + 1) * W2],
                                  qT[r, 2 * hg + j // 2, b * P:(b + 1) * P], kT[r, kv, k_lo:(b + 1) * P], start=True, stop=True)
                else:
                    for q in range(2):
                        b = (u - UP) * 2 + q
                        for kv, par in rel_pair:
                            r0 = 32 * (2 * par + kv)
                            r = slice(HD * par, HD * par + HD)
                            q4 = qs[r, b, 4 * kv:4 * kv + 4, :]
                            o = bank[2 * (u % 2) + par][r0:r0 + 32, q * (WIN + NS):(q + 1) * (WIN + NS)]
                            mm(o[:, 0:WIN], q4, kcT[r, b, kv, :], start=True, stop=True)
                            last = mm(o[:, WIN:WIN + NS], q4, kT[r, kv, SEQ:TOK], start=True, stop=True)
                last.then_inc(logits_done, 1)

            def probs_t(u):
                pe.wait_ge(pool_norm, u + 1)
                if u >= 1:
                    pe.wait_ge(pt_act, u)
                    pe.wait_ge(pt_dve, u)
                if u < UP:
                    h0_ = 1 if u < 4 else 0
                    for j in range(4):
                        for h in range(h0_, 2):
                            c = (j % 2 * 2 + h) * P
                            last = pe.transpose(bank[4 + j // 2][:, c:c + P], L[:, u % LR, j, h * P:(h + 1) * P], ident[:])
                else:
                    for q in range(2):
                        pe.transpose(bank[4][:, q * P:(q + 1) * P], L[:, u % LR, q, 0:WIN], ident[:])
                        last = pe.transpose(bank[5][0:NS, q * P:(q + 1) * P], L[:, u % LR, q, WIN:WIN + NS], ident[:])
                last.then_inc(pt_done, 1)

            def values(u):
                pe.wait_ge(pt_act, u + 1)
                pe.wait_ge(pt_dve, u + 1)
                if u >= 2:
                    pe.wait_ge(pv_act, u - 1)
                if u < UP:
                    b, hg = u // 4, u % 4
                    kv = hg // (H // 4 // KVH)
                    for j in range(4):
                        o = bank[6 + u % 2][HD * (j % 2):HD * (j % 2) + HD, (j // 2) * P:(j // 2 + 1) * P]
                        halves = [1] if b == 0 else [0, 1]
                        for h in halves:
                            last = mm(o, v_sb[:, b - 1 + h, kv * HD:(kv + 1) * HD], PTs[:, u % 2, j, h, :],
                                      start=h == halves[0], stop=h == 1)
                else:
                    for q in range(2):
                        b = (u - UP) * 2 + q
                        for kv, par in rel_pair:
                            rows = slice(32 * (2 * par + kv), 32 * (2 * par + kv) + 32)
                            o = bank[6 + u % 2][HD * par:HD * par + HD, (2 * q + kv) * 32:(2 * q + kv + 1) * 32]
                            mm(o, vc[:, b, kv * HD:(kv + 1) * HD], PTs[:, u % 2, q, 0, rows], start=True, stop=False)
                            last = mm(o, v_sb[0:NS, PT, kv * HD:(kv + 1) * HD], PTs[0:NS, u % 2, q, 1, rows],
                                      start=False, stop=True)
                last.then_inc(pv_done, 1)

            pe.wait_ge(vc_landed, 16)
            for m in range(UA + 4):
                if m < UA:
                    logits(m)
                if 0 <= m - 4 < UA:
                    values(m - 4)
                if 0 <= m - 3 < UA:
                    probs_t(m - 3)
            pe.wait_ge(pool_vs, NT)
            pe.wait_ge(pt_act, UA)
            pe.wait_ge(pt_dve, UA)
            for t, (a, w) in enumerate(TILES):
                if t >= 2:
                    pe.wait_ge(sg_dve, t - 1)
                for g in range(G):
                    wt = sgwT[:, g, :] if t < PT else sgsT[:, g, :]
                    last = mm(bank[4 + t % 2][:, g * w:(g + 1) * w], vs_sb[0:w, t, g * P:(g + 1) * P], wt, start=True, stop=True)
                last.then_inc(sg_done, 1)
            pe.wait_ge(mx_dve, UA)
            pe.wait_ge(pv_act, UA)
            pe.wait_ge(pool_gated, NT)
            pe.wait_ge(x_lo_act, 1)
            pe.wait_ge(x_lo_dve, 1)
            for n in z_merge:
                zprod(n)
            pe.wait_ge(pool_merged, D // P)
            pe.wait_ge(sg_dve, NT)
            for t, (a, w) in enumerate(TILES):
                for s in range(NSB):
                    g = t * NSB + s
                    nb = first_wo + s
                    if t == 0:
                        pe.wait_ge(block_in[nb % RAW], block_landed(nb))
                    if g >= 2:
                        pe.wait_ge(wo_dve, g - 1)
                    for c in range(DC):
                        last = mm(bank[4 + g % 2][0:w, 0:SB], mT[:, c, a:a + w], raw[nb % RAW][:, c, :],
                                  start=c == 0, stop=c == DC - 1)
                    last.then_inc(wo_done_g, 1)
            for t, (a, w) in enumerate(TILES):
                pe.wait_ge(pool_x1, t + 1)
                if t >= 2:
                    pe.wait_ge(x1t_act, t - 1)
                    pe.wait_ge(x1t_dve, t - 1)
                for h in range(2):
                    for c in range(4):
                        cc = 4 * h + c
                        last = pe.transpose(bank[2 * (t % 2) + h][:, c * w:(c + 1) * w],
                                            x1[0:w, t, :].rearrange("p (d c) -> p c d", c=DC)[:, cc, :], ident[0:w, 0:w])
                    last.then_inc(x1t_done, 1)
            pe.wait_ge(x1t_act, NT)
            pe.wait_ge(x1t_dve, NT)
            pe.wait_ge(wo_dve, NT * NSB)
            pe.wait_ge(wr_landed, 16)
            for t, (a, w) in enumerate(TILES):
                for c in range(DC):
                    last = mm(bank[4][0:w, t * E:(t + 1) * E], x1T[:, c, a:a + w], wr[:, c, :], start=c == 0, stop=c == DC - 1)
                last.then_inc(route_done, 1)

            def shared_gu(t):
                a, w = TILES[t]
                if t >= 1:
                    pe.wait_ge(ssilu_act, 2 * t)
                for c in range(DC):
                    last = mm(bank[5][0:w, :], x1T[:, c, a:a + w], swgu[:, :, c, :], start=c == 0, stop=c == DC - 1)
                last.then_inc(sgu_done, 1)

            def shared_down(t):
                a, w = TILES[t]
                pe.wait_ge(pool_sh, t + 1)
                if t >= 1:
                    pe.wait_ge(sht_act, t)
                for j in range(FE // P):
                    last = pe.transpose(bank[6][:, j * w:(j + 1) * w],
                                        ssilu[0:w, t % 2, :].rearrange("p (f j) -> p j f", j=2)[:, j, :], ident[0:w, 0:w])
                last.then_inc(sht_done, 1)
                pe.wait_ge(sht_act, t + 1)
                if t >= 1:
                    pe.wait_ge(sy_act, 2 * t)
                for h in range(2):
                    for j in range(FE // P):
                        last = mm(bank[h][0:w, :], shT[:, t % 2, j, 0:w], swd[:, j, h * 512:(h + 1) * 512],
                                  start=j == 0, stop=j == FE // P - 1)
                last.then_inc(sdn_done, 1)

            pe.wait_ge(shared_landed, 48)
            for t in range(NT + 1):
                if t < NT:
                    shared_gu(t)
                if t >= 1:
                    shared_down(t - 1)
            pe.wait_ge(chosen_dve, 1)
            pe.wait_ge(sy_act, 2 * NT)
            for t in range(NT):
                mm(bank[7][:, t * E:(t + 1) * E], before[:], chosen[:, t, :], start=True, stop=t == 0)
                for s in range(t):
                    mm(bank[7][:, t * E:(t + 1) * E], ones_b[:], chosen[:, s, :], start=False, stop=s == t - 1)
            for t in range(NT):
                last = mm(bank[7][:, NT * E:NT * E + E], ones_b[:], chosen[:, t, :], start=t == 0, stop=t == NT - 1)
            last.then_inc(pos_done, 1)

            def token_list(e, u, wait=True):
                pe.wait_ge(hot_by_dve, e + 1)
                if wait:
                    pe.wait_ge(sum_by_dve, e)
                for t in range(NT):
                    last = mm(bank[6][:, 0:6], onehot[:, u % 4, t, :], R[:, t, bass.ds(e, 1), :],
                              start=t == 0, stop=t == NT - 1)
                last.then_inc(ex_list, 1)

            def rows_t(e, u, n, wait=True):
                pe.wait_ge(xg_in[u % 2], n)
                if wait:
                    pe.wait_ge(xt_by_dve, 2 * e)
                for c in range(DC):
                    last = pe.transpose(bank[c // 4][:, c % 4 * P:(c % 4 + 1) * P],
                                        xg[:, u % 2, :].rearrange("p (d c) -> p c d", c=DC)[:, c, :], ident[:])
                last.then_inc(ex_xt, 1)

            def gate_up(e, u, wait=True):
                slot = u % WSLOTS
                pe.wait_ge(xt_by_dve, 2 * e + 2)
                pe.wait_ge(lo_by_dve, e + 1)
                if wait:
                    pe.wait_ge(h_by_dve, e)
                for c in range(DC):
                    for i, (x_, w_) in enumerate(((xgT, wgu_hi[u % 2]), (xgT, wgu_lo[slot]), (xgT_lo, wgu_hi[u % 2]))):
                        last = mm(bank[2][:, :], x_[:, u % 2, c, :], w_[:, :, c, :],
                                  start=c == 0 and i == 0, stop=c == DC - 1 and i == 2)
                last.then_inc(ex_gu, 1)

            def hidden_t(e, u):
                pe.wait_ge(h_by_dve, e + 1)
                for j in range(FE // P):
                    last = pe.transpose(bank[5][:, j * P:(j + 1) * P],
                                        hh[:, u % 2, :].rearrange("p (f j) -> p j f", j=2)[:, j, :], ident[:])
                last.then_inc(ex_ht, 1)

            def down(e, u, landed, wait=True):
                slot = u % WSLOTS
                pe.wait_ge(ht_by_dve, e + 1)
                pe.wait_ge(wd_in[slot], landed * 16)
                if wait:
                    pe.wait_ge(y_by_act, e)
                    pe.wait_ge(y_by_dve, e)
                for h in range(2):
                    for j in range(FE // P):
                        last = mm(bank[3 + h][:, :], hT[:, u % 2, j, :], wd[slot][:, j, h * 512:(h + 1) * 512],
                                  start=j == 0, stop=j == FE // P - 1)
                last.then_inc(ex_dn, 1)

            pe.wait_ge(route_dve, 1)
            for e in range(IDX_AHEAD):
                token_list(e, e, wait=e > 0)
            rows_t(0, 0, 16, wait=False)

            def step(e, u, turn, first=False, ahead=True, last=False):
                if not last:
                    rows_t(e + 1, u + 1, (turn * (UNROLL // 2) + ((u + 1) // 2 + 1)) * 16)
                if ahead:
                    token_list(e + IDX_AHEAD, u + IDX_AHEAD)
                gate_up(e, u, wait=not first)
                if not first:
                    up = u - 1
                    down(e - 1, up, turn * (UNROLL // WSLOTS) + (up // WSLOTS + 1), wait=first is not None)
                hidden_t(e, u)

            for e in range(UNROLL):
                step(e, e, 0, first=True if e == 0 else None if e == 1 else False)
            with pe.Fori(1, E // UNROLL - 1) as i:
                for u in range(UNROLL):
                    step(i * UNROLL + u, u, i)
            for e in range(E - UNROLL, E):
                step(e, e % UNROLL, E // UNROLL - 1, ahead=e + IDX_AHEAD < E, last=e == E - 1)
            down(E - 1, E - 1, E // WSLOTS)

            pe.wait_ge(y_added, 16 * E)
            most_r = pe.value_load(most[0:1, 0:1], min_val=0, max_val=TOK)
            with pe.If(most_r > P):
                for tile in range(1, NT):
                    pe.wait_ge(over_dve, 2 * tile)
                    with pe.Fori(0, E) as e:
                        n = e + E * tile
                        pe.wait_ge(hot_by_dve, n + 1)
                        pe.wait_ge(sum_by_dve, n)
                        for t in range(NT):
                            last = mm(bank[6][:, 0:6], onehot[:, 0, t, :], R[:, t, bass.ds(e, 1), :], start=t == 0, stop=t == NT - 1)
                        last.then_inc(ex_list, 1)
                        m_ = e + E * (tile - 1)
                        rows_t(n, 0, (m_ + (E // 2 + 1)) * 16)
                        gate_up(n, 0)
                        hidden_t(n, 0)
                        down(n, 0, m_ + (E // WSLOTS + 1))


def build(nc, A, O):
    hybrid_layer(nc, A, O)


_OUTS = [("y_prompt", (1, 512, 1024)), ("y_sample", (8, 8, 1024)), ("win_k_prompt", (1, 1, 128, 2, 64)),
         ("win_v_prompt", (1, 1, 128, 2, 64)), ("win_k_sample", (1, 8, 128, 2, 64)),
         ("win_v_sample", (1, 8, 128, 2, 64)), ("chunk_v_sample", (1, 8, 8, 4, 128))]


def kernel(**inputs):
    import numpy as _np
    import concourse.bacc as _bacc
    from concourse import mybir as _mybir
    from concourse.bass_utils import run_bass_kernel_spmd as _run

    nc = _bacc.Bacc("TRN2", target_bir_lowering=False, num_devices=1)
    arrays, A, O = {}, {}, {}
    for name in inputs:
        a = _np.ascontiguousarray(inputs[name])
        arrays[f"in_{name}_dram"] = a
        A[name] = nc.dram_tensor(f"in_{name}_dram", a.shape, _mybir.dt.from_np(a.dtype), kind="ExternalInput").ap()
    for name, shape in _OUTS:
        O[name] = nc.dram_tensor(f"out_{name}_dram", shape, _mybir.dt.float32, kind="ExternalOutput").ap()
    build(nc, A, O)
    r = _run(nc, [arrays], core_ids=[0])
    return tuple(r.results[0][f"out_{name}_dram"] for name, _ in _OUTS)
```

```python
from contextlib import ExitStack

import numpy as np

import concourse.bass as bass
from concourse import mybir

F32 = mybir.dt.float32
BF16 = mybir.dt.bfloat16
F32R = mybir.dt.float32r
I32 = mybir.dt.int32
U32 = mybir.dt.uint32
ALU = mybir.AluOpType
ACT = mybir.ActivationFunctionType
AX = mybir.AxisListType.X

P = 128
NEG_INF = -1e30
TAKEN = -3e38
LN_EPS = 1e-5
BUCKET_EXACT = 16
BUCKET_FAR = 128
UNROLL = 8
WSLOTS = 4
RAW = 4
SB = 256
XGSLOTS = 4
IDX_AHEAD = 4


def bucket_ranges(n_buckets, window):
    def bucket(d):
        if d < BUCKET_EXACT:
            return d
        ratio = np.float32(d) / np.float32(BUCKET_EXACT)
        far = np.log(ratio) / np.float32(np.log(BUCKET_FAR / BUCKET_EXACT)) * np.float32(n_buckets - BUCKET_EXACT)
        return min(BUCKET_EXACT + int(far), n_buckets - 1)
    out = []
    for d in range(window + 1):
        b = bucket(d)
        if out and out[-1][0] == b:
            out[-1][2] = d
        else:
            out.append([b, d, d])
    return out


def hybrid_layer(nc, A, O):
    SEQ, D = A["x_prompt"].shape[1:]
    NSEQ, DS = A["x_sample"].shape[:2]
    WIN, KVH, HD = A["cache_win_k"].shape[2:]
    NBK, H = A["rel_bias_table"].shape
    G, CH = A["sg_w"].shape[1:3]
    E, _, FE = A["w_gate_e"].shape[1:]
    SGW = G * P
    QPK = H // KVH
    NG = 8
    EPG = E // NG
    TOPG = 4
    SCALE = HD ** -0.5
    ROUTED = 2.5
    ALPHA = 2.0 ** 0.25
    DC = D // P
    TOK = SEQ + NSEQ * DS
    PT = SEQ // P
    TILES = [(t * P, P) for t in range(PT)] + [(SEQ, NSEQ * DS)]
    NT = len(TILES)
    NS = NSEQ * DS
    QE = H * HD
    KE = QE + KVH * HD
    VE = KE + KVH * HD
    UE = VE + SGW
    VSE = UE + SGW
    GAE = VSE + D
    W2 = 2 * WIN
    assert WIN == P and CH == P and HD == 64 and KVH == 2 and DS == 8 and NS == 64 and DC == 8

    PITCH = 3 * WIN
    bias_rows = nc.dram_tensor("bias_rows", (H, P, PITCH), F32, kind="Internal").ap()
    x_lo_kept = nc.dram_tensor("x_lo_kept", (P, DC, TOK), F32, kind="Internal").ap()
    x1_rows = nc.dram_tensor("x1_rows", (TOK, D), F32, kind="Internal").ap()
    y_rows = nc.dram_tensor("y_rows", (TOK + P, D), F32, kind="Internal").ap()

    at = [(nc.sbuf_base + 31) // 32 * 32]
    names = [0]

    def place(name, shape, dt, offset):
        names[0] += 1
        return nc.alloc_sbuf_tensor_at(f"{name}_{names[0]}", shape, dt, offset=offset)

    def nbytes(shape, dt):
        n = 1
        for s in shape[1:]:
            n *= s
        return (n * (2 if dt == BF16 else 4) + 31) // 32 * 32

    def keep(name, shape, dt=F32):
        off = at[0]
        at[0] += nbytes(shape, dt)
        return place(name, shape, dt, off)

    def region(size):
        off = at[0]
        at[0] += size
        return off

    ident = keep("ident", [P, P])
    iota_row = keep("iota_row", [P, P])
    pcol = keep("pcol", [P, 1])
    trash = keep("trash", [P, 1])
    spare = keep("spare", [P, 3])
    eps = keep("eps", [P, 1])
    before = keep("before", [P, P], BF16)
    ones_b = keep("ones_b", [P, P], BF16)
    tie = keep("tie", [P, NG, NG])
    NB = (GAE + D) // P
    HALF = TOK // 2
    brow = keep("brow", [NB, P])
    bcol = keep("bcol", [P, NB])
    once = at[0]
    tm_bias = keep("tm_bias", [P, P + SGW])
    sgln = keep("sgln", [P, 2, SGW])
    sgb = keep("sgb", [P, G, P])
    once_bytes = at[0] - once
    ln_gb = keep("ln_gb", [P, 2, D])
    sink = keep("sink", [P, H])
    sink_row = keep("sink_row", [P, 1])
    table_t = keep("table_t", [H, NBK])
    e_row = keep("e_row", [H, PITCH])
    rbias = keep("rbias", [P, E])
    stat6 = keep("stat6", [P, 2, 6])
    mv = keep("mv", [P, NT, 2])
    std = keep("std", [P, NT])
    rstd = keep("rstd", [P, NT])
    nmr = keep("nmr", [P, NT])
    mx = keep("mx", [P, 4, 4])
    nm = keep("nm", [P, 4, 4])
    sd = keep("sd", [P, 4, 4])
    den = keep("den", [P, 4, 4])
    es = keep("es", [P, 4, 4])
    rden = keep("rden", [P, 4, 4])
    gate_idx = keep("gate_idx", [P, UNROLL, 2])
    idx_u = keep("idx_u", [P, UNROLL], U32)
    most = keep("most", [P, 1], I32)

    wslot_bytes = 3 * DC * FE * 4
    g0 = region(wslot_bytes)
    g_at = [g0]

    def in_g(name, shape, dt=F32):
        off = g_at[0]
        g_at[0] += nbytes(shape, dt)
        return place(name, shape, dt, off)

    vs_sb = in_g("vs", [P, NT, SGW])
    v_sb = in_g("v", [P, NT, KVH * HD])
    kcT = in_g("kcT", [P, NSEQ, KVH, WIN])
    qs = in_g("qs", [P, NSEQ, DC, DS])
    assert g_at[0] - g0 <= wslot_bytes
    c0 = region(max(wslot_bytes, (DC + G) * TOK * 4))
    AT = place("AT", [P, DC, TOK], F32, c0)
    uT = place("uT", [P, G, TOK], F32, c0 + DC * TOK * 4)
    b0 = region(wslot_bytes)
    qT = place("qT", [P, DC, TOK], F32, b0)
    mT = place("mT", [P, DC, TOK], F32, b0)
    i0 = b0 + DC * TOK * 4
    sgw = place("sgw", [P, G, P], F32, i0)
    sgwT = place("sgwT", [P, G, P], F32, i0 + G * P * 4)
    sgs = place("sgs", [NS, G, NS], F32, i0 + 2 * G * P * 4)
    sgsT = place("sgsT", [NS, G, NS], F32, i0 + 2 * G * P * 4 + G * NS * 4)
    assert i0 + 2 * G * P * 4 + 2 * G * NS * 4 <= b0 + wslot_bytes
    h0 = region(RAW * DC * SB * 4)
    raw = [place(f"raw{i}", [P, DC, SB], F32, h0 + i * DC * SB * 4) for i in range(RAW)]
    a0 = region(DC * TOK * 4)
    xT = place("xT", [P, DC, TOK], F32R, a0)
    xT_lo = place("xT_lo", [P, DC, TOK], F32R, c0)
    x1T = place("x1T", [P, DC, TOK], F32, a0)
    JBYTES = 20480
    e0 = region(H * W2 * 4 + KVH * TOK * 4)
    rel = place("rel", [P, H, W2], F32, e0)
    kT = place("kT", [P, KVH, TOK], F32, e0 + H * W2 * 4)
    x_lo_back = place("x_lo_back", [P, DC, TOK], F32, e0)
    xT_lo2 = place("xT_lo2", [P, DC, TOK], F32R, e0)
    g_hi_at = [g0 + wslot_bytes - DC * SB * 4, g0]
    g_hi = [place(f"g_hi{i}", [P, DC, SB], F32R, g_hi_at[i]) for i in range(2)]
    w_lo = [place(f"w_lo{i}", [P, DC, SB], F32R, h0 + i * DC * SB * 4) for i in range(RAW)]
    assert 3 * DC * SB * 4 <= wslot_bytes and D // SB == RAW
    x1 = place("x1", [P, NT, D], F32, e0)
    assert NT * D * 4 <= H * W2 * 4 + KVH * TOK * 4
    f0 = region(NT * D * 4)
    x_in = place("x_in", [P, NT, D], F32, f0)
    w_hi = [place(f"w_hi{i}", [P, DC, SB], F32R, f0 + i * DC * SB * 4) for i in range(2)]
    LR = 3
    L = place("L", [P, LR, 4, W2], F32, f0)
    PTs = place("PTs", [P, 2, 4, 2, P], F32, f0 + LR * 4 * W2 * 4)
    assert LR * 4 * W2 * 4 + 2 * 8 * P * 4 <= NT * D * 4
    GA = place("GA", [P, 2, TOK], F32, f0)
    GB = place("GB", [P, 2, TOK], F32, f0 + 2 * TOK * 4)
    TA = place("TA", [P, 2, TOK], F32, f0 + 4 * TOK * 4)
    TB = place("TB", [P, 2, TOK], F32, f0 + 6 * TOK * 4)
    j0 = region(JBYTES)
    j_at = [j0]

    def in_j(name, shape, dt=F32):
        off = j_at[0]
        j_at[0] += nbytes(shape, dt)
        assert j_at[0] <= j0 + JBYTES, name
        return place(name, shape, dt, off)

    rel_c = in_j("rel_c", [P, WIN + DS])
    rel_n = in_j("rel_n", [P, NSEQ, NS])
    vc = in_j("vc", [P, NSEQ, KVH * HD])
    kc = in_j("kc", [P, NSEQ, KVH, 2 * HD])
    kout = in_j("kout", [P, 2, KVH * HD])
    TS = in_j("TS", [P, 2, G, P])
    j_at[0] = j0
    wr = in_j("wr", [P, DC, E])
    scores = in_j("scores", [P, NT, E])
    sel = in_j("sel", [P, NT, E])
    selm = in_j("selm", [P, NT, E])
    R = in_j("R", [P, NT, E, 6], BF16)
    chosen = in_j("chosen", [P, NT, E], BF16)
    posm = in_j("posm", [P, NT, E])
    onehot = in_j("onehot", [P, 4, NT, P], BF16)
    hh = in_j("hh", [P, 2, FE])
    silu = in_j("silu", [P, FE])
    AT_hi = place("AT_hi", [P, DC, TOK], F32R, j0)
    AT_lo = place("AT_lo", [P, DC, TOK], F32R, c0)
    u_hi_at = [i0, i0 + TOK * 4, once, once + TOK * 4]
    uT_hi = [place(f"uT_hi{i}", [P, TOK], F32R, u_hi_at[i]) for i in range(G)]
    uT_lo = place("uT_lo", [P, G, TOK], F32R, c0 + DC * TOK * 4)
    a_hi = place("a_hi", [P, DC, SB], F32R, g0 + DC * SB * 4)
    b_hi = place("b_hi", [P, G, SB], F32R, once + 2 * TOK * 4)
    assert i0 + 2 * TOK * 4 <= b0 + wslot_bytes and 2 * TOK * 4 + G * SB * 4 <= once_bytes
    o_hi_at = [g_hi_at[0], g_hi_at[1], g0 + DC * SB * 4, c0]
    o_hi = [place(f"o_hi{i}", [P, DC, SB], F32R, o_hi_at[i]) for i in range(D // SB)]
    mT_hi = place("mT_hi", [P, DC, TOK], F32R, a0)
    mT_lo = place("mT_lo", [P, DC, TOK], F32R, b0)
    assert at[0] <= nc.sbuf_usable_end, (at[0], nc.sbuf_usable_end)

    w_at = [g0, c0, b0, h0]
    wgu = [place(f"wgu{i}", [P, 2, DC, FE], F32, w_at[i]) for i in range(WSLOTS)]
    wd = [place(f"wd{i}", [P, FE // P, D], F32, w_at[i] + 2 * DC * FE * 4) for i in range(WSLOTS)]
    y_at = h0 + wslot_bytes
    ysb = place("ysb", [P, 2, D], F32, y_at)
    assert y_at + 2 * D * 4 <= h0 + RAW * DC * SB * 4
    wgu_lo = [place(f"wgu_lo{i}", [P, 2, DC, FE], F32R, w_at[i]) for i in range(WSLOTS)]
    wgu_hi = [place(f"wgu_hi{i}", [P, 2, DC, FE], F32R, a0 + i * 2 * DC * FE * 4) for i in range(2)]
    hT_at = a0 + 2 * 2 * DC * FE * 4
    hT = place("hT", [P, 2, FE // P, P], F32, hT_at)
    xgT_lo = place("xgT_lo", [P, 2, DC, P], F32R, hT_at + 2 * FE * 4)
    xg_at = [f0 + 4096, f0 + 8192, once, once + 4096]
    xg = [place(f"xg{i}", [P, D], F32, xg_at[i]) for i in range(XGSLOTS)]
    assert 2 * 4096 <= once_bytes and D * 4 == 4096
    assert hT_at + 2 * FE * 4 + 2 * D * 4 <= f0 + 4096
    xgT = place("xgT", [P, 2, DC, P], F32R, f0 + 4096 + 2 * D * 4)
    assert 4096 + 4 * D * 4 <= NT * D * 4
    top = place("top", [P, NT, NG, 8], F32, f0)
    gsc = place("gsc", [P, NT, NG], F32, f0 + 2048)
    cmp_a = place("cmp_a", [P, NT, NG, NG], F32, f0 + 2304)
    cmp_b = place("cmp_b", [P, NT, NG, NG], F32, f0 + 4096)
    rank = place("rank", [P, NT, NG], F32, f0 + 5888)
    pen = place("pen", [P, NT, NG], F32, f0 + 6144)
    top8 = place("top8", [P, NT, 8], F32, f0 + 6400)
    wsum = place("wsum", [P, NT], F32, f0 + 6720)
    rsum = place("rsum", [P, NT], F32, f0 + 6784)
    gates = place("gates", [P, NT, E], F32, f0 + 6848)
    rest = place("rest", [P, NT, E], F32, f0 + 8192)
    smask = place("smask", [P, NT, E], F32, f0 + 9536)
    mostf = place("mostf", [P, 1], F32, f0 + 10880)
    swgu = place("swgu", [P, 2, DC, FE], F32, h0)
    swd = place("swd", [P, FE // P, D], F32, h0 + 2 * DC * FE * 4)
    ssilu = place("ssilu", [P, 2, FE], F32, f0 + 12288)
    sup = place("sup", [P, 2, FE], F32, f0 + 14336)
    shT = place("shT", [P, 2, FE // P, P], F32, f0 + 16384)
    sy = place("sy", [P, 2, D], F32, y_at)

    bank = [nc.alloc_psum_tensor(f"bank{i}", [P, 512], F32) for i in range(8)]

    def sem(name):
        return nc.alloc_semaphore(name)

    def sems(name, n):
        return [sem(f"{name}{i}") for i in range(n)]

    w_in = A["w_in"][0]
    blocks = []

    def cols(w, a, n, kc=DC):
        return w[:, a:a + n].rearrange("(c p) n -> p c n", p=P), kc, n

    blocks.append(("k", [(0, *cols(w_in, QE, P))]))
    for s in range(QE // SB):
        blocks.append(("q", [(0, *cols(w_in, s * SB, SB))]))
    blocks.append(("v", [(0, *cols(w_in, KE, P))]))
    for s in range(SGW // SB):
        blocks.append(("vs", [(0, *cols(w_in, UE + s * SB, SB))]))
    for s in range(SGW // SB):
        blocks.append(("u", [(0, *cols(w_in, VE + s * SB, SB))]))
    for s in range(D // SB):
        blocks.append(("ga", [(0, *cols(w_in, VSE + s * SB, SB))]))
        blocks.append(("gb", [(0, *cols(w_in, GAE + s * SB, SB))]))
        blocks.append(("pa", [(0, *cols(A["w_proj_a"][0], s * SB, SB))]))
        blocks.append(("pb", [(0, *cols(A["w_proj_b"][0], s * SB, SB, G))]))
    for s in range(D // SB):
        blocks.append(("wo", [(0, *cols(A["w_out"][0], s * SB, SB))]))
    first_wo = len(blocks) - D // SB
    TMB = ("v", "vs")

    def block_landed(n):
        return sum(16 * len(blocks[m][1]) for m in range(n % RAW, n + 1, RAW))

    zprods = []
    seen = {}
    for n, (kind, _) in enumerate(blocks):
        if kind in TMB or kind == "wo":
            continue
        for j in range(blocks[n][1][0][3] // P):
            zprods.append((n, j, kind, seen.setdefault(kind, 0)))
            seen[kind] += 1
    BY_ACT = ("k", "q", "u", "ga", "gb")
    act_no = {}
    dve_no = {}
    for n, z in enumerate(zprods):
        d = act_no if z[2] in BY_ACT else dve_no
        d[n] = len(d) + 1
    stage_z = {k: [n for n, z in enumerate(zprods) if z[2] in k] for k in (("k", "q"), ("u",), ("ga", "gb", "pa", "pb"))}
    z_kq, z_u, z_merge = stage_z.values()

    split = [n for n, (kind, _) in enumerate(blocks) if kind != "wo"]
    split_no = {n: i for i, n in enumerate(split + list(range(first_wo, len(blocks))))}
    n_early = sum(1 for n in split if blocks[n][0] not in ("ga", "gb", "pa", "pb"))

    def hi_of(n):
        if blocks[n][0] == "wo":
            return o_hi[n - first_wo]
        if split_no[n] < n_early:
            return w_hi[split_no[n] % 2]
        return {"ga": g_hi[0], "gb": g_hi[1], "pa": a_hi, "pb": b_hi}[blocks[n][0]]

    tms = []
    col = 0
    for n, (kind, parts) in enumerate(blocks):
        if kind in TMB:
            width = parts[0][3]
            tms += [(n, width, col, t) for t in range(NT)]
            col += width

    UP = PT * (H // 4)
    US = NSEQ // 2
    UA = UP + US
    rel_pair = [(kv, par) for kv in range(KVH) for par in range(2)]

    x_landed = sems("x_landed", NT)
    consts_landed = sem("consts_landed")
    sgw_landed = sem("sgw_landed")
    brow_landed = sem("brow_landed")
    bcol_pe = sem("bcol_pe")
    bcol_dve = sem("bcol_dve")
    kc_landed = sem("kc_landed")
    vc_landed = sem("vc_landed")
    table_landed = sem("table_landed")
    rel_written = sem("rel_written")
    rel_landed = sem("rel_landed")
    block_in = sems("block_in", RAW)
    x_again = sem("x_again")
    x_lo_stored = sem("x_lo_stored")
    x_lo_landed = sem("x_lo_landed")
    ln_swap = sem("ln_swap")
    wr_landed = sem("wr_landed")
    out_done = sem("out_done")
    keys_stored = sem("keys_stored")
    x1_written = sem("x1_written")
    y_inited = sems("y_inited", 2)
    y_zeroed = sem("y_zeroed")
    shared_landed = sem("shared_landed")
    y_back = sems("y_back", NT)

    pool_consts = sem("pool_consts")
    pool_table = sem("pool_table")
    pool_reln = sem("pool_reln")
    pool_sg = sem("pool_sg")
    pool_vs = sem("pool_vs")
    pool_norm = sem("pool_norm")
    pool_gated = sem("pool_gated")
    pool_merged = sem("pool_merged")
    pool_x1 = sem("pool_x1")
    rows_cleared = sem("rows_cleared")
    pool_sh = sem("pool_sh")
    pool_sy = sem("pool_sy")
    pool_scaled = sem("pool_scaled")
    pool_zero = sem("pool_zero")
    pool_final = sem("pool_final")

    xt_done = sem("xt_done")
    z_done = sem("z_done")
    tm_done = sem("tm_done")
    misc_done = sem("misc_done")
    logits_done = sem("logits_done")
    pt_done = sem("pt_done")
    pv_done = sem("pv_done")
    sg_done = sem("sg_done")
    wo_done_g = sem("wo_done_g")
    x1t_done = sem("x1t_done")
    route_done = sem("route_done")
    pos_done = sem("pos_done")
    sgu_done = sem("sgu_done")
    sht_done = sem("sht_done")
    sdn_done = sem("sdn_done")

    xt_act = sem("xt_act")
    hi_act = sem("hi_act")
    x_lo_act = sem("x_lo_act")
    m_act = sem("m_act")
    au_act = sem("au_act")
    z_act = sem("z_act")
    gelu_act = sem("gelu_act")
    std_act = sem("std_act")
    misc_act = sem("misc_act")
    exp_act = sem("exp_act")
    pt_act = sem("pt_act")
    pv_act = sem("pv_act")
    xn_act = sem("xn_act")
    x1t_act = sem("x1t_act")
    score_act = sem("score_act")
    ssilu_act = sem("ssilu_act")
    sht_act = sem("sht_act")
    sy_act = sem("sy_act")
    fin_act = sem("fin_act")

    dve = sem("dve")
    xt_dve = sem("xt_dve")
    lo_dve = sem("lo_dve")
    x_lo_dve = sem("x_lo_dve")
    m_dve = sem("m_dve")
    x1_dve = sem("x1_dve")
    sy_dve = sem("sy_dve")
    au_dve = sem("au_dve")
    k_dve = sem("k_dve")
    z_dve = sem("z_dve")
    tm_dve = sem("tm_dve")
    stat_dve = sem("stat_dve")
    vsn_dve = sem("vsn_dve")
    misc_dve = sem("misc_dve")
    mx_dve = sem("mx_dve")
    rden_dve = sem("rden_dve")
    pt_dve = sem("pt_dve")
    sg_dve = sem("sg_dve")
    wo_dve = sem("wo_dve")
    nmr_dve = sem("nmr_dve")
    lng_dve = sem("lng_dve")
    x1t_dve = sem("x1t_dve")
    chosen_dve = sem("chosen_dve")
    route_dve = sem("route_dve")
    most_dve = sem("most_dve")

    wgu_in = sems("wgu_in", WSLOTS)
    wd_in = sems("wd_in", WSLOTS)
    xg_in = sems("xg_in", XGSLOTS)
    y_added = sem("y_added")
    gathers_sent = sem("gathers_sent")
    scatters_sent = sem("scatters_sent")
    ex_xt = sem("ex_xt")
    ex_gu = sem("ex_gu")
    ex_ht = sem("ex_ht")
    ex_dn = sem("ex_dn")
    ex_list = sem("ex_list")
    xt_by_act = sem("xt_by_act")
    hi_by_act = sem("hi_by_act")
    silu_by_act = sem("silu_by_act")
    y_by_act = sem("y_by_act")
    xt_by_dve = sem("xt_by_dve")
    lo_by_dve = sem("lo_by_dve")
    h_by_dve = sem("h_by_dve")
    ht_by_dve = sem("ht_by_dve")
    y_by_dve = sem("y_by_dve")
    hot_by_dve = sem("hot_by_dve")
    sum_by_dve = sem("sum_by_dve")
    idx_by_dve = sem("idx_by_dve")
    over_dve = sem("over_dve")
    over_res = sem("over_res")

    N_CONST = 16
    N_CDMA = 13
    NSB = D // SB

    misc = []
    misc.append([("sg", g) for g in range(G)])
    misc.append([("sgs", g) for g in range(G)])
    for b in range(0, NSEQ, 2):
        misc.append([("kc", b), ("kc", b + 1)])
    misc.append([("kout", 0), ("kout", 1)])

    def dram(ap, offset, pattern):
        return bass.AP(ap.tensor, ap.offset + offset, pattern)

    def expert_weights(e):
        one = bass.ds(e, 1)
        return (A["w_gate_e"][0][one].rearrange("a (p c) f -> p (a c) f", p=P),
                A["w_up_e"][0][one].rearrange("a (p c) f -> p (a c) f", p=P),
                A["w_down_e"][0][one].rearrange("a (p j) n -> p (a j) n", p=P))

    def x1_whole(engine, t, first=0):
        if t == NT - 1:
            engine.wait_ge(x1_dve, 2 * (first + 1))
        else:
            engine.wait_ge(pool_final if first else pool_x1, t + 1)

    block_ctx = ExitStack()
    with block_ctx:
        block = block_ctx.enter_context(nc.Block())

        @block.sync
        def _(sp):
            for t, (a, w) in enumerate(TILES):
                src = A["x_prompt"][0][a:a + w, :] if t < PT else A["x_sample"].rearrange("b s d -> (b s) d")
                sp.dma_start(x_in[0:w, t, :], src).then_inc(x_landed[t], 16)

            def load(dst, src, s=consts_landed, few=False):
                sp.dma_start(dst, src, allow_slow_non_contiguous=few).then_inc(s, 16)

            def load_block(n):
                if n >= RAW:
                    kind = blocks[n - RAW][0]
                    if kind in TMB:
                        sp.wait_ge(tm_done, 1 + max(g for g, x in enumerate(tms) if x[0] == n - RAW))
                    else:
                        sp.wait_ge(z_done, 1 + max(g for g, x in enumerate(zprods) if x[0] == n - RAW))
                for c0_, src, kc_, w_ in blocks[n][1]:
                    sp.dma_start(raw[n % RAW][:, 0:kc_, c0_:c0_ + w_], src).then_inc(block_in[n % RAW], 16)

            def load_expert(e, u, free=None):
                slot = u % WSLOTS
                if free is not None:
                    sp.wait_ge(ex_gu, free)
                g_, up_, dn_ = expert_weights(e)
                sp.dma_start(wgu[slot][:, 0, :, :], g_).then_inc(wgu_in[slot], 16)
                sp.dma_start(wgu[slot][:, 1, :, :], up_).then_inc(wgu_in[slot], 16)
                if free is not None:
                    sp.wait_ge(ex_dn, free)
                sp.dma_start(wd[slot][:, :, :], dn_).then_inc(wd_in[slot], 16)

            merge_first = zprods[z_merge[0]][0]
            last_gate = max(g for g in z_merge if zprods[g][2] == "gb")
            for n in range(len(blocks)):
                if n == RAW:
                    load(tm_bias[:, 0:P], A["b_in"][0:1, KE:VE].to_broadcast([P, P]))
                    load(tm_bias[:, P:], A["b_in"][0:1, UE:VSE].to_broadcast([P, SGW]))
                    load(sgln[:, 0, :], A["sg_ln_g"].to_broadcast([P, SGW]))
                    load(sgln[:, 1, :], A["sg_ln_b"].to_broadcast([P, SGW]))
                    load(sgb[:], A["sg_b"].rearrange("a g i -> a (g i)").to_broadcast([P, G * P]).rearrange("p (g i) -> p g i", g=G))
                    load(ln_gb[:, 0, :], A["ln1_g"].to_broadcast([P, D]))
                    load(ln_gb[:, 1, :], A["ln1_b"].to_broadcast([P, D]))
                    load(sink[:], A["attn_sinks"].to_broadcast([P, H]))
                    load(rbias[:], A["router_bias"].to_broadcast([P, E]))
                    for kv, par in rel_pair:
                        r0 = 32 * (2 * par + kv)
                        load(sink_row[r0:r0 + 32, :], dram(A["attn_sinks"], kv * QPK + par, [[2, 4], [0, DS], [1, 1]]), few=True)
                    sp.wait_ge(pool_consts, N_CONST)
                    load(sgw[:], A["sg_w"][0].rearrange("g i j -> i g j"), sgw_landed)
                    for b in range(NSEQ):
                        load(sgs[b * DS:(b + 1) * DS, :, b * DS:(b + 1) * DS],
                             A["sg_w"][0].rearrange("g i j -> i g j")[0:DS, :, 0:DS], sgw_landed)
                    load(vc[:], A["cache_win_v"][0].rearrange("b w h d -> w b (h d)"), vc_landed)
                    sp.wait_ge(xt_dve, 2 * NT)
                    sp.dma_start(x_lo_kept, xT_lo[:].bitcast(F32)).then_inc(x_lo_stored, 16)
                if n == merge_first + RAW:
                    sp.wait_ge(mx_dve, UA)
                    sp.wait_ge(x_lo_stored, 16)
                    sp.dma_start(x_lo_back[:], x_lo_kept).then_inc(x_lo_landed, 16)
                if n == first_wo + 2:
                    sp.wait_ge(z_done, last_gate + 1)
                    for t, (a, w) in enumerate(TILES):
                        src = A["x_prompt"][0][a:a + w, :] if t < PT else A["x_sample"].rearrange("b s d -> (b s) d")
                        sp.dma_start(x1[0:w, t, :], src).then_inc(x_again, 16)
                load_block(n)
                if n == merge_first:
                    sp.wait_ge(misc_dve, 1)
                    sp.dma_start(O["win_k_prompt"][0, 0].rearrange("w h d -> w (h d)"), kout[:, 0, :]).then_inc(keys_stored, 16)
                    sp.dma_start(O["win_k_sample"][0].rearrange("b w h d -> b w (h d)")[:, WIN - DS:WIN, :],
                                 kout[0:NS, 1, :]).then_inc(keys_stored, 16)
                    sp.wait_ge(tm_dve, NT)
                    sp.dma_start(O["win_v_prompt"][0, 0].rearrange("w h d -> w (h d)"), v_sb[:, PT - 1, :]).then_inc(out_done, 16)
                    sp.dma_start(O["win_v_sample"][0].rearrange("b w h d -> b w (h d)")[:, WIN - DS:WIN, :],
                                 v_sb[0:NS, PT, :]).then_inc(out_done, 16)
                    sp.wait_ge(pool_vs, NT)
                    sp.dma_start(O["chunk_v_sample"][0].rearrange("b s g c -> (b s) (g c)"), vs_sb[0:NS, PT, :]).then_inc(out_done, 16)
            for src, dst in ((A["cache_win_k"], O["win_k_sample"]), (A["cache_win_v"], O["win_v_sample"])):
                sp.dma_start(dst[0].rearrange("b w h d -> b w (h d)")[:, 0:WIN - DS, :],
                             src[0].rearrange("b w h d -> b w (h d)")[:, DS:WIN, :]).then_inc(keys_stored, 16)
            sp.wait_ge(wo_done_g, NT * NSB)
            sg_, su_, sdn_ = (A["w_gate_s"][0].rearrange("(p c) f -> p c f", p=P),
                              A["w_up_s"][0].rearrange("(p c) f -> p c f", p=P),
                              A["w_down_s"][0].rearrange("(p j) n -> p j n", p=P))
            sp.dma_start(swgu[:, 0, :, :], sg_).then_inc(shared_landed, 16)
            sp.dma_start(swgu[:, 1, :, :], su_).then_inc(shared_landed, 16)
            sp.dma_start(swd[:, :, :], sdn_).then_inc(shared_landed, 16)
            for t, (a, w) in enumerate(TILES):
                x1_whole(sp, t)
                sp.dma_start(x1_rows[a:a + w, :], x1[0:w, t, :]).then_inc(x1_written, 16)
            for i, nm_ in enumerate(("ln2_g", "ln2_b")):
                sp.dma_start(ln_gb[:, i, :], A[nm_].to_broadcast([P, D])).then_inc(ln_swap, 16)
            for e in range(3):
                load_expert(e, e)
            for t, (a, w) in enumerate(TILES):
                if t == NT - 1:
                    sp.wait_ge(sy_dve, 1)
                else:
                    sp.wait_ge(pool_sy, t + 1)
                sp.dma_start(y_rows[a:a + w, :], sy[0:w, t % 2, :]).then_inc(y_inited[t % 2], 16)
            sp.wait_ge(sdn_done, NT)
            load_expert(3, 3)
            for e in range(WSLOTS, UNROLL):
                load_expert(e, e, e - WSLOTS + 1)
            with sp.Fori(1, E // UNROLL) as i:
                for u in range(UNROLL):
                    load_expert(i * UNROLL + u, u, i * UNROLL + (u - WSLOTS + 1))

            sp.wait_ge(most_dve, 1)
            sp.wait_ge(ex_dn, E)
            most_r = sp.value_load(most[0:1, 0:1], min_val=0, max_val=TOK)
            with sp.If(most_r > P):
                for tile in range(1, NT):
                    with sp.Fori(0, E) as e:
                        done = e + (E * tile)
                        sp.wait_ge(ex_dn, done)
                        g_, up_, dn_ = expert_weights(e)
                        sp.dma_start(wgu[0][:, 0, :, :], g_).then_inc(wgu_in[0], 16)
                        sp.dma_start(wgu[0][:, 1, :, :], up_).then_inc(wgu_in[0], 16)
                        sp.dma_start(wd[0][:, :, :], dn_).then_inc(wd_in[0], 16)
                sp.wait_ge(y_added, 16 * E * NT)
            sp.wait_ge(y_added, 16 * E)
            for t, (a, w) in enumerate(TILES):
                sp.dma_start(x1[0:w, t, :], y_rows[a:a + w, :]).then_inc(y_back[t], 16)
            for t, (a, w) in enumerate(TILES):
                x1_whole(sp, t, 1)
                dst = O["y_prompt"][0][a:a + w, :] if t < PT else O["y_sample"].rearrange("b s d -> (b s) d")
                sp.dma_start(dst, x1[0:w, t, :]).then_inc(out_done, 16)
            sp.wait_ge(out_done, 16 * (3 + NT))
            sp.wait_ge(keys_stored, 16 * 4)

        @block.gpsimd
        def _(pool):
            k = [0]

            def const(ins):
                k[0] += 1
                ins.then_inc(pool_consts, 1)

            const(pool.memset(ident[:], 0.0))
            const(pool.memset(eps[:], LN_EPS))
            const(pool.iota(iota_row[:], [[1, P]], base=0, channel_multiplier=0, allow_small_or_imprecise_dtypes=True))
            const(pool.iota(pcol[:], [[0, 1]], base=0, channel_multiplier=1, allow_small_or_imprecise_dtypes=True))
            const(pool.iota(trash[:], [[0, 1]], base=TOK, channel_multiplier=1, allow_small_or_imprecise_dtypes=True))
            const(pool.memset(before[:], 1.0))
            const(pool.memset(ones_b[:], 1.0))
            const(pool.memset(tie[:], 1.0))
            const(pool.memset(e_row[:], NEG_INF))
            const(pool.memset(rel_n[:], NEG_INF))
            const(pool.memset(sgs[:], 0.0))
            const(pool.memset(mv[:], 1.0))
            const(pool.memset(spare[:], 1.0))
            n_set = k[0]
            pool.wait_ge(pool_consts, n_set)
            const(pool.affine_select(out=ident[:], in_=ident[:], compare_op=ALU.not_equal, fill=1.0, base=0,
                                     pattern=[[-1, P]], channel_multiplier=1))
            const(pool.affine_select(out=before[:], in_=before[:], compare_op=ALU.is_gt, fill=0.0, base=0,
                                     pattern=[[1, P]], channel_multiplier=-1))
            const(pool.affine_select(out=tie[:], in_=tie[:], compare_op=ALU.is_gt, fill=0.0, base=0,
                                     pattern=[[1, NG], [-1, NG]], channel_multiplier=0))
            assert k[0] == N_CONST
            pool.wait_ge(table_landed, 16)
            ranges = bucket_ranges(NBK, WIN)
            for b, lo, hi in ranges:
                pool.tensor_copy(e_row[:, W2 - 1 - hi:W2 - lo],
                                 table_t[:, b:b + 1].to_broadcast([H, hi - lo + 1])).then_inc(pool_table, 1)
            pool.wait_ge(pool_table, len(ranges))
            src = e_row[:, :]
            pool.dma_start(bias_rows,
                           src.rearrange("h (a n) -> h a n", a=1).to_broadcast([H, P, PITCH])).then_inc(rel_written, 16)
            pool.wait_ge(sgw_landed, 16 * (1 + NSEQ))
            pool.affine_select(out=sgw[:], in_=sgw[:], compare_op=ALU.is_ge, fill=0.0, base=0,
                               pattern=[[0, G], [-1, P]], channel_multiplier=1).then_inc(pool_sg, 1)
            pool.affine_select(out=sgs[:], in_=sgs[:], compare_op=ALU.is_ge, fill=0.0, base=0,
                               pattern=[[0, G], [-1, NS]], channel_multiplier=1).then_inc(pool_sg, 1)
            pool.wait_ge(rel_landed, 16 * 5)
            for b in range(NSEQ):
                pool.tensor_copy(rel_n[:, b, b * DS:(b + 1) * DS], rel_c[:, WIN:WIN + DS]).then_inc(pool_reln, 1)

            def norm(u):
                pool.wait_ge(rden_dve, u + 1)
                if u < UP:
                    lo = WIN if u < 4 else 0
                    n, a = 4, L[:, u % LR, 0:4, lo:W2]
                    w = W2 - lo
                else:
                    n, a, w = 2, L[:, u % LR, 0:2, 0:WIN + NS], WIN + NS
                r = rden[:, u % 4, 0:n].rearrange("p (n a) -> p n a", a=1).to_broadcast([P, n, w])
                pool.tensor_tensor(a, a, r, ALU.mult).then_inc(pool_norm, 1)

            pool.wait_ge(consts_landed, N_CDMA * 16)
            for t, (a, w) in enumerate(TILES):
                pool.wait_ge(vsn_dve, 2 * t + 2)
                pool.tensor_tensor(vs_sb[0:w, t, :], vs_sb[0:w, t, :], sgln[0:w, 1, :], ALU.add).then_inc(pool_vs, 1)
            pool.wait_ge(pool_vs, NT)
            pool.memset(sgln[:], 0.0).then_inc(pool_zero, 1)
            pool.wait_ge(pool_zero, 1)
            pool.dma_start(y_rows[TOK:TOK + P, :], sgln[:].rearrange("p a n -> p (a n)")).then_inc(y_zeroed, 16)
            for u in range(UA):
                norm(u)
            for t, (a, w) in enumerate(TILES):
                pool.wait_ge(sg_dve, t + 1)
                pool.tensor_tensor(uT[:, :, a:a + w], uT[:, :, a:a + w], TS[:, t % 2, :, 0:w], ALU.mult).then_inc(pool_gated, 1)
            for m in range(D // P):
                pool.wait_ge(z_dve, 2 * (m // 2) * 2 + 2 + m % 2 + 1)
                pool.tensor_tensor(mT[:, m, :], TA[:, m % 2, :], TB[:, m % 2, :], ALU.add).then_inc(pool_merged, 1)
            for t, (a, w) in enumerate(TILES[:-1]):
                pool.wait_ge(lng_dve, t + 1)
                pool.tensor_tensor(x1[0:w, t, :], x1[0:w, t, :], ln_gb[0:w, 1, :], ALU.add).then_inc(pool_x1, 1)
            def shared_y(t):
                w = TILES[t][1]
                pool.wait_ge(sy_act, 2 * (t + 1))
                pool.tensor_tensor(sy[0:w, t % 2, :], sy[0:w, t % 2, :], x1[0:w, t, :], ALU.add).then_inc(pool_sy, 1)

            bound = pool.to_reg(TOK - 1)

            def sent(n, s, i):
                if not (isinstance(n, int) and n == 0):
                    pool.wait_ge(s, n)
                pool.tensor_tensor(spare[:, i:i + 1], spare[:, 0:1], spare[:, 0:1], ALU.mult).then_inc(s, 1)

            def gather(e, u, landed=None):
                pool.wait_ge(idx_by_dve, e + 1)
                if landed is not False:
                    pool.wait_ge(ex_xt, e - (XGSLOTS - 1))
                sent(e, gathers_sent, 1)
                pool.indirect_dma_start(out=xg[u % XGSLOTS][:], out_offset=None, in_=x1_rows,
                                        in_offset=bass.IndirectOffsetOnAxis(idx_u[:, u:u + 1], 0),
                                        bounds_check=bound, oob_is_err=False).then_inc(xg_in[u % XGSLOTS], 16)

            def first_gathers():
                pool.wait_ge(route_dve, 1)
                for i in range(XGSLOTS):
                    pool.memset(xg[i][:], 0.0).then_inc(rows_cleared, 1)
                pool.wait_ge(rows_cleared, XGSLOTS)
                for e in range(XGSLOTS):
                    gather(e, e, False)

            pool.wait_ge(x1_written, 16 * NT)
            pool.wait_ge(x1t_done, 2 * NT)
            for t, (a, w) in enumerate(TILES):
                pool.tensor_scalar(x1[0:w, t, :], x1[0:w, t, :], ALPHA, None, ALU.mult).then_inc(pool_scaled, 1)
            pool.wait_ge(pool_scaled, NT)
            for t, (a, w) in enumerate(TILES):
                if t == NT - 1:
                    first_gathers()
                pool.wait_ge(ssilu_act, 2 * (t + 1))
                pool.tensor_tensor(ssilu[0:w, t % 2, :], ssilu[0:w, t % 2, :], sup[0:w, t % 2, :], ALU.mult).then_inc(pool_sh, 1)
                if t >= 1:
                    shared_y(t - 1)

            def scatter(e, u, first=False):
                pool.wait_ge(y_by_act, e + 1)
                pool.wait_ge(y_by_dve, e + 1)
                if not first:
                    pool.wait_ge(y_added, 16 * e)
                sent(e, scatters_sent, 2)
                pool.indirect_dma_start(out=y_rows, out_offset=bass.IndirectOffsetOnAxis(idx_u[:, u:u + 1], 0),
                                        in_=ysb[:, u % 2, :], in_offset=None, compute_op=ALU.add).then_inc(y_added, 16)

            pool.wait_ge(y_inited[0], 16 * ((NT + 1) // 2))
            pool.wait_ge(y_inited[1], 16 * (NT // 2))
            pool.wait_ge(y_zeroed, 16)
            for e in range(UNROLL):
                gather(e + XGSLOTS, (e + XGSLOTS) % UNROLL)
                if e >= 1:
                    scatter(e - 1, e - 1, e == 1)
            with pool.Fori(1, E // UNROLL - 1) as i:
                for u in range(UNROLL):
                    gather(i * UNROLL + (u + XGSLOTS), (u + XGSLOTS) % UNROLL)
                    scatter(i * UNROLL + (u - 1), (u - 1) % UNROLL)
            for e in range(E - UNROLL, E):
                if e + XGSLOTS < E:
                    gather(e + XGSLOTS, (e + XGSLOTS) % UNROLL)
                scatter(e - 1, (e - 1) % UNROLL)
            scatter(E - 1, UNROLL - 1)

            pool.wait_ge(y_added, 16 * E)
            most_r = pool.value_load(most[0:1, 0:1], min_val=0, max_val=TOK)
            with pool.If(most_r > P):
                for tile in range(1, NT):
                    with pool.Fori(0, E) as e:
                        n = e + E * tile
                        pool.wait_ge(idx_by_dve, n + 1)
                        pool.wait_ge(ex_xt, n)
                        sent(n, gathers_sent, 1)
                        pool.indirect_dma_start(out=xg[0][:], out_offset=None, in_=x1_rows,
                                                in_offset=bass.IndirectOffsetOnAxis(idx_u[:, 0:1], 0),
                                                bounds_check=bound, oob_is_err=False).then_inc(xg_in[0], 16)
                        pool.wait_ge(y_by_act, n + 1)
                        pool.wait_ge(y_by_dve, n + 1)
                        sent(n, scatters_sent, 2)
                        pool.indirect_dma_start(out=y_rows, out_offset=bass.IndirectOffsetOnAxis(idx_u[:, 0:1], 0),
                                                in_=ysb[:, 0, :], in_offset=None, compute_op=ALU.add).then_inc(y_added, 16)
                        pool.wait_ge(y_added, 16 * n + 16)
            for t, (a, w) in enumerate(TILES[:-1]):
                pool.wait_ge(lng_dve, NT + t + 1)
                pool.tensor_tensor(x1[0:w, t, :], x1[0:w, t, :], ln_gb[0:w, 1, :], ALU.add).then_inc(pool_final, 1)

        @block.scalar
        def _(act):
            def load(dst, src, s=consts_landed, few=False):
                act.dma_start(dst, src, allow_slow_non_contiguous=few).then_inc(s, 16)

            load(table_t[:], A["rel_bias_table"].rearrange("b h -> h b"), table_landed, few=True)
            load(brow[0:NB, :], A["b_in"].rearrange("a (c p) -> (a c) p", p=P), brow_landed)
            def load_kc(b):
                load(kc[:, b, :, :].rearrange("p k (t d) -> p k t d", t=2),
                     dram(A["cache_win_k"], b * WIN * KVH * HD, [[KVH * HD, P], [HD, KVH], [0, 2], [1, HD]]),
                     kc_landed)
            for t, (a, w) in enumerate(TILES):
                for h in range(2):
                    act.wait_ge(xt_done, 2 * t + h + 1)
                    act.activation(xT[:, 4 * h:4 * h + 4, a:a + w],
                                   bank[2 * (t % 2) + h][:, 0:4 * w].rearrange("p (c n) -> p c n", c=4),
                                   ACT.Copy).then_inc(xt_act, 1)

            def split_hi(n):
                act.wait_ge(block_in[n % RAW], block_landed(n))
                _, _, kc_, w_ = blocks[n][1][0]
                act.activation(hi_of(n)[:, 0:kc_, 0:w_], raw[n % RAW][:, 0:kc_, 0:w_], ACT.Copy).then_inc(hi_act, 1)

            split_hi(split[0])
            split_hi(split[1])
            for b in range(NSEQ):
                load_kc(b)
            act.wait_ge(bcol_dve, 1)

            def z_evac(n):
                _, _, kind, m = zprods[n]
                act.wait_ge(z_done, n + 1)
                if kind == "k":
                    for kv in range(KVH):
                        r = slice(HD * kv, HD * kv + HD)
                        for h in range(2):
                            last = act.activation(kT[r, kv, h * HALF:(h + 1) * HALF], bank[2 * h + n % 2][r, 0:HALF],
                                                  ACT.Identity, bias=bcol[r, QE // P:QE // P + 1])
                    last.then_inc(z_act, 1)
                    return
                elif kind == "q":
                    dst, b_, fn = qT[:, m, :], bcol[:, m:m + 1], ACT.Identity
                elif kind == "u":
                    dst, b_, fn = uT[:, m, :], bcol[:, VE // P + m:VE // P + m + 1], ACT.Gelu_apprx_tanh
                else:
                    off = (VSE if kind == "ga" else GAE) // P + m
                    dst, b_, fn = (GA if kind == "ga" else GB)[:, m % 2, :], bcol[:, off:off + 1], ACT.Sigmoid
                    if m >= 2:
                        act.wait_ge(z_dve, 4 * (m // 2 - 1) + (2 if kind == "ga" else 4))
                act.activation(dst[:, 0:HALF], bank[n % 2][:, 0:HALF], fn, bias=b_)
                src = bank[2 + n % 2][:, SEQ - HALF:HALF]
                if kind == "q":
                    act.activation(dst[:, HALF:SEQ], bank[2 + n % 2][:, 0:SEQ - HALF], fn, bias=b_)
                    act.activation(qs[:, :, m, :], src.rearrange("p (b e) -> p b e", b=NSEQ), fn, bias=b_).then_inc(z_act, 1)
                else:
                    act.activation(dst[:, HALF:TOK], bank[2 + n % 2][:, 0:HALF], fn, bias=b_).then_inc(z_act, 1)

            for i in range(n_early):
                nb = split[i]
                for n, z in enumerate(zprods):
                    if z[0] == nb:
                        z_evac(n)
                if i == 2:
                    act.wait_ge(rel_written, 16)
                    load(rel[:], dram(bias_rows, WIN - 1, [[PITCH - 1, P], [P * PITCH, H], [1, W2]]), rel_landed)
                    for kv, par in rel_pair:
                        r0 = 32 * (2 * par + kv)
                        load(rel_c[r0:r0 + 32, :], dram(bias_rows, (kv * QPK + par) * P * PITCH + WIN - 1,
                                                        [[2 * P * PITCH, 4], [PITCH - 1, DS], [1, WIN + DS]]), rel_landed)
                if blocks[nb][0] == "u" and blocks[nb - 1][0] != "u":
                    act.wait_ge(stat_dve, NT)
                    act.activation(std[:, :], mv[:, :, 1], ACT.Sqrt, bias=eps[:, 0:1]).then_inc(std_act, 1)
                if i + 2 < n_early:
                    if blocks[nb][0] in TMB:
                        act.wait_ge(tm_done, 1 + max(g for g, x in enumerate(tms) if x[0] == nb))
                    split_hi(split[i + 2])
                if i == split_no[tms[-1][0]]:
                    for t, (a, w) in enumerate(TILES):
                        act.wait_ge(tm_dve, NT * 2 + t + 1)
                        act.activation(vs_sb[0:w, t, :], vs_sb[0:w, t, :], ACT.Gelu_apprx_tanh).then_inc(gelu_act, 1)
            for g, items in enumerate(misc):
                if items[0][0] == "sg":
                    act.wait_ge(misc_done, g + 1)
                    act.activation(sgwT[:], bank[6 + g % 2][:, :].rearrange("p (g n) -> p g n", g=G), ACT.Copy).then_inc(misc_act, 1)
                elif items[0][0] == "sgs":
                    act.wait_ge(misc_done, g + 1)
                    act.activation(sgsT[:], bank[6 + g % 2][0:NS, 0:G * NS].rearrange("p (g n) -> p g n", g=G),
                                   ACT.Copy).then_inc(misc_act, 1)
                elif items[0][0] == "kc":
                    b = items[0][1]
                    act.wait_ge(misc_done, g + 1)
                    act.activation(kcT[:, b:b + 2, :, :], bank[6 + g % 2][:, :].rearrange("p (b k n) -> p b k n", b=2, k=KVH),
                                   ACT.Copy).then_inc(misc_act, 1)
            def exps(u):
                act.wait_ge(mx_dve, u + 1)
                k_ = u % LR
                if u < UP:
                    lo, n, w = (WIN if u < 4 else 0), 4, W2
                else:
                    lo, n, w = 0, 2, WIN + NS
                for j in range(n):
                    act.activation(L[:, k_, j, lo:w], L[:, k_, j, lo:w], ACT.Exp, bias=nm[:, u % 4, j:j + 1],
                                   accum_out=den[:, u % 4, j:j + 1])
                act.activation(es[:, u % 4, 0:n], sd[:, u % 4, 0:n], ACT.Exp).then_inc(exp_act, 1)

            def pt_evac(u):
                act.wait_ge(pt_done, u + 1)
                if u >= 2:
                    act.wait_ge(pv_done, u - 1)
                if u < UP:
                    h0_ = 1 if u < 4 else 0
                    act.activation(PTs[:, u % 2, 0:2, h0_:2, :],
                                   bank[4][:, :].rearrange("p (j h n) -> p j h n", j=2, h=2)[:, :, h0_:2, :],
                                   ACT.Copy).then_inc(pt_act, 1)
                else:
                    act.activation(PTs[:, u % 2, 0:2, 0, :], bank[4][:, 0:256].rearrange("p (j n) -> p j n", j=2),
                                   ACT.Copy).then_inc(pt_act, 1)

            act.wait_ge(x_lo_stored, 16)

            def pv_evac(u):
                act.wait_ge(pv_done, u + 1)
                if u < UP:
                    b, hg = u // 4, u % 4
                    act.activation(AT[:, 2 * hg:2 * hg + 2, b * P:(b + 1) * P],
                                   bank[6 + u % 2][:, 0:2 * P].rearrange("p (c n) -> p c n", c=2), ACT.Copy).then_inc(pv_act, 1)
                else:
                    a = SEQ + (u - UP) * 2 * DS
                    act.activation(AT[:, :, a:a + 2 * DS].rearrange("p c (q e) -> p c q e", q=2),
                                   bank[6 + u % 2][:, 0:2 * DC * DS].rearrange("p (q c e) -> p c q e", q=2, c=DC),
                                   ACT.Copy).then_inc(pv_act, 1)

            for m in range(UA + 5):
                if 0 <= m - 4 < UA:
                    pt_evac(m - 4)
                if 0 <= m - 2 < UA:
                    exps(m - 2)
                if 0 <= m - 4 < UA:
                    pv_evac(m - 4)
            act.wait_ge(x_lo_landed, 16)
            act.activation(xT_lo2[:, 0:4, :], x_lo_back[:, 0:4, :], ACT.Copy).then_inc(x_lo_act, 1)
            split_hi(split[n_early])
            act.wait_ge(sg_done, NT)
            act.wait_ge(out_done, 16 * 3)
            split_hi(split[n_early + 1])
            act.wait_ge(pool_gated, NT)
            act.wait_ge(pv_act, UA)
            act.wait_ge(keys_stored, 16 * 2)
            act.wait_ge(y_zeroed, 16)
            act.activation(AT_hi[:], AT[:], ACT.Copy).then_inc(au_act, 1)
            for g in range(G):
                act.activation(uT_hi[g][:], uT[:, g, :], ACT.Copy).then_inc(au_act, 1)
            split_hi(split[n_early + 2])
            split_hi(split[n_early + 3])
            for i in range(n_early, len(split)):
                for n in z_merge:
                    if zprods[n][0] == split[i] and zprods[n][2] in BY_ACT:
                        z_evac(n)
                if blocks[split[i]][0] == "gb" and i + 3 < len(split):
                    split_hi(split[i + 3])
                    split_hi(split[i + 4])
                    act.wait_ge(z_done, 1 + max(n for n in z_merge if zprods[n][0] == split[i + 1]))
                    split_hi(split[i + 5])
                    act.wait_ge(z_done, 1 + max(n for n in z_merge if zprods[n][0] == split[i + 2]))
                    split_hi(split[i + 6])

            def m_hi(m):
                act.wait_ge(pool_merged, m + 1)
                act.activation(mT_hi[:, m, :], mT[:, m, :], ACT.Copy).then_inc(m_act, 1)

            split_hi(first_wo)
            split_hi(first_wo + 1)
            for m in range(DC - 2):
                m_hi(m)
            act.wait_ge(z_done, 1 + max(n for n in z_merge if zprods[n][2] == "pa"))
            split_hi(first_wo + 2)
            for m in range(DC - 2, DC):
                m_hi(m)
            split_hi(first_wo + 3)
            def layer_norm_rows(first, s):
                for t, (a, w) in enumerate(TILES):
                    act.wait_ge(stat_dve, NT * (1 + first) + t + 1)
                    act.activation(std[0:w, t:t + 1], mv[0:w, t, 1:2], ACT.Sqrt, bias=eps[0:w, 0:1]).then_inc(std_act, 1)
                    act.wait_ge(nmr_dve, first * NT + t + 1)
                    act.activation(x1[0:w, t, :], x1[0:w, t, :], ACT.Identity, bias=nmr[0:w, t:t + 1],
                                   scale=rstd[0:w, t:t + 1]).then_inc(s, 1)
            act.wait_ge(mx_dve, UA)
            load(wr[:], A["w_router"][0].rearrange("(p c) e -> p c e", p=P), wr_landed)
            layer_norm_rows(0, xn_act)
            for t, (a, w) in enumerate(TILES):
                act.wait_ge(x1t_done, 2 * t + 1)
                act.activation(x1T[:, 0:4, a:a + w], bank[2 * (t % 2)][:, 0:4 * w].rearrange("p (c n) -> p c n", c=4),
                               ACT.Copy).then_inc(x1t_act, 1)
            act.wait_ge(route_done, NT)
            for t, (a, w) in enumerate(TILES):
                act.activation(scores[0:w, t, :], bank[4][0:w, t * E:(t + 1) * E], ACT.Sigmoid).then_inc(score_act, 1)

            def sh_silu(t):
                w = TILES[t][1]
                act.wait_ge(sgu_done, t + 1)
                if t >= 2:
                    act.wait_ge(sht_done, t - 1)
                act.activation(ssilu[0:w, t % 2, :], bank[5][0:w, 0:FE], ACT.Silu).then_inc(ssilu_act, 1)
                act.activation(sup[0:w, t % 2, :], bank[5][0:w, FE:2 * FE], ACT.Copy).then_inc(ssilu_act, 1)

            def sh_rest(t):
                w = TILES[t][1]
                act.wait_ge(sht_done, t + 1)
                if t >= 2:
                    act.wait_ge(sdn_done, t - 1)
                act.activation(shT[:, t % 2, :, 0:w], bank[6][:, 0:2 * w].rearrange("p (j n) -> p j n", j=2),
                               ACT.Copy).then_inc(sht_act, 1)

            def sh_out(t):
                w = TILES[t][1]
                act.wait_ge(sdn_done, t + 1)
                if t >= 2:
                    act.wait_ge(y_inited[t % 2], 16 * (t // 2))
                for j in range(2):
                    act.activation(sy[0:w, t % 2, j * 512:(j + 1) * 512], bank[j][0:w, :], ACT.Copy).then_inc(sy_act, 1)

            for t in range(NT + 1):
                if t < NT:
                    sh_silu(t)
                if t >= 1:
                    sh_out(t - 1)
                if t < NT:
                    sh_rest(t)

            def ex_xt_evac(e, u):
                act.wait_ge(ex_xt, e + 1)
                for h in range(2):
                    act.activation(xgT[:, u % 2, 4 * h:4 * h + 4, :], bank[h][:, :].rearrange("p (c n) -> p c n", c=4),
                                   ACT.Copy).then_inc(xt_by_act, 1)

            def weights_hi(u, landed):
                act.wait_ge(wgu_in[u % WSLOTS], landed * 32)
                act.activation(wgu_hi[u % 2][:], wgu[u % WSLOTS][:], ACT.Copy).then_inc(hi_by_act, 1)

            def ex_silu(e, u):
                act.wait_ge(ex_gu, e + 1)
                act.activation(silu[:], bank[2][:, 0:FE], ACT.Silu).then_inc(silu_by_act, 1)

            def ex_y(e, u, free=True):
                act.wait_ge(ex_dn, e + 1)
                if free:
                    act.wait_ge(y_added, (e - 1) * 16)
                act.activation(ysb[:, u % 2, 0:512], bank[3][:, :], ACT.Copy).then_inc(y_by_act, 1)

            ex_xt_evac(0, 0)
            act.wait_ge(pool_sy, NT - 1)
            act.wait_ge(sy_dve, 1)
            weights_hi(1, 1)
            act.wait_ge(y_inited[0], 16 * ((NT + 1) // 2))
            act.wait_ge(y_inited[1], 16 * (NT // 2))

            def step(e, u, turn, first=False, last=False, ahead=True, free=True):
                if not last:
                    ex_xt_evac(e + 1, u + 1)
                if not first:
                    act.wait_ge(h_by_dve, e)
                ex_silu(e, u)
                if ahead:
                    weights_hi(u + 2, turn * (UNROLL // WSLOTS) + ((u + 2) // WSLOTS + 1))
                if not first:
                    ex_y(e - 1, u - 1, free)

            for e in range(UNROLL):
                step(e, e, 0, first=e == 0, free=e >= 3)
            with act.Fori(1, E // UNROLL - 1) as i:
                for u in range(UNROLL):
                    step(i * UNROLL + u, u, i)
            for e in range(E - UNROLL, E):
                step(e, e % UNROLL, E // UNROLL - 1, last=e == E - 1, ahead=e + 2 < E)
            ex_y(E - 1, E - 1)

            act.wait_ge(y_added, 16 * E)
            most_r = act.value_load(most[0:1, 0:1], min_val=0, max_val=TOK)
            with act.If(most_r > P):
                for tile in range(1, NT):
                    with act.Fori(0, E) as e:
                        n = e + E * tile
                        weights_hi(0, e + E * (tile - 1) + (E // WSLOTS + 1))
                        ex_xt_evac(n, 0)
                        ex_silu(n, 0)
                        act.wait_ge(ex_dn, n + 1)
                        act.activation(ysb[:, 0, 0:512], bank[3][:, :], ACT.Copy).then_inc(y_by_act, 1)
            layer_norm_rows(1, fin_act)

        @block.vector
        def _(v):
            k = [0]

            def then(ins):
                k[0] += 1
                ins.then_inc(dve, 1)
                v.wait_ge(dve, k[0])

            v.wait_ge(bcol_pe, 1)
            v.tensor_copy(bcol[:], bank[7][:, 0:NB]).then_inc(bcol_dve, 1)
            for t, (a, w) in enumerate(TILES):
                for h in range(2):
                    v.wait_ge(xt_act, 2 * t + h + 1)
                    v.tensor_tensor(xT_lo[:, 4 * h:4 * h + 4, a:a + w],
                                    bank[2 * (t % 2) + h][:, 0:4 * w].rearrange("p (c n) -> p c n", c=4),
                                    xT[:, 4 * h:4 * h + 4, a:a + w].bitcast(F32), ALU.subtract).then_inc(xt_dve, 1)

            def split_lo(n):
                v.wait_ge(hi_act, split_no[n] + 1)
                _, _, kc_, w_ = blocks[n][1][0]
                v.tensor_tensor(w_lo[n % RAW][:, 0:kc_, 0:w_], raw[n % RAW][:, 0:kc_, 0:w_], hi_of(n)[:, 0:kc_, 0:w_].bitcast(F32),
                                ALU.subtract).then_inc(lo_dve, 1)

            for i in range(split_no[tms[0][0]] + 2):
                if i == 2:
                    v.wait_ge(z_act, 1)
                    for kv in range(KVH):
                        v.tensor_copy(kT[HD - HD * kv:2 * HD - HD * kv, kv, :],
                                      kT[HD * kv:HD * kv + HD, kv, :]).then_inc(k_dve, 1)
                split_lo(split[i])
            v.wait_ge(consts_landed, N_CDMA * 16)
            for g, (n, width, c, t) in enumerate(tms):
                w = TILES[t][1]
                v.wait_ge(tm_done, g + 1)
                dst = v_sb[0:w, t, :] if c == 0 else vs_sb[0:w, t, c - P:c - P + width]
                v.tensor_tensor(dst, bank[4 + g % 2][0:w, 0:width], tm_bias[0:w, c:c + width], ALU.add).then_inc(tm_dve, 1)
                if t == NT - 1 and split_no[n] + 2 < n_early:
                    split_lo(split[split_no[n] + 2])
            for t, (a, w) in enumerate(TILES):
                v.wait_ge(gelu_act, t + 1)
                then(v.bn_stats(stat6[0:w, 0, :], vs_sb[0:w, t, :]))
                v.bn_aggr(mv[0:w, t, :], stat6[0:w, 0, :]).then_inc(stat_dve, 1)
                v.wait_ge(stat_dve, t + 1)
            v.wait_ge(std_act, 1)
            then(v.reciprocal(rstd[:, :], std[:, :]))
            for t, (a, w) in enumerate(TILES):
                x_ = vs_sb[0:w, t, :]
                v.tensor_scalar(x_, x_, mv[0:w, t, 0:1], rstd[0:w, t:t + 1], ALU.subtract, ALU.mult).then_inc(vsn_dve, 1)
                v.wait_ge(vsn_dve, 2 * t + 1)
                v.tensor_tensor(x_, x_, sgln[0:w, 0, :], ALU.mult).then_inc(vsn_dve, 1)

            g = len(misc) - 1
            v.wait_ge(misc_done, g + 1)
            for i in range(2):
                w = TILES[PT - 1 + i][1]
                last = v.tensor_copy(kout[0:w, i, :].rearrange("p (k d) -> p k d", k=KVH),
                                     bank[6 + g % 2][0:w, :].rearrange("p (a k n) -> p a k n", a=2, k=KVH)[:, i, :, 0:HD])
            last.then_inc(misc_dve, 1)
            v.wait_ge(rel_landed, 16 * 5)
            v.wait_ge(pool_reln, NSEQ)

            def maxima(u):
                v.wait_ge(logits_done, u + 1)
                if u >= LR:
                    v.wait_ge(pt_done, u - LR + 1)
                s_, q_ = u % LR, u % 4
                if u < UP:
                    hg, lo, n = u % 4, (WIN if u < 4 else 0), 4
                    for j in range(2):
                        v.scalar_tensor_tensor(L[:, s_, j:4:2, lo:W2],
                                               bank[2 * (u % 2) + j][:, :].rearrange("p (h n) -> p h n", h=2)[:, :, lo:W2], SCALE,
                                               rel[:, 4 * hg + j:4 * hg + 4:2, lo:W2], ALU.mult, ALU.add)\
                         .then_inc(dve, 1)
                        k[0] += 1
                    v.wait_ge(dve, k[0])
                    then(v.tensor_reduce(mx[:, q_, 0:n], L[:, s_, 0:n, lo:W2], AX, ALU.max))
                    then(v.tensor_tensor(mx[:, q_, 0:n], mx[:, q_, 0:n], sink[:, 4 * hg:4 * hg + 4], ALU.max))
                    then(v.tensor_scalar(nm[:, q_, 0:n], mx[:, q_, 0:n], -1.0, None, ALU.mult))
                    v.tensor_tensor(sd[:, q_, 0:n], sink[:, 4 * hg:4 * hg + 4], nm[:, q_, 0:n], ALU.add).then_inc(mx_dve, 1)
                else:
                    b, n = (u - UP) * 2, 2
                    for par in range(2):
                        r = slice(HD * par, HD * par + HD)
                        lg = bank[2 * (u % 2) + par][r, 0:2 * (WIN + NS)].rearrange("p (q n) -> p q n", q=2)
                        v.scalar_tensor_tensor(L[r, s_, 0:2, 0:WIN], lg[:, :, 0:WIN], SCALE,
                                               rel_c[r, 0:WIN].rearrange("p (a n) -> p a n", a=1).to_broadcast([HD, 2, WIN]),
                                               ALU.mult, ALU.add).then_inc(dve, 1)
                        v.scalar_tensor_tensor(L[r, s_, 0:2, WIN:WIN + NS], lg[:, :, WIN:WIN + NS], SCALE,
                                               rel_n[r, b:b + 2, :], ALU.mult, ALU.add).then_inc(dve, 1)
                        k[0] += 2
                    v.wait_ge(dve, k[0])
                    then(v.tensor_reduce(mx[:, q_, 0:n], L[:, s_, 0:n, 0:WIN + NS], AX, ALU.max))
                    then(v.tensor_scalar(mx[:, q_, 0:n], mx[:, q_, 0:n], sink_row[:, 0:1], None, ALU.max))
                    then(v.tensor_scalar(nm[:, q_, 0:n], mx[:, q_, 0:n], -1.0, None, ALU.mult))
                    v.tensor_scalar(sd[:, q_, 0:n], nm[:, q_, 0:n], sink_row[:, 0:1], None, ALU.add).then_inc(mx_dve, 1)

            def over_sum(u):
                n = 4 if u < UP else 2
                v.wait_ge(exp_act, u + 1)
                q_ = u % 4
                then(v.tensor_tensor(den[:, q_, 0:n], den[:, q_, 0:n], es[:, q_, 0:n], ALU.add))
                v.reciprocal(rden[:, q_, 0:n], den[:, q_, 0:n]).then_inc(rden_dve, 1)

            def pt_evac(u):
                v.wait_ge(pt_done, u + 1)
                if u >= 2:
                    v.wait_ge(pv_done, u - 1)
                if u < UP:
                    h0_ = 1 if u < 4 else 0
                    v.tensor_copy(PTs[:, u % 2, 2:4, h0_:2, :],
                                  bank[5][:, :].rearrange("p (j h n) -> p j h n", j=2, h=2)[:, :, h0_:2, :]).then_inc(pt_dve, 1)
                else:
                    v.tensor_copy(PTs[0:NS, u % 2, 0:2, 1, :], bank[5][0:NS, 0:256].rearrange("p (j n) -> p j n", j=2))\
                     .then_inc(pt_dve, 1)

            for m in range(UA + 5):
                if 0 <= m - 4 < UA:
                    pt_evac(m - 4)
                if 0 <= m - 1 < UA:
                    maxima(m - 1)
                if 0 <= m - 2 < UA:
                    over_sum(m - 2)
            for t, (a, w) in enumerate(TILES):
                if t == 2:
                    v.wait_ge(x_lo_landed, 16)
                    v.tensor_copy(xT_lo2[:, 4:8, :], x_lo_back[:, 4:8, :]).then_inc(x_lo_dve, 1)
                v.wait_ge(sg_done, t + 1)
                if t >= 2:
                    v.wait_ge(pool_gated, t - 1)
                if t < PT:
                    v.tensor_tensor(TS[:, t % 2, :, :], bank[4 + t % 2][:, :].rearrange("p (g n) -> p g n", g=G), sgb[:],
                                    ALU.add).then_inc(sg_dve, 1)
                else:
                    for g in range(G):
                        last = v.tensor_tensor(TS[:, t % 2, g, 0:w].rearrange("p (b i) -> p b i", b=NSEQ),
                                               bank[4 + t % 2][:, g * w:(g + 1) * w].rearrange("p (b i) -> p b i", b=NSEQ),
                                               sgb[:, g, 0:DS].rearrange("p (a i) -> p a i", a=1).to_broadcast([P, NSEQ, DS]),
                                               ALU.add)
                    last.then_inc(sg_dve, 1)
            for i in range(n_early, n_early + 2):
                split_lo(split[i])
            v.wait_ge(au_act, 1)
            v.tensor_tensor(AT_lo[:], AT[:], AT_hi[:].bitcast(F32), ALU.subtract).then_inc(au_dve, 1)
            for g in range(G):
                v.wait_ge(au_act, g + 2)
                v.tensor_tensor(uT_lo[:, g, :], uT[:, g, :], uT_hi[g][:].bitcast(F32), ALU.subtract).then_inc(au_dve, 1)
            for i in range(n_early + 2, n_early + 4):
                split_lo(split[i])
            def m_lo(m):
                v.wait_ge(m_act, m + 1)
                v.tensor_tensor(mT_lo[:, m, :], mT[:, m, :], mT_hi[:, m, :].bitcast(F32), ALU.subtract).then_inc(m_dve, 1)

            for n in z_merge:
                _, _, kind, m = zprods[n]
                if kind in BY_ACT:
                    continue
                v.wait_ge(z_done, n + 1)
                gate, dst, name = (GA, TA, "ga") if kind == "pa" else (GB, TB, "gb")
                gn = [i for i in z_merge if zprods[i][2] == name and zprods[i][3] == m][0]
                v.wait_ge(z_act, act_no[gn])
                if m >= 2:
                    v.wait_ge(pool_merged, m - 1)
                v.tensor_tensor(dst[:, m % 2, 0:HALF], bank[n % 2][:, 0:HALF], gate[:, m % 2, 0:HALF], ALU.mult)
                v.tensor_tensor(dst[:, m % 2, HALF:TOK], bank[2 + n % 2][:, 0:HALF], gate[:, m % 2, HALF:TOK], ALU.mult)\
                 .then_inc(z_dve, 1)
                later = n_early + 4 * (m // 2 + 1) + m % 2
                if kind == "pa" and later < len(split):
                    split_lo(split[later])
                elif kind == "pb" and m % 2 and later < len(split):
                    split_lo(split[later + 1])
                    split_lo(split[later + 2])
                elif kind == "pa" and m == DC - 2:
                    split_lo(first_wo)
                    split_lo(first_wo + 1)
                elif kind == "pa" and m == DC - 1:
                    for i in range(DC - 2):
                        m_lo(i)
            for m in range(DC - 2, DC):
                m_lo(m)
            split_lo(first_wo + 2)
            split_lo(first_wo + 3)
            v.wait_ge(x_again, 16 * NT)

            def stats(t, first):
                w = TILES[t][1]
                for j in range(2):
                    v.bn_stats(stat6[0:w, j, :], x1[0:w, t, j * 512:(j + 1) * 512]).then_inc(dve, 1)
                    k[0] += 1
                v.wait_ge(dve, k[0])
                v.bn_aggr(mv[0:w, t, :], stat6[0:w, :, :]).then_inc(stat_dve, 1)

            def norm_terms(t, first):
                w = TILES[t][1]
                v.wait_ge(std_act, 1 + first * NT + t + 1)
                then(v.reciprocal(rstd[0:w, t:t + 1], std[0:w, t:t + 1]))
                v.scalar_tensor_tensor(nmr[0:w, t:t + 1], mv[0:w, t, 0:1], -1.0, rstd[0:w, t:t + 1], ALU.mult, ALU.mult)\
                 .then_inc(nmr_dve, 1)

            def gain(t, first, s):
                w = TILES[t][1]
                v.wait_ge(s, t + 1)
                v.tensor_tensor(x1[0:w, t, :], x1[0:w, t, :], ln_gb[0:w, 0, :], ALU.mult).then_inc(lng_dve, 1)
                if t == NT - 1:
                    v.wait_ge(lng_dve, NT * (first + 1))
                    for h in range(2):
                        c = slice(h * D // 2, (h + 1) * D // 2)
                        v.tensor_tensor(x1[0:w, t, c], x1[0:w, t, c], ln_gb[0:w, 1, c], ALU.add).then_inc(x1_dve, 1)

            for t, (a, w) in enumerate(TILES):
                for s in range(D // SB):
                    g = t * (D // SB) + s
                    v.wait_ge(wo_done_g, g + 1)
                    v.scalar_tensor_tensor(x1[0:w, t, s * SB:(s + 1) * SB], x1[0:w, t, s * SB:(s + 1) * SB], ALPHA,
                                           bank[4 + g % 2][0:w, 0:SB], ALU.mult, ALU.add).then_inc(wo_dve, 1)
                    if s == 0 and t >= 1:
                        gain(t - 1, 0, xn_act)
                v.wait_ge(wo_dve, (t + 1) * (D // SB))
                stats(t, 0)
                norm_terms(t, 0)

            def x1t_evac(t):
                a, w = TILES[t]
                v.wait_ge(x1t_done, 2 * t + 2)
                v.tensor_copy(x1T[:, 4:8, a:a + w], bank[2 * (t % 2) + 1][:, 0:4 * w].rearrange("p (c n) -> p c n", c=4))\
                 .then_inc(x1t_dve, 1)

            x1t_evac(0)
            x1t_evac(1)
            gain(NT - 1, 0, xn_act)
            for t in range(2, NT):
                x1t_evac(t)

            v.wait_ge(keys_stored, 64)
            then(v.memset(scores[NS:P, NT - 1, :], 0.0))
            v.wait_ge(score_act, NT)
            EG = [P, NT, NG, EPG]
            then(v.tensor_tensor(sel[:], scores[:], rbias[:].rearrange("p (a e) -> p a e", a=1).to_broadcast([P, NT, E]), ALU.add))
            for t in range(NT):
                for g in range(NG):
                    v.max(top[:, t, g, :], sel[:, t, g * EPG:(g + 1) * EPG]).then_inc(dve, 1)
                    k[0] += 1
            v.wait_ge(dve, k[0])
            then(v.tensor_tensor(gsc[:], top[:, :, :, 0], top[:, :, :, 1], ALU.add))
            for t in range(NT):
                mine = gsc[:, t, :].rearrange("p (g a) -> p g a", a=1).to_broadcast([P, NG, NG])
                other = gsc[:, t, :].rearrange("p (a g) -> p a g", a=1).to_broadcast([P, NG, NG])
                v.tensor_tensor(cmp_a[:, t, :, :], other, mine, ALU.is_gt).then_inc(dve, 1)
                v.tensor_tensor(cmp_b[:, t, :, :], other, mine, ALU.is_equal).then_inc(dve, 1)
                k[0] += 2
            v.wait_ge(dve, k[0])
            for t in range(NT):
                v.tensor_tensor(cmp_b[:, t, :, :], cmp_b[:, t, :, :], tie[:], ALU.mult).then_inc(dve, 1)
                k[0] += 1
            v.wait_ge(dve, k[0])
            then(v.tensor_tensor(cmp_a[:], cmp_a[:], cmp_b[:], ALU.add))
            then(v.tensor_reduce(rank[:], cmp_a[:], AX, ALU.add))
            then(v.tensor_scalar(rank[:], rank[:], float(TOPG), None, ALU.is_lt))
            then(v.tensor_scalar(pen[:], rank[:], 1.0, -NEG_INF, ALU.subtract, ALU.mult))
            bc = lambda a: a.rearrange("p t (g a) -> p t g a", a=1).to_broadcast(EG)
            v4 = lambda a: a.rearrange("p t (g e) -> p t g e", g=NG)
            then(v.tensor_tensor(v4(sel[:]), v4(sel[:]), bc(rank[:]), ALU.mult))
            then(v.tensor_tensor(v4(sel[:]), v4(sel[:]), bc(pen[:]), ALU.add))
            for t in range(NT):
                v.max(top8[:, t, :], sel[:, t, :]).then_inc(dve, 1)
                k[0] += 1
            v.wait_ge(dve, k[0])
            for t in range(NT):
                v.match_replace(selm[:, t, :], top8[:, t, :], sel[:, t, :], TAKEN).then_inc(dve, 1)
                k[0] += 1
            v.wait_ge(dve, k[0])
            then(v.tensor_tensor(smask[:], selm[:], sel[:], ALU.not_equal))
            then(v.memset(smask[NS:P, NT - 1, :], 0.0))
            v.tensor_copy(chosen[:], smask[:]).then_inc(chosen_dve, 1)
            then(v.tensor_tensor(gates[:], scores[:], smask[:], ALU.mult))
            then(v.tensor_reduce(wsum[:], gates[:], AX, ALU.add))
            then(v.memset(wsum[NS:P, NT - 1:NT], 1.0))
            then(v.reciprocal(rsum[:], wsum[:]))
            then(v.tensor_tensor(gates[:], gates[:], rsum[:].rearrange("p (t a) -> p t a", a=1).to_broadcast([P, NT, E]), ALU.mult))
            then(v.tensor_scalar(gates[:], gates[:], ROUTED, None, ALU.mult))
            then(v.tensor_copy(R[:, :, :, 3], gates[:]))
            then(v.tensor_tensor(rest[:], gates[:], R[:, :, :, 3], ALU.subtract))
            then(v.tensor_copy(R[:, :, :, 4], rest[:]))
            then(v.tensor_tensor(rest[:], rest[:], R[:, :, :, 4], ALU.subtract))
            then(v.tensor_copy(R[:, :, :, 5], rest[:]))
            then(v.tensor_copy(R[:, :, :, 0], pcol[:, 0:1].rearrange("p (a b) -> p a b", a=1).to_broadcast([P, NT, E])))
            for t in range(NT):
                then(v.memset(R[:, t, :, 1], float(t * P - TOK)))
            v.wait_ge(pos_done, 1)
            then(v.scalar_tensor_tensor(posm[:], bank[7][:, 0:NT * E].rearrange("p (t e) -> p t e", t=NT), 1.0, smask[:],
                                        ALU.add, ALU.mult))
            then(v.tensor_scalar(posm[:], posm[:], -1.0, None, ALU.add))
            then(v.tensor_scalar(R[:, :, :, 2], posm[:], -1.0, None, ALU.mult))
            then(v.tensor_reduce(mostf[:], bank[7][:, NT * E:NT * E + E], AX, ALU.max))
            v.tensor_copy(most[:], mostf[:]).then_inc(most_dve, 1)
            v.wait_ge(most_dve, 1)
            v.memset(mostf[:], 0.0).then_inc(route_dve, 1)

            def hot(e, u, base=iota_row, wait=True):
                if wait:
                    v.wait_ge(ex_list, e - 3)
                pos = posm[:, :, bass.ds(e, 1)].to_broadcast([P, NT, P])
                v.tensor_tensor(onehot[:, u % 4, :, :], base[:].rearrange("p (a n) -> p a n", a=1).to_broadcast([P, NT, P]),
                                pos, ALU.is_equal).then_inc(hot_by_dve, 1)

            def idx(e, u, wait=True):
                v.wait_ge(ex_list, e + 1)
                if wait:
                    v.wait_ge(y_added, 16 * (e - UNROLL + 1))
                v.tensor_reduce(gate_idx[:, u, :], bank[7][:, 0:6].rearrange("p (a n) -> p a n", a=2), AX, ALU.add)\
                 .then_inc(sum_by_dve, 1)
                v.wait_ge(sum_by_dve, e + 1)
                v.tensor_scalar(idx_u[:, u:u + 1], gate_idx[:, u, 0:1], trash[:, 0:1], None, ALU.add).then_inc(idx_by_dve, 1)

            def xt_evac(e, u):
                for h in range(2):
                    v.wait_ge(xt_by_act, 2 * e + (h + 1))
                    v.tensor_tensor(xgT_lo[:, u % 2, 4 * h:4 * h + 4, :], bank[h][:, :].rearrange("p (c n) -> p c n", c=4),
                                    xgT[:, u % 2, 4 * h:4 * h + 4, :].bitcast(F32), ALU.subtract).then_inc(xt_by_dve, 1)

            def weights_lo(e, u):
                if not (isinstance(e, int) and e == 0):
                    v.wait_ge(hi_by_act, e)
                w_ = wgu[u % WSLOTS]
                v.tensor_tensor(wgu_lo[u % WSLOTS][:], w_[:], wgu_hi[u % 2][:].bitcast(F32), ALU.subtract).then_inc(lo_by_dve, 1)

            def hidden(e, u):
                v.wait_ge(silu_by_act, e + 1)
                v.scalar_tensor_tensor(hh[:, u % 2, :], bank[2][:, FE:2 * FE], gate_idx[:, u % UNROLL, 1:2], silu[:],
                                       ALU.mult, ALU.mult).then_inc(h_by_dve, 1)

            def ht_evac(e, u):
                v.wait_ge(ex_ht, e + 1)
                v.tensor_copy(hT[:, u % 2, :, :], bank[5][:, 0:FE].rearrange("p (j n) -> p j n", j=2)).then_inc(ht_by_dve, 1)

            def y_evac(e, u, free=True):
                v.wait_ge(ex_dn, e + 1)
                if free:
                    v.wait_ge(y_added, (e - 1) * 16)
                v.tensor_copy(ysb[:, u % 2, 512:1024], bank[4][:, :]).then_inc(y_by_dve, 1)

            for e in range(IDX_AHEAD):
                hot(e, e, wait=False)
                idx(e, e, wait=False)
            v.wait_ge(sgu_done, NT)
            v.wait_ge(wgu_in[0], 32)
            then(v.tensor_copy(wgu_hi[0][:], wgu[0][:]))
            weights_lo(0, 0)
            t, w = NT - 1, NS
            v.wait_ge(sy_act, 2 * NT)
            v.wait_ge(pool_scaled, NT)
            v.tensor_tensor(sy[0:w, t % 2, :], sy[0:w, t % 2, :], x1[0:w, t, :], ALU.add).then_inc(sy_dve, 1)
            v.wait_ge(sy_dve, 1)
            v.wait_ge(pool_sy, NT - 1)
            xt_evac(0, 0)
            v.wait_ge(y_inited[0], 16 * ((NT + 1) // 2))
            v.wait_ge(y_inited[1], 16 * (NT // 2))

            def step(e, u, first=False, ahead=True, wait=True, last=False, free=True):
                if ahead:
                    hot(e + IDX_AHEAD, u + IDX_AHEAD)
                if not first:
                    ht_evac(e - 1, u - 1)
                if not last:
                    weights_lo(e + 1, u + 1)
                    xt_evac(e + 1, u + 1)
                if ahead:
                    idx(e + IDX_AHEAD, (u + IDX_AHEAD) % UNROLL, wait)
                hidden(e, u)
                if not first:
                    y_evac(e - 1, u - 1, free)

            for e in range(UNROLL):
                step(e, e, first=e == 0, wait=e + IDX_AHEAD >= UNROLL, free=e >= 3)
            with v.Fori(1, E // UNROLL - 1) as i:
                for u in range(UNROLL):
                    step(i * UNROLL + u, u)
            for e in range(E - UNROLL, E):
                step(e, e % UNROLL, ahead=e + IDX_AHEAD < E, last=e == E - 1)
            ht_evac(E - 1, E - 1)
            y_evac(E - 1, E - 1)

            v.wait_ge(y_added, 16 * E)
            most_r = v.value_load(most[0:1, 0:1], min_val=0, max_val=TOK)
            with v.If(most_r > P):
                for tile in range(1, NT):
                    v.tensor_scalar(R[:, :, :, 2], posm[:], -1.0, float(tile * P), ALU.mult, ALU.add).then_inc(over_dve, 1)
                    v.tensor_scalar(iota_row[:], iota_row[:], float(P), None, ALU.add).then_inc(over_dve, 1)
                    v.wait_ge(over_dve, 2 * tile)
                    with v.Fori(0, E) as e:
                        n = e + E * tile
                        pos = posm[:, :, bass.ds(e, 1)].to_broadcast([P, NT, P])
                        v.wait_ge(y_added, 16 * n)
                        v.tensor_tensor(onehot[:, 0, :, :], iota_row[:].rearrange("p (a n) -> p a n", a=1).to_broadcast([P, NT, P]),
                                        pos, ALU.is_equal).then_inc(hot_by_dve, 1)
                        v.wait_ge(ex_list, n + 1)
                        v.tensor_reduce(gate_idx[:, 0, :], bank[7][:, 0:6].rearrange("p (a n) -> p a n", a=2), AX, ALU.add)\
                         .then_inc(sum_by_dve, 1)
                        v.wait_ge(sum_by_dve, n + 1)
                        v.tensor_scalar(idx_u[:, 0:1], gate_idx[:, 0, 0:1], trash[:, 0:1], None, ALU.add).then_inc(idx_by_dve, 1)
                        weights_lo(n, 0)
                        xt_evac(n, 0)
                        hidden(n, 0)
                        ht_evac(n, 0)
                        v.wait_ge(ex_dn, n + 1)
                        v.tensor_copy(ysb[:, 0, 512:1024], bank[4][:, :]).then_inc(y_by_dve, 1)
            v.wait_ge(ln_swap, 32)
            for t in range(NT):
                v.wait_ge(y_back[t], 16)
                stats(t, 1)
                norm_terms(t, 1)
                if t >= 1:
                    gain(t - 1, 1, fin_act)
            gain(NT - 1, 1, fin_act)

        @block.tensor
        def _(pe):
            mm = pe.matmul
            pe.wait_ge(pool_consts, N_CONST)
            pe.wait_ge(brow_landed, 16)
            pe.transpose(bank[7][:, 0:NB], brow[:], ident[0:NB, 0:NB]).then_inc(bcol_pe, 1)
            for t, (a, w) in enumerate(TILES):
                pe.wait_ge(x_landed[t], 16)
                if t >= 2:
                    pe.wait_ge(xt_dve, 2 * (t - 1))
                for h in range(2):
                    for c in range(4):
                        last = pe.transpose(bank[2 * (t % 2) + h][:, c * w:(c + 1) * w], x_in[0:w, t, (4 * h + c) * P:(4 * h + c + 1) * P],
                                            ident[0:w, 0:w])
                    last.then_inc(xt_done, 1)
            pe.wait_ge(xt_dve, 2 * NT)

            def zprod(n):
                nb, j, kind, _ = zprods[n]
                if j == 0:
                    pe.wait_ge(lo_dve, split_no[nb] + 1)
                if n >= 2:
                    if n - 2 in act_no:
                        pe.wait_ge(z_act, act_no[n - 2])
                    else:
                        pe.wait_ge(z_dve, dve_no[n - 2])
                kc_ = blocks[nb][1][0][2]
                for c in range(kc_):
                    if kind == "pa":
                        x_hi, x_lo = AT_hi[:, c, :], AT_lo[:, c, :]
                    elif kind == "pb":
                        x_hi, x_lo = uT_hi[c][:], uT_lo[:, c, :]
                    else:
                        x_hi, x_lo = xT[:, c, :], (xT_lo if split_no[nb] < n_early else xT_lo2)[:, c, :]
                    hi, lo = [f[:, c, j * P:(j + 1) * P] for f in (hi_of(nb), w_lo[nb % RAW])]
                    for i, (w_, x_) in enumerate(((hi, x_hi), (hi, x_lo), (lo, x_hi))):
                        first, final = c == 0 and i == 0, c == kc_ - 1 and i == 2
                        mm(bank[n % 2][:, 0:HALF], w_, x_[:, 0:HALF], start=first, stop=final)
                        last = mm(bank[2 + n % 2][:, 0:HALF], w_, x_[:, HALF:TOK], start=first, stop=final)
                last.then_inc(z_done, 1)

            for n in z_kq:
                zprod(n)
            for g, (nb, width, c0_, t) in enumerate(tms):
                a, w = TILES[t]
                if t == 0:
                    pe.wait_ge(lo_dve, split_no[nb] + 1)
                if g >= 2:
                    pe.wait_ge(tm_dve, g - 1)
                for c in range(DC):
                    for i, (x_, w_) in enumerate(((xT, hi_of(nb)), (xT, w_lo[nb % RAW]), (xT_lo, hi_of(nb)))):
                        last = mm(bank[4 + g % 2][0:w, 0:width], x_[:, c, a:a + w], w_[:, c, 0:width],
                                  start=c == 0 and i == 0, stop=c == DC - 1 and i == 2)
                last.then_inc(tm_done, 1)
            for n in z_u:
                zprod(n)
            pe.wait_ge(pool_sg, 2)
            pe.wait_ge(kc_landed, 16 * NSEQ)
            pe.wait_ge(k_dve, KVH)
            pe.wait_ge(z_act, act_no[z_kq[-1]])
            for g, items in enumerate(misc):
                if g >= 2:
                    pe.wait_ge(misc_act, g - 1)
                bk = bank[6 + g % 2]
                kind = items[0][0]
                for i, (_, x) in enumerate(items):
                    if kind == "sg":
                        last = pe.transpose(bk[:, i * P:(i + 1) * P], sgw[:, x, :], ident[:])
                    elif kind == "sgs":
                        last = pe.transpose(bk[0:NS, i * NS:(i + 1) * NS], sgs[:, x, :], ident[0:NS, 0:NS])
                    elif kind == "kc":
                        for kv in range(KVH):
                            last = pe.transpose(bk[:, (2 * i + kv) * P:(2 * i + kv + 1) * P], kc[:, x, kv, :], ident[:])
                    else:
                        a, w = TILES[PT - 1 + x]
                        for kv in range(KVH):
                            last = pe.transpose(bk[0:w, (2 * i + kv) * P:(2 * i + kv + 1) * P], kT[:, kv, a:a + w], ident[:])
                last.then_inc(misc_done, 1)

            pe.wait_ge(misc_act, len(misc) - 1)
            pe.wait_ge(misc_dve, 1)
            pe.wait_ge(tm_dve, len(tms))
            pe.wait_ge(z_act, act_no[z_u[-1]])

            def logits(u):
                if u >= 2:
                    pe.wait_ge(mx_dve, u - 1)
                if u < UP:
                    b, hg = u // 4, u % 4
                    kv = hg // (H // 4 // KVH)
                    k_lo = b * P if b == 0 else (b - 1) * P
                    lo = WIN if b == 0 else 0
                    for j in range(4):
                        r = slice(HD * (j % 2), HD * (j % 2) + HD)
                        last = mm(bank[2 * (u % 2) + j % 2][:, (j // 2) * W2 + lo:(j // 2 + 1) * W2],
                                  qT[r, 2 * hg + j // 2, b * P:(b + 1) * P], kT[r, kv, k_lo:(b + 1) * P], start=True, stop=True)
                else:
                    for q in range(2):
                        b = (u - UP) * 2 + q
                        for kv, par in rel_pair:
                            r0 = 32 * (2 * par + kv)
                            r = slice(HD * par, HD * par + HD)
                            q4 = qs[r, b, 4 * kv:4 * kv + 4, :]
                            o = bank[2 * (u % 2) + par][r0:r0 + 32, q * (WIN + NS):(q + 1) * (WIN + NS)]
                            mm(o[:, 0:WIN], q4, kcT[r, b, kv, :], start=True, stop=True)
                            last = mm(o[:, WIN:WIN + NS], q4, kT[r, kv, SEQ:TOK], start=True, stop=True)
                last.then_inc(logits_done, 1)

            def probs_t(u):
                pe.wait_ge(pool_norm, u + 1)
                if u >= 1:
                    pe.wait_ge(pt_act, u)
                    pe.wait_ge(pt_dve, u)
                if u < UP:
                    h0_ = 1 if u < 4 else 0
                    for j in range(4):
                        for h in range(h0_, 2):
                            c = (j % 2 * 2 + h) * P
                            last = pe.transpose(bank[4 + j // 2][:, c:c + P], L[:, u % LR, j, h * P:(h + 1) * P], ident[:])
                else:
                    for q in range(2):
                        pe.transpose(bank[4][:, q * P:(q + 1) * P], L[:, u % LR, q, 0:WIN], ident[:])
                        last = pe.transpose(bank[5][0:NS, q * P:(q + 1) * P], L[:, u % LR, q, WIN:WIN + NS], ident[:])
                last.then_inc(pt_done, 1)

            def values(u):
                pe.wait_ge(pt_act, u + 1)
                pe.wait_ge(pt_dve, u + 1)
                if u >= 2:
                    pe.wait_ge(pv_act, u - 1)
                if u < UP:
                    b, hg = u // 4, u % 4
                    kv = hg // (H // 4 // KVH)
                    for j in range(4):
                        o = bank[6 + u % 2][HD * (j % 2):HD * (j % 2) + HD, (j // 2) * P:(j // 2 + 1) * P]
                        halves = [1] if b == 0 else [0, 1]
                        for h in halves:
                            last = mm(o, v_sb[:, b - 1 + h, kv * HD:(kv + 1) * HD], PTs[:, u % 2, j, h, :],
                                      start=h == halves[0], stop=h == 1)
                else:
                    for q in range(2):
                        b = (u - UP) * 2 + q
                        for kv, par in rel_pair:
                            rows = slice(32 * (2 * par + kv), 32 * (2 * par + kv) + 32)
                            o = bank[6 + u % 2][HD * par:HD * par + HD, (2 * q + kv) * 32:(2 * q + kv + 1) * 32]
                            mm(o, vc[:, b, kv * HD:(kv + 1) * HD], PTs[:, u % 2, q, 0, rows], start=True, stop=False)
                            last = mm(o, v_sb[0:NS, PT, kv * HD:(kv + 1) * HD], PTs[0:NS, u % 2, q, 1, rows],
                                      start=False, stop=True)
                last.then_inc(pv_done, 1)

            pe.wait_ge(vc_landed, 16)
            for m in range(UA + 4):
                if m < UA:
                    logits(m)
                if 0 <= m - 4 < UA:
                    values(m - 4)
                if 0 <= m - 3 < UA:
                    probs_t(m - 3)
            pe.wait_ge(pool_vs, NT)
            pe.wait_ge(pt_act, UA)
            pe.wait_ge(pt_dve, UA)
            for t, (a, w) in enumerate(TILES):
                if t >= 2:
                    pe.wait_ge(sg_dve, t - 1)
                for g in range(G):
                    wt = sgwT[:, g, :] if t < PT else sgsT[:, g, :]
                    last = mm(bank[4 + t % 2][:, g * w:(g + 1) * w], vs_sb[0:w, t, g * P:(g + 1) * P], wt, start=True, stop=True)
                last.then_inc(sg_done, 1)
            pe.wait_ge(mx_dve, UA)
            pe.wait_ge(pv_act, UA)
            pe.wait_ge(x_lo_act, 1)
            pe.wait_ge(x_lo_dve, 1)
            first_pa = [zprods[n][2] for n in z_merge].index("pa")
            for i, n in enumerate(z_merge):
                if i == first_pa:
                    pe.wait_ge(au_dve, 1 + G)
                zprod(n)
            pe.wait_ge(sg_dve, NT)
            for t, (a, w) in enumerate(TILES):
                for s in range(NSB):
                    g = t * NSB + s
                    nb = first_wo + s
                    if t == 0:
                        pe.wait_ge(lo_dve, split_no[nb] + 1)
                    if g >= 2:
                        pe.wait_ge(wo_dve, g - 1)
                    for c in range(DC):
                        if g == 0:
                            pe.wait_ge(m_dve, c + 1)
                        for i, (m_, w_) in enumerate(((mT_hi, hi_of(nb)), (mT_hi, w_lo[nb % RAW]), (mT_lo, hi_of(nb)))):
                            last = mm(bank[4 + g % 2][0:w, 0:SB], m_[:, c, a:a + w], w_[:, c, :],
                                      start=c == 0 and i == 0, stop=c == DC - 1 and i == 2)
                    last.then_inc(wo_done_g, 1)
            for t, (a, w) in enumerate(TILES):
                x1_whole(pe, t)
                if t >= 2:
                    pe.wait_ge(x1t_act, t - 1)
                    pe.wait_ge(x1t_dve, t - 1)
                for h in range(2):
                    for c in range(4):
                        cc = 4 * h + c
                        last = pe.transpose(bank[2 * (t % 2) + h][:, c * w:(c + 1) * w],
                                            x1[0:w, t, :].rearrange("p (d c) -> p c d", c=DC)[:, cc, :], ident[0:w, 0:w])
                    last.then_inc(x1t_done, 1)
            pe.wait_ge(x1t_act, NT)
            pe.wait_ge(x1t_dve, NT)
            pe.wait_ge(wo_dve, NT * NSB)
            pe.wait_ge(wr_landed, 16)
            for t, (a, w) in enumerate(TILES):
                for c in range(DC):
                    last = mm(bank[4][0:w, t * E:(t + 1) * E], x1T[:, c, a:a + w], wr[:, c, :], start=c == 0, stop=c == DC - 1)
                last.then_inc(route_done, 1)

            def shared_gu(t):
                a, w = TILES[t]
                if t >= 1:
                    pe.wait_ge(ssilu_act, 2 * t)
                for c in range(DC):
                    last = mm(bank[5][0:w, :], x1T[:, c, a:a + w], swgu[:, :, c, :], start=c == 0, stop=c == DC - 1)
                last.then_inc(sgu_done, 1)

            def shared_down(t):
                a, w = TILES[t]
                pe.wait_ge(pool_sh, t + 1)
                if t >= 1:
                    pe.wait_ge(sht_act, t)
                for j in range(FE // P):
                    last = pe.transpose(bank[6][:, j * w:(j + 1) * w],
                                        ssilu[0:w, t % 2, :].rearrange("p (f j) -> p j f", j=2)[:, j, :], ident[0:w, 0:w])
                last.then_inc(sht_done, 1)
                pe.wait_ge(sht_act, t + 1)
                if t >= 1:
                    pe.wait_ge(sy_act, 2 * t)
                for h in range(2):
                    for j in range(FE // P):
                        last = mm(bank[h][0:w, :], shT[:, t % 2, j, 0:w], swd[:, j, h * 512:(h + 1) * 512],
                                  start=j == 0, stop=j == FE // P - 1)
                last.then_inc(sdn_done, 1)

            def places():
                pe.wait_ge(chosen_dve, 1)
                for t in range(NT):
                    mm(bank[7][:, t * E:(t + 1) * E], before[:], chosen[:, t, :], start=True, stop=t == 0)
                    for s in range(t):
                        mm(bank[7][:, t * E:(t + 1) * E], ones_b[:], chosen[:, s, :], start=False, stop=s == t - 1)
                for t in range(NT):
                    last = mm(bank[7][:, NT * E:NT * E + E], ones_b[:], chosen[:, t, :], start=t == 0, stop=t == NT - 1)
                last.then_inc(pos_done, 1)


            def token_list(e, u, wait=True):
                pe.wait_ge(hot_by_dve, e + 1)
                if wait:
                    pe.wait_ge(sum_by_dve, e)
                for t in range(NT):
                    last = mm(bank[7][:, 0:6], onehot[:, u % 4, t, :], R[:, t, bass.ds(e, 1), :],
                              start=t == 0, stop=t == NT - 1)
                last.then_inc(ex_list, 1)

            pe.wait_ge(shared_landed, 48)
            for t in range(NT + 1):
                if t < NT:
                    shared_gu(t)
                if t == NT - 3:
                    places()
                if t in (NT - 2, NT - 1):
                    pe.wait_ge(route_dve, 1)
                    for e in range(IDX_AHEAD // 2):
                        n = e + (t - NT + 2) * (IDX_AHEAD // 2)
                        token_list(n, n, wait=n > 0)
                if t >= 1:
                    shared_down(t - 1)
            pe.wait_ge(sy_act, 2 * NT)
            def rows_t(e, u, n, wait=True):
                pe.wait_ge(xg_in[u % XGSLOTS], n)
                if wait:
                    pe.wait_ge(xt_by_dve, 2 * e)
                for c in range(DC):
                    last = pe.transpose(bank[c // 4][:, c % 4 * P:(c % 4 + 1) * P],
                                        xg[u % XGSLOTS][:].rearrange("p (d c) -> p c d", c=DC)[:, c, :], ident[:])
                last.then_inc(ex_xt, 1)

            def gate_up(e, u, wait=True):
                slot = u % WSLOTS
                pe.wait_ge(xt_by_dve, 2 * e + 2)
                pe.wait_ge(lo_by_dve, e + 1)
                if wait:
                    pe.wait_ge(h_by_dve, e)
                for c in range(DC):
                    for i, (x_, w_) in enumerate(((xgT, wgu_hi[u % 2]), (xgT, wgu_lo[slot]), (xgT_lo, wgu_hi[u % 2]))):
                        last = mm(bank[2][:, :], x_[:, u % 2, c, :], w_[:, :, c, :],
                                  start=c == 0 and i == 0, stop=c == DC - 1 and i == 2)
                last.then_inc(ex_gu, 1)

            def hidden_t(e, u):
                pe.wait_ge(h_by_dve, e + 1)
                for j in range(FE // P):
                    last = pe.transpose(bank[5][:, j * P:(j + 1) * P],
                                        hh[:, u % 2, :].rearrange("p (f j) -> p j f", j=2)[:, j, :], ident[:])
                last.then_inc(ex_ht, 1)

            def down(e, u, landed, wait=True):
                slot = u % WSLOTS
                pe.wait_ge(ht_by_dve, e + 1)
                pe.wait_ge(wd_in[slot], landed * 16)
                if wait:
                    pe.wait_ge(y_by_act, e)
                    pe.wait_ge(y_by_dve, e)
                for h in range(2):
                    for j in range(FE // P):
                        last = mm(bank[3 + h][:, :], hT[:, u % 2, j, :], wd[slot][:, j, h * 512:(h + 1) * 512],
                                  start=j == 0, stop=j == FE // P - 1)
                last.then_inc(ex_dn, 1)

            rows_t(0, 0, 16, wait=False)

            def step(e, u, turn, first=False, ahead=True, last=False):
                if not last:
                    rows_t(e + 1, u + 1, (turn * (UNROLL // XGSLOTS) + ((u + 1) // XGSLOTS + 1)) * 16)
                if ahead:
                    token_list(e + IDX_AHEAD, u + IDX_AHEAD)
                gate_up(e, u, wait=not first)
                if not first:
                    up = u - 1
                    down(e - 1, up, turn * (UNROLL // WSLOTS) + (up // WSLOTS + 1), wait=first is not None)
                hidden_t(e, u)

            for e in range(UNROLL):
                step(e, e, 0, first=True if e == 0 else None if e == 1 else False)
            with pe.Fori(1, E // UNROLL - 1) as i:
                for u in range(UNROLL):
                    step(i * UNROLL + u, u, i)
            for e in range(E - UNROLL, E):
                step(e, e % UNROLL, E // UNROLL - 1, ahead=e + IDX_AHEAD < E, last=e == E - 1)
            down(E - 1, E - 1, E // WSLOTS)

            pe.wait_ge(y_added, 16 * E)
            most_r = pe.value_load(most[0:1, 0:1], min_val=0, max_val=TOK)
            with pe.If(most_r > P):
                for tile in range(1, NT):
                    pe.wait_ge(over_dve, 2 * tile)
                    with pe.Fori(0, E) as e:
                        n = e + E * tile
                        pe.wait_ge(hot_by_dve, n + 1)
                        pe.wait_ge(sum_by_dve, n)
                        for t in range(NT):
                            last = mm(bank[7][:, 0:6], onehot[:, 0, t, :], R[:, t, bass.ds(e, 1), :], start=t == 0, stop=t == NT - 1)
                        last.then_inc(ex_list, 1)
                        m_ = e + E * (tile - 1)
                        rows_t(n, 0, (m_ + (E // XGSLOTS + 1)) * 16)
                        gate_up(n, 0)
                        hidden_t(n, 0)
                        down(n, 0, m_ + (E // WSLOTS + 1))


def build(nc, A, O):
    hybrid_layer(nc, A, O)


_OUTS = [("y_prompt", (1, 512, 1024)), ("y_sample", (8, 8, 1024)), ("win_k_prompt", (1, 1, 128, 2, 64)),
         ("win_v_prompt", (1, 1, 128, 2, 64)), ("win_k_sample", (1, 8, 128, 2, 64)),
         ("win_v_sample", (1, 8, 128, 2, 64)), ("chunk_v_sample", (1, 8, 8, 4, 128))]


def kernel(**inputs):
    import numpy as _np
    import concourse.bacc as _bacc
    from concourse import mybir as _mybir
    from concourse.bass_utils import run_bass_kernel_spmd as _run

    nc = _bacc.Bacc("TRN2", target_bir_lowering=False, num_devices=1)
    arrays, A, O = {}, {}, {}
    for name in inputs:
        a = _np.ascontiguousarray(inputs[name])
        arrays[f"in_{name}_dram"] = a
        A[name] = nc.dram_tensor(f"in_{name}_dram", a.shape, _mybir.dt.from_np(a.dtype), kind="ExternalInput").ap()
    for name, shape in _OUTS:
        O[name] = nc.dram_tensor(f"out_{name}_dram", shape, _mybir.dt.float32, kind="ExternalOutput").ap()
    build(nc, A, O)
    r = _run(nc, [arrays], core_ids=[0])
    return tuple(r.results[0][f"out_{name}_dram"] for name, _ in _OUTS)
```
